# Optimizing a Trainium2 kernel written in Bass

```python
import jax, jax.numpy as jnp
from jax import lax
import numpy as np
import jax
import jax.numpy as jnp

D_MODEL = 1024
BATCH = 1
SEQ = 256
DEPTH = 2

N_EVEN = (DEPTH + 1) // 2
N_ODD = DEPTH // 2

MLA_HEADS = 8
MLA_Q_RANK = 384
MLA_KV_RANK = 256
MLA_NOPE = 64
MLA_ROPE = 32
MLA_V = 64
MLA_QK = MLA_NOPE + MLA_ROPE
Q_BLOCK = 128

RET_HEADS = 8
RET_DK = 64
RET_DV = 64
RET_CHUNK = 128
RET_DECAY_BASE = 5.0

GLA_HEADS = 4
GLA_DK = 128
GLA_DV = 256
GLA_GATE_RANK = 16
GLA_TAU = 16.0
GLA_CHUNK = 64

D_FF = 2816
CONV_W = 3

ROPE_THETA = 10000.0
EPS = 1e-6

EVEN_SPLIT = (MLA_Q_RANK, MLA_KV_RANK, MLA_ROPE,
              RET_HEADS * RET_DK, RET_HEADS * RET_DK, RET_HEADS * RET_DV, RET_HEADS * RET_DV)
EVEN_IN = MLA_Q_RANK + MLA_KV_RANK + MLA_ROPE + 2 * RET_HEADS * RET_DK + 2 * RET_HEADS * RET_DV
EVEN_OUT = MLA_HEADS * MLA_V + RET_HEADS * RET_DV
ODD_SPLIT = (GLA_HEADS * GLA_DK, GLA_HEADS * GLA_DK, GLA_HEADS * GLA_DV, GLA_HEADS * GLA_DV,
             GLA_GATE_RANK, GLA_GATE_RANK)
ODD_IN = 2 * GLA_HEADS * GLA_DK + 2 * GLA_HEADS * GLA_DV + 2 * GLA_GATE_RANK
ODD_OUT = GLA_HEADS * GLA_DV


def _split(p, sizes):
    outs, s = [], 0
    for n in sizes:
        outs.append(p[..., s:s + n])
        s += n
    return outs

def _rmsnorm(x, g):
    xf = x.astype(jnp.float32)
    y = xf * lax.rsqrt(jnp.mean(xf * xf, axis=-1, keepdims=True) + EPS)
    return (y * g.astype(jnp.float32)).astype(x.dtype)

def _rope(x, positions):
    half = x.shape[-1] // 2
    inv = ROPE_THETA ** (-jnp.arange(half, dtype=jnp.float32) / half)
    ang = positions.astype(jnp.float32)[:, :, None] * inv
    cos = jnp.cos(ang)[:, :, None, :]
    sin = jnp.sin(ang)[:, :, None, :]
    x1 = x[..., :half].astype(jnp.float32)
    x2 = x[..., half:].astype(jnp.float32)
    return jnp.concatenate([x1 * cos - x2 * sin, x2 * cos + x1 * sin], axis=-1).astype(x.dtype)

def _mla(cq, ckv, k_rope, positions, q_norm, kv_norm, w_uq, w_ukv, q_head_norm, k_head_norm):
    B, S, _ = cq.shape
    H = MLA_HEADS
    q = (_rmsnorm(cq, q_norm) @ w_uq).reshape(B, S, H, MLA_QK)
    kv = (_rmsnorm(ckv, kv_norm) @ w_ukv).reshape(B, S, H, MLA_NOPE + MLA_V)
    k_nope, v = kv[..., :MLA_NOPE], kv[..., MLA_NOPE:]
    k = jnp.concatenate([k_nope, jnp.broadcast_to(k_rope[:, :, None, :], (B, S, H, MLA_ROPE))], axis=-1)
    q = _rmsnorm(q, q_head_norm)
    k = _rmsnorm(k, k_head_norm)
    q = jnp.concatenate([q[..., :MLA_NOPE], _rope(q[..., MLA_NOPE:], positions)], axis=-1)
    k = jnp.concatenate([k[..., :MLA_NOPE], _rope(k[..., MLA_NOPE:], positions)], axis=-1)
    scale = MLA_QK ** -0.5
    nb = S // Q_BLOCK
    qb = q.reshape(B, nb, Q_BLOCK, H, MLA_QK).transpose(1, 0, 2, 3, 4)

    def block(qi):
        s = jnp.einsum('bqhd,bkhd->bhqk', qi, k).astype(jnp.float32) * scale
        p = jax.nn.softmax(s, axis=-1).astype(v.dtype)
        return jnp.einsum('bhqk,bkhe->bqhe', p, v)

    o = lax.map(block, qb)
    return o.transpose(1, 0, 2, 3, 4).reshape(B, S, H * MLA_V)

def _retention_dir(q, k, v, log_gamma, include_diag):
    B, S, H, dk = q.shape
    dv = v.shape[-1]
    C = RET_CHUNK
    n = S // C
    q = q.reshape(B, n, C, H, dk)
    k = k.reshape(B, n, C, H, dk)
    v = v.reshape(B, n, C, H, dv)
    lg = log_gamma.astype(jnp.float32)
    pos = jnp.arange(C, dtype=jnp.float32)
    rel = pos[:, None] - pos[None, :]
    mask = (rel >= 0) if include_diag else (rel > 0)
    decay = jnp.where(mask[None], jnp.exp(lg[:, None, None] * jnp.maximum(rel, 0.0)[None]), 0.0)
    scores = jnp.einsum('bnihd,bnjhd->bnhij', q, k) * decay
    intra = jnp.einsum('bnhij,bnjhe->bnihe', scores, v)
    zeta = jnp.exp(lg[:, None] * (C - 1 - pos)[None])
    chunk_state = jnp.einsum('bnjhd,bnjhe,hj->bnhde', k, v, zeta)
    chunk_decay = jnp.exp(lg * C)[None, :, None, None]

    def step(R, s):
        return chunk_decay * R + s, R

    R0 = jnp.zeros((B, H, dk, dv), chunk_state.dtype)
    _, R_prev = lax.scan(step, R0, jnp.moveaxis(chunk_state, 1, 0))
    R_prev = jnp.moveaxis(R_prev, 0, 1)
    xi = jnp.exp(lg[:, None] * (pos + 1.0)[None]).T
    cross = jnp.einsum('bnihd,bnhde->bnihe', q, R_prev) * xi[None, None, :, :, None]
    return (intra + cross).reshape(B, S, H, dv)

def _retention(rq, rk, rv, rg, positions, theta_fwd, theta_bwd, out_norm):
    B, S, _ = rq.shape
    H = RET_HEADS
    q = _rope(rq.reshape(B, S, H, RET_DK), positions)
    k = _rope(rk.reshape(B, S, H, RET_DK), positions) * (RET_DK ** -0.5)
    v = rv.reshape(B, S, H, RET_DV)
    lg_f = jnp.log1p(-jnp.exp2(-theta_fwd.astype(jnp.float32)))
    lg_b = jnp.log1p(-jnp.exp2(-theta_bwd.astype(jnp.float32)))
    o_f = _retention_dir(q, k, v, lg_f, True)
    o_b = jnp.flip(_retention_dir(jnp.flip(q, 1), jnp.flip(k, 1), jnp.flip(v, 1), lg_b, False), 1)
    o = _rmsnorm(o_f + o_b, out_norm)
    return jax.nn.silu(rg) * o.reshape(B, S, H * RET_DV)

def _gla_dir(q, k, v, log_a, include_diag):
    B, S, H, dk = q.shape
    dv = v.shape[-1]
    C = GLA_CHUNK
    n = S // C
    q = q.reshape(B, n, C, H, dk)
    k = k.reshape(B, n, C, H, dk)
    v = v.reshape(B, n, C, H, dv)
    b = jnp.cumsum(log_a.astype(jnp.float32).reshape(B, n, C, H, dk), axis=2)
    b_mid = b[:, :, C // 2:C // 2 + 1]
    b_last = b[:, :, -1]
    qc = q * jnp.exp(b - b_mid)
    kc = k * jnp.exp(b_mid - b)
    A = jnp.einsum('bnihd,bnjhd->bnhij', qc, kc)
    pos = jnp.arange(C)
    mask = (pos[:, None] >= pos[None, :]) if include_diag else (pos[:, None] > pos[None, :])
    A = jnp.where(mask, A, 0.0)
    intra = jnp.einsum('bnhij,bnjhe->bnihe', A, v)
    k_dec = k * jnp.exp(b_last[:, :, None] - b)
    chunk_state = jnp.einsum('bnjhd,bnjhe->bnhde', k_dec, v)
    chunk_decay = jnp.exp(b_last)

    def step(Sm, xs):
        dcy, st = xs
        return dcy[..., None] * Sm + st, Sm

    S0 = jnp.zeros((B, H, dk, dv), chunk_state.dtype)
    _, S_prev = lax.scan(step, S0, (jnp.moveaxis(chunk_decay, 1, 0), jnp.moveaxis(chunk_state, 1, 0)))
    S_prev = jnp.moveaxis(S_prev, 0, 1)
    inter = jnp.einsum('bnihd,bnhde->bnihe', q * jnp.exp(b), S_prev)
    return (intra + inter).reshape(B, S, H, dv)

def _gla(gq, gk, gv, gr, ga_f, ga_b, w_gate_fwd, b_gate_fwd, w_gate_bwd, b_gate_bwd, out_norm):
    B, S, _ = gq.shape
    H = GLA_HEADS
    q = gq.reshape(B, S, H, GLA_DK) * (GLA_DK ** -0.5)
    k = gk.reshape(B, S, H, GLA_DK)
    v = gv.reshape(B, S, H, GLA_DV)
    la_f = (jax.nn.log_sigmoid((ga_f @ w_gate_fwd + b_gate_fwd).astype(jnp.float32)) / GLA_TAU).reshape(B, S, H, GLA_DK)
    la_b = (jax.nn.log_sigmoid((ga_b @ w_gate_bwd + b_gate_bwd).astype(jnp.float32)) / GLA_TAU).reshape(B, S, H, GLA_DK)
    o_f = _gla_dir(q, k, v, la_f, True)
    o_b = jnp.flip(_gla_dir(jnp.flip(q, 1), jnp.flip(k, 1), jnp.flip(v, 1), jnp.flip(la_b, 1), False), 1)
    o = _rmsnorm(o_f + o_b, out_norm)
    return jax.nn.silu(gr) * o.reshape(B, S, H * GLA_DV)

def _conv_ffn(x, norm_g, w_up, conv_w, conv_b, w_down):
    h = _rmsnorm(x, norm_g)
    up = h @ w_up
    gate, val = up[..., :D_FF], up[..., D_FF:]
    gate = lax.conv_general_dilated(gate, conv_w[:, None, :].astype(gate.dtype), window_strides=(1,),
                                    padding='SAME', dimension_numbers=('NWC', 'WIO', 'NWC'),
                                    feature_group_count=D_FF) + conv_b
    return (jax.nn.silu(gate) * val) @ w_down

def first_inputs(seed: int = 0) -> dict:
    key = jax.random.key(seed)
    ks = iter(jax.random.split(key, 40))

    def dense(shape, fan_in):
        return jax.random.normal(next(ks), shape, jnp.float32) * (fan_in ** -0.5)

    def gain(shape):
        return 1.0 + 0.02 * jax.random.normal(next(ks), shape, jnp.float32)

    def small(shape, s):
        return s * jax.random.normal(next(ks), shape, jnp.float32)

    x = jax.random.normal(next(ks), (BATCH, SEQ, D_MODEL), jnp.float32)
    start = jax.random.randint(next(ks), (BATCH, 1), 0, 4096)
    positions = (start + jnp.arange(SEQ)[None, :]).astype(jnp.int32)
    ret_base = RET_DECAY_BASE + jnp.arange(RET_HEADS, dtype=jnp.float32)
    return {
        "x": x,
        "positions": positions,
        "mix_norm_even": gain((N_EVEN, D_MODEL)),
        "w_in_even": dense((N_EVEN, D_MODEL, EVEN_IN), D_MODEL),
        "mla_q_norm": gain((N_EVEN, MLA_Q_RANK)),
        "mla_kv_norm": gain((N_EVEN, MLA_KV_RANK)),
        "mla_w_uq": dense((N_EVEN, MLA_Q_RANK, MLA_HEADS * MLA_QK), MLA_Q_RANK),
        "mla_w_ukv": dense((N_EVEN, MLA_KV_RANK, MLA_HEADS * (MLA_NOPE + MLA_V)), MLA_KV_RANK),
        "mla_q_head_norm": gain((N_EVEN, MLA_QK)),
        "mla_k_head_norm": gain((N_EVEN, MLA_QK)),
        "ret_theta_fwd": ret_base + small((N_EVEN, RET_HEADS), 0.1),
        "ret_theta_bwd": ret_base + small((N_EVEN, RET_HEADS), 0.1),
        "ret_out_norm": gain((N_EVEN, RET_HEADS, RET_DV)),
        "w_out_even": dense((N_EVEN, EVEN_OUT, D_MODEL), EVEN_OUT),
        "mix_norm_odd": gain((N_ODD, D_MODEL)),
        "w_in_odd": dense((N_ODD, D_MODEL, ODD_IN), D_MODEL),
        "gla_w_gate_fwd": dense((N_ODD, GLA_GATE_RANK, GLA_HEADS * GLA_DK), GLA_GATE_RANK),
        "gla_b_gate_fwd": small((N_ODD, GLA_HEADS * GLA_DK), 0.1),
        "gla_w_gate_bwd": dense((N_ODD, GLA_GATE_RANK, GLA_HEADS * GLA_DK), GLA_GATE_RANK),
        "gla_b_gate_bwd": small((N_ODD, GLA_HEADS * GLA_DK), 0.1),
        "gla_out_norm": gain((N_ODD, GLA_HEADS, GLA_DV)),
        "w_out_odd": dense((N_ODD, ODD_OUT, D_MODEL), ODD_OUT),
        "ffn_norm": gain((DEPTH, D_MODEL)),
        "ffn_w_up": dense((DEPTH, D_MODEL, 2 * D_FF), D_MODEL),
        "ffn_conv_w": dense((DEPTH, CONV_W, D_FF), CONV_W),
        "ffn_conv_b": small((DEPTH, D_FF), 0.02),
        "ffn_w_down": dense((DEPTH, D_FF, D_MODEL), D_FF),
    }

def first_block(x, positions, mix_norm_even, w_in_even, mla_q_norm, mla_kv_norm, mla_w_uq, mla_w_ukv,
              mla_q_head_norm, mla_k_head_norm, ret_theta_fwd, ret_theta_bwd, ret_out_norm, w_out_even,
              mix_norm_odd, w_in_odd, gla_w_gate_fwd, gla_b_gate_fwd, gla_w_gate_bwd, gla_b_gate_bwd,
              gla_out_norm, w_out_odd, ffn_norm, ffn_w_up, ffn_conv_w, ffn_conv_b, ffn_w_down):
    for layer in range(DEPTH):
        i = layer // 2
        if layer % 2 == 0:
            h = _rmsnorm(x, mix_norm_even[i])
            cq, ckv, k_rope, rq, rk, rv, rg = _split(h @ w_in_even[i], EVEN_SPLIT)
            a = _mla(cq, ckv, k_rope, positions, mla_q_norm[i], mla_kv_norm[i], mla_w_uq[i], mla_w_ukv[i],
                     mla_q_head_norm[i], mla_k_head_norm[i])
            r = _retention(rq, rk, rv, rg, positions, ret_theta_fwd[i], ret_theta_bwd[i], ret_out_norm[i])
            x = x + jnp.concatenate([a, r], axis=-1) @ w_out_even[i]
        else:
            h = _rmsnorm(x, mix_norm_odd[i])
            gq, gk, gv, gr, ga_f, ga_b = _split(h @ w_in_odd[i], ODD_SPLIT)
            g = _gla(gq, gk, gv, gr, ga_f, ga_b, gla_w_gate_fwd[i], gla_b_gate_fwd[i],
                     gla_w_gate_bwd[i], gla_b_gate_bwd[i], gla_out_norm[i])
            x = x + g @ w_out_odd[i]
        x = x + _conv_ffn(x, ffn_norm[layer], ffn_w_up[layer], ffn_conv_w[layer], ffn_conv_b[layer],
                          ffn_w_down[layer])
    return x


GRID_W = 64
CTX_LEN = 256
ATT_HEADS = 8
ATT_KV_HEADS = 2
ATT_HEAD_DIM = 64
ATT_GROUP = ATT_HEADS // ATT_KV_HEADS
WINDOW = 128
ATT_BLOCK = 128
ATT_SPAN = ATT_BLOCK + 2 * WINDOW
ML_HEADS = 4
ML_QK_DIM = 64
ML_V_DIM = 128
ML_CHUNK = 64
ML_CONV = 5
GATE_CAP = 15.0
ATT_WIDTH = ATT_HEADS * ATT_HEAD_DIM
ATT_KV_WIDTH = ATT_KV_HEADS * ATT_HEAD_DIM
ML_QK_WIDTH = ML_HEADS * ML_QK_DIM
ML_WIDTH = ML_HEADS * ML_V_DIM
ML_GATES = 4 * ML_HEADS
MIX_WIDTH = ATT_WIDTH + ML_WIDTH
SPLIT_SIZES = (ATT_WIDTH, ATT_KV_WIDTH, ATT_KV_WIDTH, ML_QK_WIDTH, ML_QK_WIDTH, ML_WIDTH, ML_WIDTH, ML_GATES)
IN_WIDTH = ATT_WIDTH + 2 * ATT_KV_WIDTH + 2 * ML_QK_WIDTH + 2 * ML_WIDTH + ML_GATES
FFN_DIM = 2816
N_EXPERTS = 8
TOP_K = 2


def rmsnorm(x, g):
    xf = x.astype(jnp.float32)
    y = xf * lax.rsqrt(jnp.mean(xf * xf, axis=-1, keepdims=True) + EPS)
    return (y * g.astype(jnp.float32)).astype(x.dtype)

def adaln(x, g, shift, scale):
    return rmsnorm(x, g) * (1 + scale) + shift

def split_columns(u):
    points = [int(p) for p in np.cumsum(SPLIT_SIZES)[:-1]]
    return jnp.split(u, points, axis=-1)

def axial_rope_tables(n_tokens):
    rows = n_tokens // GRID_W
    t = jnp.arange(rows * GRID_W)
    row = jnp.repeat(jnp.arange(rows), GRID_W).astype(jnp.float32)
    col = (t % GRID_W).astype(jnp.float32)
    quarter = ATT_HEAD_DIM // 4
    inv = ROPE_THETA ** (-jnp.arange(quarter, dtype=jnp.float32) / quarter)
    ang_r = row[:, None] * inv[None, :]
    ang_c = col[:, None] * inv[None, :]
    return (jnp.cos(ang_r), jnp.sin(ang_r), jnp.cos(ang_c), jnp.sin(ang_c))

def _rotate_half(x, cos, sin):
    x1, x2 = jnp.split(x, 2, axis=-1)
    return jnp.concatenate([x1 * cos - x2 * sin, x2 * cos + x1 * sin], axis=-1)

def apply_axial_rope(x, tabs):
    cos_r, sin_r, cos_c, sin_c = [t[:, None, :] for t in tabs]
    xf = x.astype(jnp.float32)
    half = x.shape[-1] // 2
    out = jnp.concatenate([_rotate_half(xf[..., :half], cos_r, sin_r),
                           _rotate_half(xf[..., half:], cos_c, sin_c)], axis=-1)
    return out.astype(x.dtype)

def sink_attention(qg, kv_sets, sink_g):
    sink = sink_g[None, :, :, None]
    m = sink
    scores = []
    for k, v, mask in kv_sets:
        s = jnp.einsum('bqhgd,bkhd->bhgqk', qg, k).astype(jnp.float32)
        if mask is not None:
            s = jnp.where(mask, s, -jnp.inf)
        scores.append(s)
        m = jnp.maximum(m, s.max(-1))
    denom = jnp.exp(sink - m)
    num = None
    for s, (k, v, mask) in zip(scores, kv_sets):
        p = jnp.exp(s - m[..., None])
        denom = denom + p.sum(-1)
        o = jnp.einsum('bhgqk,bkhd->bhgqd', p, v.astype(jnp.float32))
        num = o if num is None else num + o
    out = num / denom[..., None]
    return jnp.transpose(out, (0, 3, 1, 2, 4))

def window_attention(q, k, v, k_ctx, v_ctx, sink_g):
    B, S = q.shape[:2]
    nb = S // ATT_BLOCK
    qg = (q * (ATT_HEAD_DIM ** -0.5)).reshape(B, nb, ATT_BLOCK, ATT_KV_HEADS, ATT_GROUP, ATT_HEAD_DIM)
    pad = ((0, 0), (WINDOW, WINDOW), (0, 0), (0, 0))
    kp = jnp.pad(k, pad)
    vp = jnp.pad(v, pad)
    valid = jnp.pad(jnp.ones((S,), dtype=bool), (WINDOW, WINDOW))
    rel = jnp.abs(jnp.arange(ATT_BLOCK)[:, None] + WINDOW - jnp.arange(ATT_SPAN)[None, :]) <= WINDOW

    def block(j):
        start = j * ATT_BLOCK
        qb = lax.dynamic_index_in_dim(qg, j, axis=1, keepdims=False)
        kb = lax.dynamic_slice_in_dim(kp, start, ATT_SPAN, axis=1)
        vb = lax.dynamic_slice_in_dim(vp, start, ATT_SPAN, axis=1)
        mask = rel & lax.dynamic_slice_in_dim(valid, start, ATT_SPAN)[None, :]
        out = sink_attention(qb, ((kb, vb, mask), (k_ctx, v_ctx, None)), sink_g)
        return out.reshape(B, ATT_BLOCK, ATT_WIDTH).astype(q.dtype)

    outs = lax.map(block, jnp.arange(nb))
    return jnp.moveaxis(outs, 0, 1).reshape(B, S, ATT_WIDTH)

def mlstm_chunkwise(q, k, v, i_pre, f_pre, state):
    B, T, H, DK = q.shape
    DV = v.shape[-1]
    nc = T // ML_CHUNK
    f32 = jnp.float32

    def chunks(a):
        return jnp.moveaxis(a.reshape((B, nc, ML_CHUNK) + a.shape[2:]), 1, 0)

    qs = chunks(q.astype(f32) * (DK ** -0.5))
    ks = chunks(k.astype(f32))
    vs = chunks(v.astype(f32))
    lis = chunks(i_pre.astype(f32))
    lfs = chunks(jax.nn.log_sigmoid(f_pre.astype(f32)))
    causal = jnp.tril(jnp.ones((ML_CHUNK, ML_CHUNK), dtype=bool))

    def step(carry, inp):
        C, n, m = carry
        qc, kc, vc, li, lf = inp
        b = jnp.cumsum(lf, axis=1).transpose(0, 2, 1)
        ig = li.transpose(0, 2, 1)
        d = jnp.where(causal, b[..., :, None] - b[..., None, :] + ig[..., None, :], -jnp.inf)
        inter = b + m[..., None]
        m_t = jnp.maximum(inter, d.max(-1))
        w_inter = jnp.exp(inter - m_t)
        s = jnp.einsum('bthd,bshd->bhts', qc, kc) * jnp.exp(d - m_t[..., None])
        num = jnp.einsum('bhts,bshe->bhte', s, vc) + w_inter[..., None] * jnp.einsum('bthd,bhde->bhte', qc, C)
        den = s.sum(-1) + w_inter * jnp.einsum('bthd,bhd->bht', qc, n)
        h = num / jnp.maximum(jnp.abs(den), jnp.exp(-m_t))[..., None]
        b_end = b[..., -1]
        g = b_end[..., None] - b + ig
        m_new = jnp.maximum(b_end + m, g.max(-1))
        decay = jnp.exp(b_end + m - m_new)
        wk = jnp.exp(g - m_new[..., None])
        C_new = decay[..., None, None] * C + jnp.einsum('bhs,bshd,bshe->bhde', wk, kc, vc)
        n_new = decay[..., None] * n + jnp.einsum('bhs,bshd->bhd', wk, kc)
        return (C_new, n_new, m_new), h.transpose(0, 2, 1, 3)

    state, hs = lax.scan(step, state, (qs, ks, vs, lis, lfs))
    h = jnp.moveaxis(hs, 0, 1).reshape(B, T, H, DV)
    return h, state

def depthwise_conv(x, w, b):
    C = x.shape[-1]
    y = lax.conv_general_dilated(x, w.reshape(ML_CONV, 1, C).astype(x.dtype), (1,),
                                 [(ML_CONV // 2, ML_CONV // 2)],
                                 dimension_numbers=('NWC', 'WIO', 'NWC'), feature_group_count=C)
    return y + b

def mlstm_inputs(qm, km, vm, gt, conv_w, conv_b, b_gates):
    B, T, _ = qm.shape
    qk = jax.nn.silu(depthwise_conv(jnp.concatenate([qm, km], axis=-1), conv_w, conv_b))
    q, k = jnp.split(qk, 2, axis=-1)
    q = q.reshape(B, T, ML_HEADS, ML_QK_DIM)
    k = k.reshape(B, T, ML_HEADS, ML_QK_DIM)
    v = vm.reshape(B, T, ML_HEADS, ML_V_DIM)
    g = gt.astype(jnp.float32) + b_gates.astype(jnp.float32)
    g = (GATE_CAP * jnp.tanh(g / GATE_CAP)).reshape(B, T, 4, ML_HEADS)
    return q, k, v, g[:, :, 0], g[:, :, 1], g[:, :, 2], g[:, :, 3]

def init_state(B):
    f32 = jnp.float32
    return (jnp.zeros((B, ML_HEADS, ML_QK_DIM, ML_V_DIM), f32),
            jnp.zeros((B, ML_HEADS, ML_QK_DIM), f32),
            jnp.zeros((B, ML_HEADS), f32))

def merge_groups(att, h_ml, o_pre, g_att, g_ml, w_out):
    B, T = att.shape[:2]
    att_n = rmsnorm(att, g_att)
    hf = h_ml.astype(jnp.float32)
    hn = hf * lax.rsqrt(jnp.mean(hf * hf, axis=-1, keepdims=True) + EPS)
    hn = hn * g_ml.astype(jnp.float32).reshape(ML_HEADS, ML_V_DIM)
    ml = hn.reshape(B, T, ML_WIDTH).astype(att.dtype) * jax.nn.sigmoid(o_pre)
    return jnp.concatenate([att_n, ml], axis=-1) @ w_out

def token_mixing(hx, hc, w_in, conv_w, conv_b, b_gates, attn_sink, g_att, g_ml, w_out, rope, with_ctx_out):
    B, S, _ = hx.shape
    L = hc.shape[1]
    qa_x, ka_x, va_x, qm_x, km_x, vm_x, om_x, gt_x = split_columns(hx @ w_in)
    qa_c, ka_c, va_c, qm_c, km_c, vm_c, om_c, gt_c = split_columns(hc @ w_in)
    sink_g = attn_sink.astype(jnp.float32).reshape(ATT_KV_HEADS, ATT_GROUP)
    k_ctx = ka_c.reshape(B, L, ATT_KV_HEADS, ATT_HEAD_DIM)
    v_ctx = va_c.reshape(B, L, ATT_KV_HEADS, ATT_HEAD_DIM)
    q = apply_axial_rope(qa_x.reshape(B, S, ATT_HEADS, ATT_HEAD_DIM), rope)
    k = apply_axial_rope(ka_x.reshape(B, S, ATT_KV_HEADS, ATT_HEAD_DIM), rope)
    v = va_x.reshape(B, S, ATT_KV_HEADS, ATT_HEAD_DIM)
    att_x = window_attention(q, k, v, k_ctx, v_ctx, sink_g)
    qc_, kc_, vc_, icf, fcf, icb, fcb = mlstm_inputs(qm_c, km_c, vm_c, gt_c, conv_w, conv_b, b_gates)
    qx_, kx_, vx_, ixf, fxf, ixb, fxb = mlstm_inputs(qm_x, km_x, vm_x, gt_x, conv_w, conv_b, b_gates)
    flip = lambda a: jnp.flip(a, axis=1)
    h_cf, st_f = mlstm_chunkwise(qc_, kc_, vc_, icf, fcf, init_state(B))
    h_cb, st_b = mlstm_chunkwise(flip(qc_), flip(kc_), flip(vc_), flip(icb), flip(fcb), init_state(B))
    h_xf, _ = mlstm_chunkwise(qx_, kx_, vx_, ixf, fxf, st_f)
    h_xb, _ = mlstm_chunkwise(flip(qx_), flip(kx_), flip(vx_), flip(ixb), flip(fxb), st_b)
    out_x = merge_groups(att_x, h_xf + flip(h_xb), om_x, g_att, g_ml, w_out)
    if not with_ctx_out:
        return out_x, None
    qg_c = (qa_c * (ATT_HEAD_DIM ** -0.5)).reshape(B, L, ATT_KV_HEADS, ATT_GROUP, ATT_HEAD_DIM)
    att_c = sink_attention(qg_c, ((k_ctx, v_ctx, None),), sink_g).reshape(B, L, ATT_WIDTH).astype(hc.dtype)
    out_c = merge_groups(att_c, h_cf + flip(h_cb), om_c, g_att, g_ml, w_out)
    return out_x, out_c

def swiglu(t, w1, w3, w2):
    return (jax.nn.silu(t @ w1) * (t @ w3)) @ w2

def moe_swiglu(h, w_router, b_router, w1, w3, w2):
    shp = h.shape
    t = h.reshape(-1, shp[-1])
    logits = (t @ w_router).astype(jnp.float32) + b_router.astype(jnp.float32)
    top_v, top_i = lax.top_k(logits, TOP_K)
    top_w = jax.nn.softmax(top_v, axis=-1)
    combine = jnp.sum(jax.nn.one_hot(top_i, N_EXPERTS, dtype=jnp.float32) * top_w[..., None], axis=1)
    y = None
    for e in range(N_EXPERTS):
        ye = combine[:, e:e + 1] * swiglu(t, w1[e], w3[e], w2[e]).astype(jnp.float32)
        y = ye if y is None else y + ye
    return y.astype(h.dtype).reshape(shp)

def channel_mix(h, layer, ffn_w1, ffn_w3, ffn_w2, w_router, b_router, exp_w1, exp_w3, exp_w2):
    i = layer // 2
    if layer % 2 == 0:
        return swiglu(h, ffn_w1[i], ffn_w3[i], ffn_w2[i])
    return moe_swiglu(h, w_router[i], b_router[i], exp_w1[i], exp_w3[i], exp_w2[i])

def second_inputs(seed: int = 0) -> dict:
    key = jax.random.key(seed)
    ks = jax.random.split(key, 26)
    D = D_MODEL
    n_dense = (DEPTH + 1) // 2
    n_moe = DEPTH // 2

    def nrm(i, shape, scale):
        return jax.random.normal(ks[i], shape, jnp.float32) * scale

    i_bias = -2.0 + nrm(11, (DEPTH, 2, ML_HEADS), 0.1)
    f_bias = 4.0 + nrm(12, (DEPTH, 2, ML_HEADS), 0.5)
    b_gates = jnp.stack([i_bias[:, 0], f_bias[:, 0], i_bias[:, 1], f_bias[:, 1]], axis=1).reshape(DEPTH, ML_GATES)
    return {
        'x': nrm(0, (BATCH, SEQ, D), 1.0),
        'c': nrm(1, (BATCH, D), 1.0),
        'ctx': nrm(2, (BATCH, CTX_LEN, D), 1.0),
        'c_ctx': nrm(3, (D,), 1.0),
        'norm1_g': 1.0 + nrm(4, (DEPTH, D), 0.02),
        'norm2_g': 1.0 + nrm(5, (DEPTH, D), 0.02),
        'w_mod': nrm(6, (DEPTH, D, 6 * D), 0.5 * D ** -0.5),
        'b_mod': nrm(7, (DEPTH, 6 * D), 0.02),
        'w_in': nrm(8, (DEPTH, D, IN_WIDTH), D ** -0.5),
        'conv_w': nrm(9, (DEPTH, ML_CONV, 2 * ML_QK_WIDTH), ML_CONV ** -0.5),
        'conv_b': nrm(10, (DEPTH, 2 * ML_QK_WIDTH), 0.02),
        'b_gates': b_gates,
        'attn_sink': nrm(13, (DEPTH, ATT_HEADS), 0.5),
        'g_att': 1.0 + nrm(14, (DEPTH, ATT_WIDTH), 0.02),
        'g_ml': 1.0 + nrm(15, (DEPTH, ML_WIDTH), 0.02),
        'w_out': nrm(16, (DEPTH, MIX_WIDTH, D), MIX_WIDTH ** -0.5),
        'ffn_w1': nrm(17, (n_dense, D, FFN_DIM), D ** -0.5),
        'ffn_w3': nrm(18, (n_dense, D, FFN_DIM), D ** -0.5),
        'ffn_w2': nrm(19, (n_dense, FFN_DIM, D), FFN_DIM ** -0.5),
        'w_router': nrm(20, (n_moe, D, N_EXPERTS), D ** -0.5),
        'b_router': nrm(21, (n_moe, N_EXPERTS), 0.01),
        'exp_w1': nrm(22, (n_moe, N_EXPERTS, D, FFN_DIM), D ** -0.5),
        'exp_w3': nrm(23, (n_moe, N_EXPERTS, D, FFN_DIM), D ** -0.5),
        'exp_w2': nrm(24, (n_moe, N_EXPERTS, FFN_DIM, D), FFN_DIM ** -0.5),
        'final_g': 1.0 + nrm(25, (D,), 0.02),
    }

def second_block(x, c, ctx, c_ctx, norm1_g, norm2_g, w_mod, b_mod, w_in, conv_w, conv_b, b_gates,
              attn_sink, g_att, g_ml, w_out, ffn_w1, ffn_w3, ffn_w2, w_router, b_router,
              exp_w1, exp_w3, exp_w2, final_g):
    rope = axial_rope_tables(x.shape[1])
    cond_x = jax.nn.silu(c)
    cond_c = jax.nn.silu(c_ctx)[None]
    for layer in range(DEPTH):
        last = layer == DEPTH - 1
        mod_x = jnp.split((cond_x @ w_mod[layer] + b_mod[layer])[:, None, :], 6, axis=-1)
        mod_c = jnp.split((cond_c @ w_mod[layer] + b_mod[layer])[:, None, :], 6, axis=-1)
        hx = adaln(x, norm1_g[layer], mod_x[0], mod_x[1])
        hc = adaln(ctx, norm1_g[layer], mod_c[0], mod_c[1])
        mix_x, mix_c = token_mixing(hx, hc, w_in[layer], conv_w[layer], conv_b[layer], b_gates[layer],
                                    attn_sink[layer], g_att[layer], g_ml[layer], w_out[layer], rope,
                                    not last)
        x = x + mod_x[2] * mix_x
        hx = adaln(x, norm2_g[layer], mod_x[3], mod_x[4])
        x = x + mod_x[5] * channel_mix(hx, layer, ffn_w1, ffn_w3, ffn_w2, w_router, b_router,
                                       exp_w1, exp_w3, exp_w2)
        if not last:
            ctx = ctx + mod_c[2] * mix_c
            hc = adaln(ctx, norm2_g[layer], mod_c[3], mod_c[4])
            ctx = ctx + mod_c[5] * channel_mix(hc, layer, ffn_w1, ffn_w3, ffn_w2, w_router, b_router,
                                               exp_w1, exp_w3, exp_w2)
    return rmsnorm(x, final_g)


def setup_inputs(seed=0):
    out = dict(first_inputs(seed))
    for name, value in second_inputs(seed + 1).items():
        if name != "x":
            out[name + "_2"] = value
    return out


def reference(
    x, positions, mix_norm_even, w_in_even, mla_q_norm, mla_kv_norm, mla_w_uq, mla_w_ukv,
    mla_q_head_norm, mla_k_head_norm, ret_theta_fwd, ret_theta_bwd, ret_out_norm, w_out_even,
    mix_norm_odd, w_in_odd, gla_w_gate_fwd, gla_b_gate_fwd, gla_w_gate_bwd, gla_b_gate_bwd,
    gla_out_norm, w_out_odd, ffn_norm, ffn_w_up, ffn_conv_w, ffn_conv_b, ffn_w_down, c_2, ctx_2,
    c_ctx_2, norm1_g_2, norm2_g_2, w_mod_2, b_mod_2, w_in_2, conv_w_2, conv_b_2, b_gates_2,
    attn_sink_2, g_att_2, g_ml_2, w_out_2, ffn_w1_2, ffn_w3_2, ffn_w2_2, w_router_2, b_router_2,
    exp_w1_2, exp_w3_2, exp_w2_2, final_g_2,
):
    x = first_block(
        x, positions, mix_norm_even, w_in_even, mla_q_norm, mla_kv_norm, mla_w_uq, mla_w_ukv,
        mla_q_head_norm, mla_k_head_norm, ret_theta_fwd, ret_theta_bwd, ret_out_norm,
        w_out_even, mix_norm_odd, w_in_odd, gla_w_gate_fwd, gla_b_gate_fwd, gla_w_gate_bwd,
        gla_b_gate_bwd, gla_out_norm, w_out_odd, ffn_norm, ffn_w_up, ffn_conv_w, ffn_conv_b,
        ffn_w_down,
    )
    return second_block(
        x, c_2, ctx_2, c_ctx_2, norm1_g_2, norm2_g_2, w_mod_2, b_mod_2, w_in_2, conv_w_2,
        conv_b_2, b_gates_2, attn_sink_2, g_att_2, g_ml_2, w_out_2, ffn_w1_2, ffn_w3_2,
        ffn_w2_2, w_router_2, b_router_2, exp_w1_2, exp_w3_2, exp_w2_2, final_g_2,
    )


_drawn_inputs = setup_inputs


def setup_inputs(seed=0):
    import zlib

    import numpy as np

    out = dict(_drawn_inputs(seed))
    spreads = {}
    factors = {'mla_q_norm': 8.0,
     'mla_kv_norm': 8.0,
     'mla_q_head_norm': 8.0,
     'mla_k_head_norm': 8.0,
     'ret_out_norm': 4.107,
     'gla_b_gate_fwd': 3.365,
     'gla_b_gate_bwd': 3.527,
     'gla_out_norm': 3.943,
     'ffn_conv_b': 3.226,
     'norm1_g_2': 7.67,
     'norm2_g_2': 5.42,
     'conv_b_2': 64.0,
     'attn_sink_2': 8.0,
     'g_att_2': 8.0,
     'g_ml_2': 8.0,
     'b_router_2': 6.631,
     'final_g_2': 7.998}
    for name, (base, spread) in spreads.items():
        noise = np.random.default_rng([zlib.crc32(name.encode()), seed]).standard_normal(out[name].shape)
        drawn = base * np.exp(spread * noise) if base else spread * noise
        out[name] = jnp.asarray(drawn.astype(out[name].dtype))
    for name, factor in factors.items():
        out[name] = (out[name] * factor).astype(out[name].dtype)
    return out
```

```python
from collections import namedtuple
from contextlib import ExitStack

import numpy as np

import concourse.bass as bass
from concourse import mybir
from concourse.alu_op_type import AluOpType as ALU

ACT = mybir.ActivationFunctionType
AX = mybir.AxisListType
F32 = mybir.dt.float32
I32 = mybir.dt.int32

P = 128
T = 256
TT = T // P
D = 1024
KD = D // P
F = 2816
KF = F // P
EPS = 1e-6
HUGE = 1e30

MH, MQK, MNOPE, MROPE, MV = 8, 96, 64, 32, 64
CQ, CKV = 384, 256
EVEN = dict(cq=0, ckv=384, kr=640, rq=672, rk=1184, rv=1696, rg=2208, end=2720)
ODD = dict(q=0, k=512, v=1024, r=2048, gf=3072, gb=3088, end=3104)
RH, RD = 8, 64
GH, GK, GV, GC, GR, TAU = 4, 128, 256, 64, 16, 16.0
AH, AG, AD = 8, 2, 64
LH, LK, LV = 4, 64, 128
CAP = 15.0
NE = 8
IN2 = dict(q=0, k=512, v=640, conv=768, mv=1280, o=1792, g=2304)

SLOTS = 11
SLOT = 2048
CPE = KF + KF // 2

COLS = {}
NCOLS = 0
for _name, _n in (("mix_even", 8), ("mix_odd", 8), ("ffn", 16), ("conv_w", 132), ("conv_b", 44), ("q_norm", 3),
                  ("kv_norm", 2), ("ret_g", 4), ("gla_g", 8), ("norm1", 16), ("norm2", 16), ("b_mod", 96),
                  ("conv_w2", 40), ("conv_b2", 8), ("g_att", 8), ("g_ml", 8), ("final", 8), ("cond", 16),
                  ("b_gates", 8)):
    COLS[_name] = NCOLS
    NCOLS += _n
ROWS = {}
NROWS = 0
for _name, _n in (("qh", 96), ("kh", 96), ("theta", 16), ("sink", 16), ("b_router", 8)):
    ROWS[_name] = NROWS
    NROWS += _n
CST = {}
NCST = 0
for _name, _n in (("ident", 128), ("ones", 128), ("sel4", 512), ("axial", 128), ("inv", 48), ("iota8", 8), ("eps", 1),
                  ("relp", 512), ("relm", 512), ("gla_m", 768), ("gla_mask", 256), ("wmask", 512),
                  ("lmask", 1024), ("sel8", 1024)):
    CST[_name] = NCST
    NCST += _n
NKEEP = CST["relp"]

Use = namedtuple("Use", "bank nth")
PROJ = {"even_in": 1, "odd_in": 2, "q0": 3, "kv0": 4, "mv0": 5, "o0": 6, "q1": 7, "kv1": 8, "mv1": 9, "o1": 10}
ITEMS = {"mla": 0, "wx0": 16, "wc0": 32, "wx1": 48}
SINKS = {"wx0": 0, "wc0": 2, "wx1": 4}
MOD_PIECES = 48
FILL = {"start": 3, "latents": 2, "heads": 7, "attention": 16, "ret_rope": 3, "even_mix": 2, "ffn0": 1, "odd": 1,
        "gla_gates": 2, "gla": 8, "odd_mix": 2, "ffn1": 1}
assert sum(FILL.values()) == MOD_PIECES
MIXED = {"even": 0, "odd": 2, "mix0": 4, "mix1": 8}


def constants():
    c = np.zeros((P, NCST), np.float32)
    p = np.arange(P)

    def put(name, a):
        a = np.asarray(a, np.float32)
        a = a.reshape(a.shape[0], -1)
        c[:a.shape[0], CST[name]:CST[name] + a.shape[1]] = a

    put("ident", np.eye(P))
    put("ones", np.ones((P, P)))
    put("sel4", np.repeat(np.eye(4), P, axis=1))
    put("sel8", np.repeat(np.eye(8), P, axis=1))
    put("iota8", np.broadcast_to(8.0 - np.arange(8), (P, 8)))
    put("eps", np.full((P, 1), EPS))
    inv16 = np.float32(10000.0) ** (-np.arange(16, dtype=np.float32) / np.float32(16))
    inv32 = np.float32(10000.0) ** (-np.arange(32, dtype=np.float32) / np.float32(32))
    put("inv", np.broadcast_to(np.concatenate([inv16, inv32]), (P, 48)))
    tok = np.arange(T)
    ang = np.stack([(tok // 64).astype(np.float32)[:, None] * inv16, (tok % 64).astype(np.float32)[:, None] * inv16], 1)
    axial = np.stack([np.cos(ang), np.sin(ang)], 1)
    put("axial", axial.reshape(TT, P, 64).transpose(1, 0, 2))
    i = np.arange(T)[None, None, :]
    j = (np.arange(TT)[None, :] * P + p[:, None])[:, :, None]
    put("relp", np.maximum(i - j, 0))
    put("relm", np.maximum(j - i, 0))
    s, t = p[:, None], p[None, :]
    same = (s // GC) == (t // GC)
    cf, cb = (same & (s <= t)).astype(np.float32), (same & (s >= t)).astype(np.float32)
    tot = same.astype(np.float32)
    midf, midb = (t // GC) * GC + GC // 2, (t // GC) * GC + GC // 2 - 1
    mats = [cf, cf - cf[s, midf], tot - cf, cb, cb - cb[s, midb], tot - cb]
    put("gla_m", np.concatenate(mats, 1))
    put("gla_mask", np.concatenate([same & (s <= t), same & (s > t)], 1))
    q = np.arange(T).reshape(TT, P).T[:, :, None]
    k = np.arange(T)[None, None, :]
    put("wmask", np.where(np.abs(q - k) <= 128, 0.0, -HUGE))
    put("lmask", np.stack([j <= i, j >= i], 1))
    return c


class Lane:

    def __init__(self, engine, sig, name):
        self.engine, self.sig, self.order, self.steps, self.told = engine, sig, sig(name), 0, {}

    def step(self, ins):
        ins.then_inc(self.order, 1)
        self.steps += 1
        self.engine.wait_ge(self.order, self.steps)

    def tell(self, ins, name):
        ins.then_inc(self.sig(name), 1)
        self.told[name] = self.told.get(name, 0) + 1
        self.engine.wait_ge(self.sig(name), self.told[name])

    def wait(self, name, n):
        self.engine.wait_ge(self.sig(name), n)


def build(nc, A, out):
    ctx = ExitStack()
    with ctx:
        def sb(name, shape, dt=F32):
            return ctx.enter_context(nc.sbuf_tensor(name, shape, dt))

        sems = {}

        def sig(name):
            if name not in sems:
                sems[name] = ctx.enter_context(nc.semaphore(name))
            return sems[name]

        ring = sb("ring", [P, SLOTS, SLOT])
        res = sb("res", [P, 2, KD, T])
        h = sb("h", [P, 2, KD, T])
        areaA = sb("areaA", [P, 11280])
        areaB = sb("areaB", [P, 8192])
        temp = sb("temp", [P, 1024])
        cst = sb("cst", [P, NKEEP])
        cols = sb("cols", [P, NCOLS])
        rows = sb("rows", [P, NROWS])
        mods = sb("mods", [P, 2, 48, 2])
        stat = sb("stat", [P, 96])
        ps = ctx.enter_context(nc.psum_tensor("ps", [P, 8, 512], F32))

        def keep(name, n):
            return cst[:, CST[name]:CST[name] + n]

        def col(name, i):
            return cols[:, COLS[name] + i:COLS[name] + i + 1]

        ident, ones = keep("ident", P), keep("ones", P)
        eps = keep("eps", 1)
        hflat = h[:, :, :, :].rearrange("p a k t -> p (a k t)")
        spare = h[:, 1, :, :].rearrange("p k t -> p (k t)")

        def area(t, at, *dims):
            n = int(np.prod(dims))
            names = "abcdef"[:len(dims)]
            v = t[:, at:at + n]
            if len(dims) > 1:
                v = v.rearrange(f"p ({' '.join(names)}) -> p {' '.join(names)}", **dict(zip(names, dims)))
            return v

        pe_ = area(areaA, 0, TT, EVEN["end"])
        qh = area(areaA, 5440, TT, MH, MQK)
        kv = area(areaA, 6976, TT, MH, 128)
        kx = area(areaA, 9024, TT, MH, MQK)
        qT = area(areaB, 0, MH, T)
        kT = area(areaB, 2048, MH, T)
        mix0 = area(areaB, 4096, TT, D)
        cT = area(areaB, 6144, 5, T)
        relp, relm = area(areaA, 5440, TT, T), area(areaA, 5952, TT, T)
        rqk = area(areaA, 6976, TT, 2, RH, RD)
        rT = area(areaB, 0, 8, T)
        decay = area(areaB, 2048, 2, TT, T)
        sdec = area(areaB, 3072, 2, TT, T)
        ang = area(temp, 0, TT, 48)
        angn = area(temp, 96, TT, 48)
        sin = area(areaA, 11088, TT, 48)
        cos = area(areaA, 11184, TT, 48)
        posi = temp[:, 192:194].bitcast(I32)
        posf = temp[:, 194:196]
        po = area(areaA, 0, TT, ODD["end"])
        gqk = area(areaA, 6208, 8, T)
        la = area(areaA, 8256, 2, TT, 512)
        gaT = area(areaA, 10304, 2, T)
        kdT = area(areaB, 0, 2, TT, 512)
        glam = area(areaB, 2048, 6, P)
        glamask = area(areaB, 2816, 2, P)
        wg = area(areaB, 3072, 2, 512)
        gex = area(areaB, 4096, 3, T)
        gqkx = area(areaB, 4864, 2, 3, T)
        gst = area(areaB, 6400, 2, 3, GV)
        gA = area(spare, 0, 2, 2, P)
        gbias = area(spare, 512, 2, 512)
        p2 = area(areaA, 0, 4, 1280)
        vaug = area(areaA, 5120, 4, LH, LV + 1)
        mix2 = area(areaA, 7184, 4, D)
        conv = area(areaB, 0, 4, 2 * T)
        aqT = area(areaB, 2048, 4, 2 * T)
        akT = area(areaB, 4096, 2, 2 * T)
        wmask = area(areaB, 5120, TT, T)
        lmask = area(areaB, 2048, 2, TT, T)
        gates = area(areaB, 6144, 4, 2 * T)
        ro = area(hflat, 0, TT, 512)
        kdup = area(hflat, 1024, 4, AG, 2, AD)
        brow = area(hflat, 0, 2, 2 * T)
        mrow = area(hflat, 1024, 2, 2 * T)
        lw = [area(hflat, 2048, 4, T), area(areaB, 3072, 4, T)]
        lp = [area(hflat, 3072, 4, T), area(areaB, 4096, 4, T)]
        g1 = area(areaA, 0, 2, KF, T)
        g2 = area(areaA, 0, KF, 2 * T)
        fconv = area(areaB, 0, 2, 512)
        fsil = area(areaB, 1024, 2, 512)
        comb = area(areaB, 2048, NE, T)
        combT = area(areaB, 4096, T)
        sel8 = area(areaB, 4352, NE * P)
        fval = area(areaB, 5376, 2, T)
        modrow = area(res[:, 1, :, :].rearrange("p k t -> p (k t)"), 0, 2, 256)
        gT = area(temp, 960, 4, 16)

        bank_full = [sig(f"bank{b}_full") for b in range(8)]
        bank_free = [sig(f"bank{b}_free") for b in range(8)]
        slot_full = [sig(f"slot{s}_full") for s in range(SLOTS)]
        chunk_used = sig("chunk_used")

        uses, bank_uses, turn = {}, [0] * 8, [0, 6]
        chunks = []
        slot_loads = [0] * SLOTS
        used = [0]
        moe = {}

        block = ctx.enter_context(nc.Block())

        STILES = {0: [2, 3, 0, 1], 1: [2, 3]}

        def lsteps(l):
            return [(sq, x, d) for sq in range(2 - l) for x in range(LH) for d in range(2)]

        Att = namedtuple("Att", "tag items keys nbuf scale dk")

        ATT = {"mla": Att("mla", [(t, x) for t in range(TT) for x in range(MH)], T, 3, MQK ** -0.5, MQK)}
        for l in range(2):
            ATT[f"wx{l}"] = Att(f"wx{l}", [(t, x) for t in range(TT) for x in range(AH)], 2 * T, 2, AD ** -0.5, AD)
        ATT["wc0"] = Att("wc0", [(t, x) for t in range(2, 4) for x in range(AH)], T, 2, AD ** -0.5, AD)
        att_p = {"mla": area(spare, 0, 3, T)}
        att_pT = {"mla": area(spare, 768, 3, T)}
        for k in ("wx0", "wx1", "wc0"):
            att_p[k] = area(hflat, 2048, 2, 2 * T)
            att_pT[k] = area(hflat, 3072, 2, 2 * T)

        @block.tensor
        def _(pe):
            def take(*key, bank=None):
                if bank is None:
                    bank = turn[0] % turn[1]
                    turn[0] += 1
                u = Use(bank, bank_uses[bank])
                bank_uses[bank] += 1
                assert key not in uses, key
                uses[key] = u
                if u.nth:
                    pe.wait_ge(bank_free[bank], u.nth)
                return u

            def full(ins, u):
                ins.then_inc(bank_full[u.bank], 1)

            def chunk(src, n, pattern, **dims):
                i = len(chunks)
                view = ring[:, i % SLOTS, 0:n].rearrange(pattern, **dims)
                chunks.append([src, view, None])
                slot_loads[i % SLOTS] += 16 * (2 if isinstance(src, tuple) else 1)
                pe.wait_ge(slot_full[i % SLOTS], slot_loads[i % SLOTS])
                return view

            def release(ins):
                ins.then_inc(chunk_used, 1)
                used[0] += 1
                chunks[-1][2] = (chunk_used, used[0])

            def release_with(u, n=1):
                for c in chunks[-n:]:
                    if c[2] is None:
                        c[2] = (bank_full[u.bank], u.nth + 1)

            def mm(o, l, r, start=True, stop=True):
                return pe.matmul(o, l, r, start=start, stop=stop, skip_group_check=True)

            def kpm(w):
                return w.rearrange("(k p) c -> p k c", p=P)

            def sum_squares(tag, halves):
                pe.wait_ge(sig("squares_ready"), norm_count[0] + 1)
                norm_count[0] += 1
                u = take("norm", tag)
                n = len(halves)
                for k in range(KD):
                    m = mm(ps[:, u.bank, 0:n * T], ones, h[:, 0:n, k, :] if n > 1 else h[:, 0, k, :],
                           k == 0, k == KD - 1)
                full(m, u)

            norm_count = [0]

            def project(tag, w, c0, c1, tiles, done):
                for j, a in enumerate(range(c0, c1, 512)):
                    b = min(a + 512, c1)
                    us = []
                    for half in range(2):
                        v = chunk(kpm(w[half * 512:(half + 1) * 512, a:b]), 4 * (b - a), "p (k c) -> p k c", k=4)
                        for x, t in enumerate(tiles):
                            if half == 0:
                                us.append(take(tag, j, t))
                            for k in range(4):
                                kk = 4 * half + k
                                m = mm(ps[:, us[x].bank, 0:b - a], h[:, t // 2, kk, (t % 2) * P:(t % 2) * P + P],
                                       v[:, k, :], kk == 0, kk == KD - 1)
                            if half == 1:
                                full(m, us[x])
                        if half == 0:
                            release(m)
                    release_with(us[-1])

            def out_project(tag, w, halves, n):
                pe.wait_ge(sig("mixT_ready"), n)
                for c in range(4):
                    v = chunk(kpm(w[:, c * 256:(c + 1) * 256]), SLOT, "p (k c) -> p k c", k=8)
                    for m2 in range(2):
                        u = take(tag, 2 * c + m2)
                        for k in range(KD):
                            m = mm(ps[:, u.bank, 0:halves * T], v[:, k, m2 * P:(m2 + 1) * P],
                                   h[:, 0:2, k, :] if halves > 1 else h[:, 0, k, :], k == 0, k == KD - 1)
                        full(m, u)
                    release_with(u)

            def transpose_mix(tag, src, tiles):
                for t in tiles:
                    pe.wait_ge(sig("mix_ready"), MIXED[tag] + t + 1)
                    for g in range(2):
                        u = take(tag, "mixT", t, g)
                        for j in range(4):
                            f = 4 * g + j
                            m = pe.transpose(ps[:, u.bank, j * P:(j + 1) * P], src[:, t, f * P:(f + 1) * P], ident)
                        full(m, u)

            def ffn(tag, wa, wb, wd, halves, first_bank):
                for m0 in range(KF):
                    src = (kpm(wa[:, m0 * P:(m0 + 1) * P]), kpm(wb[:, m0 * P:(m0 + 1) * P]))
                    v = chunk(src, SLOT, "p (k a c) -> p k a c", k=8, a=2)
                    if halves == 1:
                        u = take(tag, "up", m0, bank=m0 % 4)
                        for a in range(2):
                            for k in range(KD):
                                m = mm(ps[:, u.bank, a * T:(a + 1) * T], v[:, k, a, :], h[:, 0, k, :],
                                       k == 0, k == KD - 1)
                        full(m, u)
                        release_with(u)
                    else:
                        for a in range(2):
                            u = take(tag, "up", m0, a, bank=2 * (m0 % 2) + a)
                            for k in range(KD):
                                m = mm(ps[:, u.bank, :], v[:, k, a, :], h[:, 0:2, k, :], k == 0, k == KD - 1)
                            full(m, u)
                        release_with(u)
                us = {}
                for hf in range(halves):
                    for q in range(4):
                        us[hf, q] = None
                for c in range(KF // 2):
                    v = chunk(kpm(wd[c * 256:(c + 1) * 256, :]), SLOT, "p (k c) -> p k c", k=2)
                    for kk in range(2):
                        kt = 2 * c + kk
                        pe.wait_ge(sig("hidden_ready"), hidden[0] + kt + 1)
                        for hf in range(halves):
                            for m0 in range(KD):
                                if us[hf, m0 // 2] is None:
                                    us[hf, m0 // 2] = take(tag, "down", hf, m0 // 2, bank=(4 + m0 // 2 + 4 * hf) % 8)
                                u = us[hf, m0 // 2]
                                r = g1[:, 0, kt, :] if halves == 1 else g2[:, kt, hf * T:(hf + 1) * T]
                                m = mm(ps[:, u.bank, (m0 % 2) * T:(m0 % 2 + 1) * T], v[:, kk, m0 * P:(m0 + 1) * P], r,
                                       kt == 0 and m0 % 2 == 0, kt == KF - 1)
                                if kt == KF - 1 and m0 % 2 == 1:
                                    full(m, u)
                    if c < KF // 2 - 1:
                        release(m)
                    else:
                        release_with(u)
                hidden[0] += KF

            hidden = [0]

            def attend(at, qk, v):
                n_items, nk = len(at.items), at.keys // P

                def scores(n):
                    u = take(at.tag, "s", n, bank=n % 3)
                    parts = qk(*at.items[n])
                    for i, (l, r, c0, w, st, sp) in enumerate(parts):
                        m = mm(ps[:, u.bank, c0:c0 + w], l, r, st, sp)
                    full(m, u)

                def turn_p(n):
                    pe.wait_ge(sig("att_p"), ITEMS[at.tag] + n + 1)
                    u = take(at.tag, "pT", n, bank=3 if at.tag == "mla" else 3 + n % 3)
                    for k in range(nk):
                        m = pe.transpose(ps[:, u.bank, k * P:(k + 1) * P],
                                         att_p[at.tag][:, n % at.nbuf, k * P:(k + 1) * P], ident)
                    full(m, u)

                def pv(n):
                    t, hd = at.items[n]
                    if hd == 0:
                        attend.o = take(at.tag, "o", t, bank=(4 if at.tag == "mla" else 6) + t % 2)
                    pe.wait_ge(sig("att_pT"), ITEMS[at.tag] + n + 1)
                    for k in range(nk):
                        m = mm(ps[:, attend.o.bank, hd * 64:hd * 64 + 64],
                               att_pT[at.tag][:, n % at.nbuf, k * P:(k + 1) * P], v(k, hd), k == 0, k == nk - 1)
                    if hd == 7:
                        full(m, attend.o)
                    else:
                        m.then_inc(sig("att_pv"), 1)

                scores(0)
                scores(1)
                for n in range(n_items):
                    if n + 2 < n_items:
                        scores(n + 2)
                    if at.tag == "mla":
                        fill(1)
                    turn_p(n)
                    if n:
                        pv(n - 1)
                pv(n_items - 1)

            pe.wait_ge(sig("const_loaded"), 48)

            def turn_mod(i):
                pe.wait_ge(sig("mod_row"), i + 1)
                u = take("modT", i, bank=6)
                for m2 in range(2):
                    m = pe.transpose(ps[:, u.bank, 2 * m2:2 * m2 + 2], modrow[0:2, i % 2, m2 * P:(m2 + 1) * P],
                                     ident[0:2, 0:2])
                full(m, u)

            filled = [0]

            def fill(n):
                for i in range(filled[0], filled[0] + n):
                    l, c = divmod(i, MOD_PIECES // 2)
                    v = chunk(kpm(A["w_mod_2"][l, :, c * 256:(c + 1) * 256]), SLOT, "p (k c) -> p k c", k=8)
                    u = take("mod", i, bank=7)
                    for k in range(KD):
                        m = mm(ps[0:2, u.bank, 0:256], cols[:, COLS["cond"] + 2 * k:COLS["cond"] + 2 * k + 2],
                               v[:, k, :], k == 0, k == KD - 1)
                    full(m, u)
                    release_with(u)
                    if i:
                        turn_mod(i - 1)
                filled[0] += n

            pe.wait_ge(sig("cond_ready"), 1)
            fill(FILL["start"])

            sum_squares("even", [0])
            pe.wait_ge(sig("h_ready"), 1)
            project("even_in", A["w_in_even"][0], 0, EVEN["end"], range(TT), None)
            fill(FILL["latents"])
            for t in range(TT):
                pe.wait_ge(sig("mla_c"), t + 1)
                for g, (a, n) in enumerate(((0, 3), (3, 2))):
                    u = take("mla_cT", t, g)
                    for j in range(n):
                        m = pe.transpose(ps[:, u.bank, j * P:(j + 1) * P], pe_[:, t, (a + j) * P:(a + j + 1) * P], ident)
                    full(m, u)
            pe.wait_ge(sig("mla_cT"), TT)
            for half in range(2):
                v = chunk(A["mla_w_uq"][0][:, half * 384:(half + 1) * 384].rearrange("(k p) c -> p k c", p=P),
                          3 * 384, "p (k c) -> p k c", k=3)
                for t in range(TT):
                    u = take("mla_q", t, half)
                    for k in range(3):
                        m = mm(ps[:, u.bank, 0:384], cT[:, k, t * P:(t + 1) * P], v[:, k, :], k == 0, k == 2)
                    full(m, u)
                release_with(u)
            v = chunk(A["mla_w_ukv"][0].rearrange("(k p) c -> p k c", p=P), SLOT, "p (k c) -> p k c", k=2)
            for half in range(2):
                for t in range(TT):
                    u = take("mla_kv", t, half)
                    for k in range(2):
                        m = mm(ps[:, u.bank, :], cT[:, 3 + k, t * P:(t + 1) * P], v[:, k, half * 512:(half + 1) * 512],
                               k == 0, k == 1)
                    full(m, u)
            release_with(u)
            fill(FILL["heads"])
            pe.wait_ge(sig("mla_heads"), 2)
            for t in range(TT):
                for name, src in (("qT", qh), ("kT", kx)):
                    for g in range(2):
                        u = take("mla", name, t, g)
                        for j in range(4):
                            m = pe.transpose(ps[0:MQK, u.bank, j * P:(j + 1) * P], src[:, t, 4 * g + j, :], ident)
                        full(m, u)
            pe.wait_ge(sig("mla_qT"), 4)
            pe.wait_ge(sig("mla_kT"), 4)
            attend(ATT["mla"],
                   lambda t, x: [(qT[0:MQK, x, t * P:(t + 1) * P], kT[0:MQK, x, :], 0, T, True, True)],
                   lambda k, x: kv[:, k, x, MNOPE:])
            fill(FILL["ret_rope"])
            pe.wait_ge(sig("ret_rope"), 1)
            for t in range(TT):
                for g in range(2):
                    u = take("ret_T", t, g)
                    for j in range(4):
                        src = rqk[:, t, g, 2 * j:2 * j + 2, :].rearrange("p a b -> p (a b)")
                        m = pe.transpose(ps[:, u.bank, j * P:(j + 1) * P], src, ident)
                    full(m, u)
            pe.wait_ge(sig("ret_T"), 4)
            for x in range(RH + 1):
                if x < RH:
                    u = take("ret_s", x, bank=x % 4)
                    b0 = 64 * (x % 2)
                    for s in range(TT):
                        m = mm(ps[:, u.bank, s * T:(s + 1) * T], rT[b0:b0 + 64, 4 + x // 2, s * P:(s + 1) * P],
                               rT[b0:b0 + 64, x // 2, :])
                    full(m, u)
                if x >= 1:
                    y = x - 1
                    if y == 0:
                        ro_use = [take("ret_o", t, bank=4 + t) for t in range(TT)]
                    pe.wait_ge(sig("ret_sdec"), y + 1)
                    for t in range(TT):
                        for s in range(TT):
                            m = mm(ps[:, ro_use[t].bank, y * 64:y * 64 + 64], sdec[:, y % 2, s, t * P:(t + 1) * P],
                                   pe_[:, s, EVEN["rv"] + 64 * y:EVEN["rv"] + 64 * y + 64], s == 0, s == TT - 1)
                        if y == RH - 1:
                            full(m, ro_use[t])
                    if y < RH - 1:
                        m.then_inc(sig("ret_pv"), 1)
            fill(FILL["even_mix"])
            transpose_mix("even", mix0, range(TT))
            out_project("even_out", A["w_out_even"][0], 1, 2 * (MIXED["even"] + TT))

            def first_ffn(l):
                fill(FILL[f"ffn{l}"])
                sum_squares(f"ffn{l}", [0])
                pe.wait_ge(sig("h_ready"), 2 + 2 * l)
                ffn(f"ffn{l}", A["ffn_w_up"][l][:, 0:F], A["ffn_w_up"][l][:, F:2 * F], A["ffn_w_down"][l], 1, 4)

            first_ffn(0)

            fill(FILL["odd"])
            sum_squares("odd", [0])
            pe.wait_ge(sig("h_ready"), 3)
            project("odd_in", A["w_in_odd"][0], 0, ODD["end"], range(TT), None)
            pe.wait_ge(sig("proj_act"), PROJ["odd_in"])
            pe.wait_ge(sig("proj_dve"), PROJ["odd_in"])
            for t in range(TT):
                u = take("gla_gT", t)
                for d in range(2):
                    a = ODD["gf"] + GR * d
                    m = pe.transpose(ps[0:GR, u.bank, d * P:(d + 1) * P], po[:, t, a:a + GR], ident)
                full(m, u)
            for t in range(TT):
                for g in range(2):
                    u = take("gla_T", t, g)
                    for j in range(4):
                        a = 512 * g + P * j
                        m = pe.transpose(ps[:, u.bank, j * P:(j + 1) * P], po[:, t, a:a + P], ident)
                    full(m, u)
            pe.wait_ge(sig("gla_gT"), TT)
            pe.wait_ge(sig("gla_const"), 80)
            for d in range(2):
                for t in range(TT):
                    u = take("gla_la", d, t)
                    mm(ps[:, u.bank, :], gaT[0:GR, d, t * P:(t + 1) * P], wg[0:GR, d, :], True, False)
                    m = mm(ps[:, u.bank, :], cst[0:1, CST["ones"]:CST["ones"] + P], gbias[0:1, d, :], False, True)
                    full(m, u)
            fill(FILL["gla_gates"])
            for d in range(2):
                for t in range(TT):
                    pe.wait_ge(sig("gla_la"), 2 * d + t + 1)
                    u = take("gla_kd", d, t)
                    m = mm(ps[:, u.bank, :], glam[:, 3 * d + 2, :], la[:, d, t, :])
                    full(m, u)
            pe.wait_ge(sig("gla_T"), 2 * TT)
            for x in range(GH):
                oacc = None
                for d in range(2):
                    n = 2 * x + d
                    u = take("gla_b", n)
                    for w in range(2):
                        for t in range(TT):
                            m = mm(ps[:, u.bank, w * T + t * P:w * T + (t + 1) * P],
                                   la[:, d, t, x * P:(x + 1) * P], glam[:, 3 * d + w, :])
                    full(m, u)
                    pe.wait_ge(sig("gla_kdT"), 4)
                    for i in range(3):
                        c = i if d == 0 else 3 - i
                        u = take("gla_st", n, i)
                        b0 = GC * (c % 2)
                        m = mm(ps[:, u.bank, 0:GV],
                               kdT[b0:b0 + GC, d, c // 2, x * P:(x + 1) * P],
                               po[b0:b0 + GC, c // 2, ODD["v"] + x * GV:ODD["v"] + (x + 1) * GV])
                        full(m, u)
                    fill(FILL["gla"] // (2 * GH))
                    pe.wait_ge(sig("gla_qk"), n + 1)
                    u = take("gla_A", n)
                    for t in range(TT):
                        m = mm(ps[:, u.bank, t * P:(t + 1) * P], gqkx[:, d, 1, t * P:(t + 1) * P],
                               gqkx[:, d, 0, t * P:(t + 1) * P])
                    full(m, u)
                pe.wait_ge(sig("gla_Am"), 2 * x + 2)
                pe.wait_ge(sig("gla_states"), 2 * x + 2)
                u = take("gla_o", x)
                for t in range(TT):
                    parts = []
                    for d in range(2):
                        parts.append((slice(0, P), gA[:, d, t, :],
                                      po[:, t, ODD["v"] + x * GV:ODD["v"] + (x + 1) * GV]))
                    first = True
                    for (_, l, r) in parts:
                        mm(ps[:, u.bank, t * GV:(t + 1) * GV], l, r, first, False)
                        first = False
                    for d in range(2):
                        for c in (2 * t, 2 * t + 1):
                            i = c if d == 0 else 3 - c
                            if i == 0:
                                continue
                            b0 = GC * (c % 2)
                            m = mm(ps[b0:b0 + GC, u.bank, t * GV:(t + 1) * GV], gqkx[:, d, 2, c * GC:(c + 1) * GC],
                                   gst[:, d, i - 1, :], False, True)
                full(m, u)
            fill(FILL["odd_mix"])
            transpose_mix("odd", po, range(TT))
            out_project("odd_out", A["w_out_odd"][0], 1, 2 * (MIXED["odd"] + TT))
            first_ffn(1)

            turn_mod(MOD_PIECES - 1)
            turn[1] = 8
            for l in range(2):
                sum_squares(f"n1_{l}", [0, 1])
                pe.wait_ge(sig("h_ready"), 5 + 2 * l)
                w = A["w_in_2"][l]
                xs, both = range(TT), range(4)
                project(f"q{l}", w, 0, 512, both if l == 0 else xs, None)
                project(f"kv{l}", w, 512, 768, both, None)
                for c in range(2):
                    v = chunk(kpm(w[:, 768 + c * 256:768 + (c + 1) * 256]), SLOT, "p (k c) -> p k c", k=8)
                    for m2 in range(2):
                        u = take("conv", l, 2 * c + m2)
                        for k in range(KD):
                            if l == 0 or c == 1:
                                m = mm(ps[:, u.bank, :], v[:, k, m2 * P:(m2 + 1) * P], h[:, :, k, :],
                                       k == 0, k == KD - 1)
                            else:
                                m = mm(ps[:, u.bank, 0:T], v[:, k, m2 * P:(m2 + 1) * P], h[:, 0, k, :],
                                       k == 0, k == KD - 1)
                        full(m, u)
                    release_with(u)
                project(f"mv{l}", w, 1280, 1792, both, None)
                project(f"o{l}", w, 1792, 2304, both if l == 0 else xs, None)
                v = chunk(kpm(w[:, 2304:2320]), 128, "p (k c) -> p k c", k=8)
                u = take("gT", l)
                for t in both:
                    for k in range(KD):
                        m = mm(ps[:, u.bank, 16 * t:16 * t + 16], h[:, t // 2, k, (t % 2) * P:(t % 2) * P + P],
                               v[:, k, :], k == 0, k == KD - 1)
                full(m, u)
                release_with(u)
                pe.wait_ge(sig("gT"), l + 1)
                for g in range(4):
                    u = take("gates", l, g)
                    for t in both:
                        m = pe.transpose(ps[0:4, u.bank, t * P:(t + 1) * P], gT[:, t, 4 * g:4 * g + 4], ident)
                    full(m, u)
                pe.wait_ge(sig("att_rope"), 2 * (l + 1))
                for t in both:
                    if t < 2 or l == 0:
                        u = take("aqT", l, t)
                        for j in range(4):
                            src = ro[:, t, j * P:(j + 1) * P] if t < 2 else p2[:, t, j * P:(j + 1) * P]
                            m = pe.transpose(ps[:, u.bank, j * P:(j + 1) * P], src, ident)
                        full(m, u)
                for g in range(AG):
                    u = take("akT", l, g)
                    for t in both:
                        src = kdup[:, t, g, :, :].rearrange("p a b -> p (a b)")
                        m = pe.transpose(ps[:, u.bank, t * P:(t + 1) * P], src, ident)
                    full(m, u)
                pe.wait_ge(sig("aqT"), 4 if l == 0 else 6)
                pe.wait_ge(sig("akT"), 2 * (l + 1))
                pe.wait_ge(sig("wmask"), 16)

                def window(t, x):
                    b0 = 64 * (x % 2)
                    q = aqT[b0:b0 + 64, x // 2, t * P:(t + 1) * P]
                    return [(q, akT[b0:b0 + 64, x // 4, 0:T], 0, T, True, False),
                            (ident, wmask[:, t, :], 0, T, False, True),
                            (q, akT[b0:b0 + 64, x // 4, T:2 * T], T, T, True, True)]

                attend(ATT[f"wx{l}"], window, lambda k, x: p2[:, k, 640 + 64 * (x // 4):704 + 64 * (x // 4)])
                if l == 0:
                    def to_ctx(t, x):
                        b0 = 64 * (x % 2)
                        return [(aqT[b0:b0 + 64, x // 2, t * P:(t + 1) * P], akT[b0:b0 + 64, x // 4, T:2 * T],
                                 0, T, True, True)]

                    attend(ATT["wc0"], to_ctx, lambda k, x: p2[:, 2 + k, 640 + 64 * (x // 4):704 + 64 * (x // 4)])
                pe.wait_ge(sig("lrows"), l + 1)
                u = take("lcols", l)
                for t in both:
                    for w_, src in enumerate((gates, brow)):
                        for d in range(2):
                            c0 = (t * 4 + w_ * 2 + d) * 4
                            s_ = (gates[0:4, 2 * d, t * P:(t + 1) * P] if w_ == 0 else brow[0:4, d, t * P:(t + 1) * P])
                            m = pe.transpose(ps[:, u.bank, c0:c0 + 4], s_, ident[0:4, 0:4])
                full(m, u)
                pe.wait_ge(sig("conv_done"), 4 * (l + 1))
                pe.wait_ge(sig("vaug_ones"), l + 1)
                pe.wait_ge(sig("proj_act"), PROJ[f"mv{l}"])
                pe.wait_ge(sig("proj_dve"), PROJ[f"mv{l}"])
                steps = lsteps(l)

                def row_max(n):
                    sq, x, d = steps[n]
                    if d == 0:
                        b0 = 64 * (x % 2)
                        for i, s in enumerate(STILES[sq]):
                            if i % 2 == 0:
                                u = take("ls", l, sq, x, i // 2, bank=i // 2 + 2 * (x % 2))
                            m = mm(ps[:, u.bank, (i % 2) * T:(i % 2 + 1) * T],
                                   conv[b0:b0 + 64, 2 + x // 2, s * P:(s + 1) * P],
                                   conv[b0:b0 + 64, x // 2, sq * T:(sq + 1) * T])
                            if i % 2 == 1:
                                full(m, u)
                    u = take("lm", l, n, bank=4 + n % 2)
                    full(mm(ps[:, u.bank, 0:T], cst[0:4, CST["sel4"] + x * P:CST["sel4"] + (x + 1) * P],
                            mrow[0:4, d, sq * T:(sq + 1) * T]), u)

                row_max(0)
                for n, (sq, x, d) in enumerate(steps):
                    if n + 1 < len(steps):
                        row_max(n + 1)
                    pe.wait_ge(sig("lp"), 16 * l + n + 1)
                    u = take("lo", l, n, bank=6 + n % 2)
                    for t in range(TT):
                        tiles = [i for i, s in enumerate(STILES[sq])
                                 if s // 2 != sq or (s % 2 <= t if d == 0 else s % 2 >= t)]
                        for i in tiles:
                            m = mm(ps[:, u.bank, t * 129:t * 129 + 129], lp[n % 2][:, i, t * P:(t + 1) * P],
                                   vaug[:, STILES[sq][i], x, :], i == tiles[0], i == tiles[-1])
                    full(m, u)
                turn[0] = 0
                tiles = both if l == 0 else xs
                transpose_mix(f"mix{l}", mix2, tiles)
                out_project(f"out{l}", A["w_out_2"][l], 2 if l == 0 else 1, 2 * (MIXED[f"mix{l}"] + len(tiles)))
                sum_squares(f"n2_{l}", [0, 1] if l == 0 else [0])
                pe.wait_ge(sig("h_ready"), 6 + 2 * l)
                if l == 0:
                    ffn("ffn2", A["ffn_w1_2"][0], A["ffn_w3_2"][0], A["ffn_w2_2"][0], 2, 4)

            us = []
            for t in range(TT):
                u = take("router", t)
                us.append(u)
            v = chunk(kpm(A["w_router_2"][0]), 64, "p (k c) -> p k c", k=8)
            for t in range(TT):
                for k in range(KD):
                    m = mm(ps[:, us[t].bank, 0:NE], h[:, 0, k, t * P:(t + 1) * P], v[:, k, :], k == 0, k == KD - 1)
                full(m, us[t])
            release_with(us[-1])
            u = take("combT")
            for t in range(TT):
                pe.wait_ge(sig("combine"), t + 1)
                m = pe.transpose(ps[0:NE, u.bank, t * P:(t + 1) * P], stat[:, 16 * t:16 * t + NE], ident)
            full(m, u)
            pe.wait_ge(sig("combT"), 1)
            pe.wait_ge(sig("sel8"), 16)
            for e in range(NE):
                if e % 2 == 0:
                    u = take("comb", e // 2)
                m = mm(ps[:, u.bank, (e % 2) * T:(e % 2 + 1) * T], sel8[0:NE, e * P:(e + 1) * P], combT[0:NE, :])
                if e % 2 == 1:
                    full(m, u)
            moe_acc = [take("moe_acc", q, bank=4 + q) for q in range(4)]
            pe.wait_ge(sig("zero_ready"), 1)
            for q in range(4):
                mm(ps[:, 4 + q, :], temp[:, 0:P], temp[:, 0:512], True, False)
            base_chunk, base_used = len(chunks), used[0]
            base_bank = bank_uses[0:2]
            loads = list(slot_loads)
            plan = []
            for n in range(2 * CPE):
                e, c = divmod(n, CPE)
                slot = (base_chunk + n) % SLOTS
                loads[slot] += 32 if c < KF else 16
                if c < KF:
                    tells = (bank_full[c % 2], base_bank[c % 2] + e * (KF // 2) + c // 2 + 1, KF)
                else:
                    tells = (chunk_used, base_used + e * (KF // 2) + c - KF + 1, KF)
                plan.append((slot, loads[slot], tells))
            per_slot = [b - a for a, b in zip(slot_loads, loads)]
            moe.update(chunk=base_chunk, used=base_used, bank=base_bank, plan=plan, hidden=hidden[0])
            for b in range(2):
                pe.wait_ge(bank_free[b], base_bank[b])
            with pe.Fori(0, NE // 2) as i:
                for e in range(2):
                    for m0 in range(KF):
                        s, loaded, _ = plan[e * CPE + m0]
                        v = ring[:, s, :].rearrange("p (k a c) -> p k a c", k=8, a=2)
                        pe.wait_ge(slot_full[s], i * per_slot[s] + loaded)
                        b = m0 % 2
                        pe.wait_ge(bank_free[b], i * KF + (base_bank[b] + e * (KF // 2) + m0 // 2))
                        for a in range(2):
                            for k in range(KD):
                                m = mm(ps[:, b, a * T:(a + 1) * T], v[:, k, a, :], h[:, 0, k, :], k == 0, k == KD - 1)
                        m.then_inc(bank_full[b], 1)
                    for c in range(KF // 2):
                        s, loaded, _ = plan[e * CPE + KF + c]
                        v = ring[:, s, :].rearrange("p (k c) -> p k c", k=2)
                        pe.wait_ge(slot_full[s], i * per_slot[s] + loaded)
                        for kk in range(2):
                            kt = 2 * c + kk
                            pe.wait_ge(sig("hidden_ready"), i * (2 * KF) + (hidden[0] + e * KF + kt + 1))
                            for m0 in range(KD):
                                m = mm(ps[:, 4 + m0 // 2, (m0 % 2) * T:(m0 % 2 + 1) * T],
                                       v[:, kk, m0 * P:(m0 + 1) * P], g1[:, e, kt, :], False, False)
                        m.then_inc(chunk_used, 1)
            pe.wait_ge(sig("zero_ready"), 1)
            for q in range(4):
                full(mm(ps[:, 4 + q, :], temp[:, 0:P], temp[:, 0:512], False, True), moe_acc[q])
            for b in range(2):
                bank_uses[b] += NE * KF // 2
            turn[0] = 0
            sum_squares("final", [0])

        @block.sync
        def _(sp):
            def load(src, view, slot):
                if isinstance(src, tuple):
                    for a in range(2):
                        sp.dma_start(view[:, :, a, :], src[a]).then_inc(slot_full[slot], 16)
                else:
                    sp.dma_start(view, src).then_inc(slot_full[slot], 16)

            def kpm(w):
                return w.rearrange("(k p) c -> p k c", p=P)

            sp.dma_start(cst[:, :], A["consts"][:, 0:NKEEP]).then_inc(sig("const_loaded"), 16)
            sp.dma_start(cols[:, :], A["cols"]).then_inc(sig("const_loaded"), 16)
            sp.dma_start(rows[:, :], A["rows"].partition_broadcast(P)).then_inc(sig("const_loaded"), 16)
            sp.dma_start(res[:, 0, :, :], A["xT"]).then_inc(sig("x_loaded"), 16)
            for n, (src, view, _) in enumerate(chunks):
                if n >= SLOTS:
                    sp.wait_ge(*chunks[n - SLOTS][2])
                load(src, view, n % SLOTS)

            def load_expert(pair, n):
                e, c = divmod(n, CPE)
                slot = moe["plan"][n][0]
                x = pair * 2 + e
                if c < KF:
                    src = tuple(kpm(A[w][0, x, :, c * P:(c + 1) * P]) for w in ("exp_w1_2", "exp_w3_2"))
                    load(src, ring[:, slot, :].rearrange("p (k a c) -> p k a c", k=8, a=2), slot)
                else:
                    src = kpm(A["exp_w2_2"][0, x, (c - KF) * 256:(c - KF + 1) * 256, :])
                    load(src, ring[:, slot, :].rearrange("p (k c) -> p k c", k=2), slot)

            for n in range(SLOTS):
                sp.wait_ge(*chunks[moe["chunk"] + n - SLOTS][2])
                load_expert(0, n)
            with sp.Fori(0, NE // 2 - 1) as i:
                for n in range(SLOTS, 2 * CPE):
                    sem, value, per = moe["plan"][n - SLOTS][2]
                    sp.wait_ge(sem, i * per + value)
                    sp.sem_inc(sig("slot_open"), 1)
                    load_expert(i, n)
                for n in range(SLOTS):
                    sem, value, per = moe["plan"][2 * CPE - SLOTS + n][2]
                    sp.wait_ge(sem, i * per + value)
                    sp.sem_inc(sig("slot_open"), 1)
                    load_expert(i + 1, n)
            for n in range(SLOTS, 2 * CPE):
                sem, value, per = moe["plan"][n - SLOTS][2]
                sp.wait_ge(sem, (NE // 2 - 1) * per + value)
                load_expert(NE // 2 - 1, n)

        @block.gpsimd
        def _(pool):
            C = A["consts"]
            pool.dma_start(posi, A["pos"]).then_inc(sig("pos_loaded"), 16)
            pool.wait_ge(sig("mla_qT"), 4)
            pool.dma_start(areaA[:, 5440:6464], C[:, CST["relp"]:CST["relp"] + 1024]).then_inc(sig("rel_loaded"), 16)
            pool.wait_ge(sig("residual"), 1)
            pool.dma_start(areaB[:, 2048:3072], C[:, CST["gla_m"]:CST["gla_m"] + 1024]).then_inc(sig("gla_const"), 16)
            for d, x in enumerate(("fwd", "bwd")):
                pool.dma_start(wg[0:GR, d, :], A[f"gla_w_gate_{x}"][0]).then_inc(sig("gla_const"), 16)
                pool.dma_start(gbias[0:1, d, :], A[f"gla_b_gate_{x}"]).then_inc(sig("gla_const"), 16)
            pool.wait_ge(sig("mod_done"), 1)
            pool.dma_start(res[:, 1, :, :], A["ctxT"]).then_inc(sig("ctx_loaded"), 16)
            pool.wait_ge(sig("residual"), 4)
            pool.dma_start(areaB[:, 5120:5632], C[:, CST["wmask"]:CST["wmask"] + 512]).then_inc(sig("wmask"), 16)
            for l in range(2):
                pool.wait_ge(sig("att_done"), l + 1)
                pool.dma_start(areaB[:, 2048:3072], C[:, CST["lmask"]:CST["lmask"] + 1024]).then_inc(sig("lmask"), 16)
                pool.wait_ge(sig("lmask"), 16 * (l + 1))
                for n, (sq, x, d) in enumerate(lsteps(l)):
                    pool.wait_ge(sig("lweights"), 16 * l + n + 1)
                    ns = len(STILES[sq])
                    own = lp[n % 2][:, ns - 2:ns, :]
                    pool.tensor_tensor(own, own, lmask[:, d, :, :], ALU.mult).then_inc(sig("lp"), 1)
            pool.wait_ge(sig("residual"), 7)
            pool.dma_start(areaB[:, 4352:5376], C[:, CST["sel8"]:CST["sel8"] + 1024]).then_inc(sig("sel8"), 16)
            pool.wait_ge(sig("out_ready"), 1)
            pool.dma_start(out, h[:, 0, :, :]).then_inc(sig("out_stored"), 16)
            pool.wait_ge(sig("out_stored"), 16)

        def look(engine, *key):
            u = uses[key]
            engine.wait_ge(bank_full[u.bank], u.nth + 1)
            return u

        def free(lane, ins, u, name=None):
            ins.then_inc(bank_free[u.bank], 1)
            lane.engine.wait_ge(bank_free[u.bank], u.nth + 1)
            if name:
                lane.engine.sem_inc(sig(name), 1)

        def evacuate(lane, copy, tag, c0, c1, tiles, mine, dst, name):
            for j, a in enumerate(range(c0, c1, 512)):
                b = min(a + 512, c1)
                for t in tiles:
                    if t % 2 == mine:
                        u = look(lane.engine, tag, j, t)
                        ins = copy(dst(t, a - c0, b - c0), ps[:, u.bank, 0:b - a])
                        free(lane, ins, u)
            lane.engine.sem_inc(sig(name), 1)

        def in_stages(l):
            b = range(4)
            x = b if l == 0 else range(TT)
            return [(f"q{l}", 0, 512, x, lambda t, a, c: p2[:, t, a:c]),
                    (f"kv{l}", 512, 768, b, lambda t, a, c: p2[:, t, 512 + a:512 + c])], \
                   [(f"mv{l}", 1280, 1792, b, lambda t, a, c: vaug[:, t, :, 0:LV]),
                    (f"o{l}", 1792, 2304, x, lambda t, a, c: p2[:, t, 768 + a:768 + c])]

        def pv_done(engine, at, n):
            t, hd = at.items[n]
            if hd == 7:
                look(engine, at.tag, "o", t)
            else:
                engine.wait_ge(sig("att_pv"), ITEMS[at.tag] * 7 // 8 + sum(1 for i in at.items[:n + 1] if i[1] < 7))

        @block.scalar
        def _(act):
            L = Lane(act, sig, "act_step")

            def copy(dst, src):
                return act.activation(dst, src, ACT.Copy)

            def rstd(dst, src, n):
                L.step(act.activation(dst, src, ACT.Ln, bias=eps, scale=1.0 / n))

            def norm(tag, n, before):
                act.wait_ge(*before)
                L.tell(act.activation(h[:, 0:n, :, :], res[:, 0:n, :, :], ACT.Square), "squares_ready")
                u = look(act, "norm", tag)
                free(L, act.activation(temp[:, 0:n * T], ps[:, u.bank, 0:n * T], ACT.Ln, bias=eps, scale=1.0 / D), u)
                L.tell(act.activation(temp[:, 0:n * T], temp[:, 0:n * T], ACT.Exp, scale=-0.5), "rstd_ready")

            def attend(at):
                k0 = at.keys
                for n, (t, hd) in enumerate(at.items):
                    L.wait("att_m", ITEMS[at.tag] + n + 1)
                    if n >= at.nbuf:
                        look(act, at.tag, "pT", n - at.nbuf)
                    u = look(act, at.tag, "s", n)
                    free(L, act.activation(att_p[at.tag][:, n % at.nbuf, 0:k0], ps[:, u.bank, 0:k0], ACT.Exp,
                                           bias=stat[:, n:n + 1], scale=at.scale, accum_out=stat[:, 16 + n:17 + n]),
                         u, "att_p")
                    if at.tag == "mla":
                        fill(1)
                    if hd == 7 and at.tag != "mla":
                        L.wait("att_sink", SINKS[at.tag] + n // 8 + 1)
                        L.tell(act.activation(stat[:, 32 + n - 7:33 + n], stat[:, 32 + n - 7:33 + n], ACT.Exp),
                               "att_esink")

            filled = [0]

            def turned_mod(i):
                l, c = divmod(i, MOD_PIECES // 2)
                u = look(act, "modT", i)
                free(L, copy(mods[:, l, 2 * c:2 * c + 2, :], ps[:, u.bank, 0:4].rearrange("p (a b) -> p a b", a=2)), u)

            def fill(n):
                for i in range(filled[0], filled[0] + n):
                    u = look(act, "mod", i)
                    free(L, copy(modrow[0:2, i % 2, :], ps[0:2, u.bank, 0:256]), u, "mod_row")
                    if i:
                        turned_mod(i - 1)
                filled[0] += n

            act.wait_ge(sig("const_loaded"), 48)
            c = cols[:, COLS["cond"]:COLS["cond"] + 16]
            L.tell(act.activation(c, c, ACT.Silu), "cond_ready")
            u16 = stat[:, 80:96]
            L.step(act.activation(u16, rows[:, ROWS["theta"]:ROWS["theta"] + 16], ACT.Exp, scale=-float(np.log(2.0))))
            L.tell(act.activation(temp[:, 256:272], u16, ACT.Ln, scale=-1.0, bias=1.0), "theta_ready")
            L.wait("angle_ready", 1)
            L.step(act.activation(sin, ang, ACT.Sin))
            L.tell(act.activation(cos, ang, ACT.Sin, scale=0.5), "sin_ready")

            fill(FILL["start"])
            norm("even", 1, (sig("x_loaded"), 16))
            evacuate(L, copy, "even_in", 0, EVEN["end"], range(TT), 0, lambda t, a, b: pe_[:, t, a:b], "proj_act")
            L.wait("proj_dve", PROJ["even_in"])
            for t in range(TT):
                for i, (a, n) in enumerate(((0, CQ), (CQ, CKV))):
                    L.step(act.activation(spare[:, 0:n], pe_[:, t, a:a + n], ACT.Square,
                                          accum_out=stat[:, 2 * i + t:2 * i + t + 1]))
            for i, n in enumerate((CQ, CKV)):
                rstd(stat[:, 2 * i:2 * i + 2], stat[:, 2 * i:2 * i + 2], n)
            L.tell(act.activation(stat[:, 0:4], stat[:, 0:4], ACT.Exp, scale=-0.5), "mla_c_rstd")
            fill(FILL["latents"])
            for t in range(TT):
                r = pe_[:, t, EVEN["rg"]:EVEN["end"]]
                L.step(act.activation(r, r, ACT.Silu))
            act.sem_inc(sig("rg_ready"), 1)
            for half in range(2):
                for t in range(TT):
                    u = look(act, "mla_q", t, half)
                    dst = qh[:, t, 4 * half:4 * half + 4, :].rearrange("p a b -> p (a b)")
                    free(L, copy(dst, ps[:, u.bank, 0:384]), u)
            for half in range(2):
                for t in range(TT):
                    u = look(act, "mla_kv", t, half)
                    dst = kv[:, t, 4 * half:4 * half + 4, :].rearrange("p a b -> p (a b)")
                    free(L, copy(dst, ps[:, u.bank, :]), u)
            act.sem_inc(sig("mla_qkv"), 1)
            fill(2)
            L.wait("mla_sumsq", 1)
            rstd(stat[:, 0:32], stat[:, 0:32], MQK)
            L.tell(act.activation(stat[:, 0:32], stat[:, 0:32], ACT.Exp, scale=-0.5), "mla_rstd")
            fill(FILL["heads"] - 2)
            for t in range(TT):
                for g in range(2):
                    u = look(act, "mla", "qT", t, g)
                    free(L, copy(qT[0:MQK, 4 * g:4 * g + 4, t * P:(t + 1) * P],
                                 ps[0:MQK, u.bank, :].rearrange("p (a b) -> p a b", a=4)), u, "mla_qT")
            attend(ATT["mla"])
            fill(FILL["ret_rope"])
            for t in range(TT):
                for g in range(2):
                    u = look(act, "ret_T", t, g)
                    free(L, copy(rT[:, 4 * g:4 * g + 4, t * P:(t + 1) * P],
                                 ps[:, u.bank, :].rearrange("p (a b) -> p a b", a=4)), u, "ret_T")
            for x in range(RH):
                L.wait("ret_e", x + 1)
                L.tell(act.activation(decay[:, x % 2, :, :], decay[:, x % 2, :, :], ACT.Exp), "ret_d")
            L.wait("ret_sumsq", 1)
            rstd(stat[:, 0:16], stat[:, 0:16], RD)
            L.tell(act.activation(stat[:, 0:16], stat[:, 0:16], ACT.Exp, scale=-0.5), "ret_rstd")

            fill(FILL["even_mix"])

            def ffn1(l):
                fill(FILL[f"ffn{l}"])
                norm(f"ffn{l}", 1, (sig("residual"), 1 + 2 * l))
                for m in range(KF):
                    L.wait("conv1", KF * l + m + 1)
                    L.tell(act.activation(fsil[:, m % 2, 0:T], fconv[:, m % 2, 0:T], ACT.Silu), "silu1")

            ffn1(0)

            fill(FILL["odd"])
            norm("odd", 1, (sig("residual"), 2))
            evacuate(L, copy, "odd_in", 0, ODD["end"], range(TT), 0, lambda t, a, b: po[:, t, a:b], "proj_act")
            L.wait("proj_dve", PROJ["odd_in"])
            for t in range(TT):
                for g in range(2):
                    u = look(act, "gla_T", t, g)
                    free(L, copy(gqk[:, 4 * g:4 * g + 4, t * P:(t + 1) * P],
                                 ps[:, u.bank, :].rearrange("p (a b) -> p a b", a=4)), u, "gla_T")
            for i in range(4):
                u = look(act, "gla_la", i // 2, i % 2)
                if i >= 2:
                    L.wait("gla_la", i - 1)
                b = temp[:, 512 * (i % 2):512 * (i % 2) + 512]
                L.step(act.activation(b, ps[:, u.bank, :], ACT.Abs))
                L.step(act.activation(b, b, ACT.Exp, scale=-1.0))
                L.tell(act.activation(b, b, ACT.Ln, bias=1.0), "gla_soft")
            fill(FILL["gla_gates"])
            for i in range(4):
                u = look(act, "gla_kd", i // 2, i % 2)
                if i < 2:
                    L.wait("gla_la", 3 + i)
                else:
                    L.wait("gla_kdT", i - 1)
                free(L, act.activation(temp[:, 512 * (i % 2):512 * (i % 2) + 512], ps[:, u.bank, :], ACT.Exp), u, "gla_kd")
            for t in range(TT):
                r = po[:, t, ODD["r"]:ODD["gf"]]
                L.step(act.activation(r, r, ACT.Silu))
            act.sem_inc(sig("gr_ready"), 1)
            for n in range(2 * GH):
                u = look(act, "gla_b", n)
                if n:
                    L.wait("gla_states", n)
                L.step(act.activation(gex[:, 0:2, :], ps[:, u.bank, :].rearrange("p (a b) -> p a b", a=2), ACT.Exp))
                free(L, act.activation(gex[:, 2, :], ps[:, u.bank, T:2 * T], ACT.Exp, scale=-1.0), u, "gla_ex")
                fill(FILL["gla"] // (2 * GH))
            L.wait("gla_sumsq", 1)
            rstd(stat[:, 0:8], stat[:, 0:8], GV)
            L.tell(act.activation(stat[:, 0:8], stat[:, 0:8], ACT.Exp, scale=-0.5), "gla_rstd")
            fill(FILL["odd_mix"])
            ffn1(1)
            turned_mod(MOD_PIECES - 1)
            act.sem_inc(sig("mod_done"), 1)

            for l in range(2):
                if l == 0:
                    L.wait("ctx_loaded", 16)
                norm(f"n1_{l}", 2, (sig("residual"), 4 + 2 * l))
                before, after = in_stages(l)
                for tag, a, b, tiles, dst in before:
                    evacuate(L, copy, tag, a, b, tiles, 0, dst, "proj_act")
                for c in range(4):
                    L.wait("conv2", 4 * l + c + 1)
                    v = conv[:, c, :] if l == 0 or c >= 2 else conv[:, c, 0:T]
                    L.tell(act.activation(v, v, ACT.Silu), "conv_done")
                for tag, a, b, tiles, dst in after:
                    evacuate(L, copy, tag, a, b, tiles, 0, dst, "proj_act")
                for g in range(4):
                    u = look(act, "gates", l, g)
                    free(L, act.activation(gates[0:4, g, :], ps[0:4, u.bank, :], ACT.Tanh,
                                           bias=cols[0:4, COLS["b_gates"] + 4 * l + g:COLS["b_gates"] + 4 * l + g + 1],
                                           scale=1.0 / CAP), u)
                for d in range(2):
                    f = gates[0:4, 2 * d + 1, :]
                    L.step(act.activation(f, f, ACT.Exp, scale=-CAP))
                    L.step(act.activation(f, f, ACT.Ln, bias=1.0))
                act.sem_inc(sig("gates_ready"), 1)
                L.wait("proj_dve", PROJ[f"o{l}"])
                for t in (range(4) if l == 0 else range(TT)):
                    o = p2[:, t, 768:1280]
                    L.step(act.activation(o, o, ACT.Sigmoid))
                act.sem_inc(sig("o_ready"), 1)
                for g in range(AG):
                    u = look(act, "akT", l, g)
                    free(L, copy(akT[:, g, :], ps[:, u.bank, :]), u, "akT")
                attend(ATT[f"wx{l}"])
                if l == 0:
                    attend(ATT["wc0"])
                L.wait("lc_ready", l + 1)
                L.tell(act.activation(temp[:, 64:128], temp[:, 0:64], ACT.Exp, scale=-1.0), "lem_ready")
                lc = temp[:, 0:64].rearrange("p (t w d h) -> p t w d h", t=4, w=2, d=2)
                for n, (sq, x, d) in enumerate(lsteps(l)):
                    ns = len(STILES[sq])
                    L.wait("lw", 16 * l + n + 1)
                    own = lw[n % 2][:, ns - 2:ns, :]
                    L.step(act.activation(own, own, ACT.Exp, scale=-1.0))
                    u = uses["lm", l, n]
                    for i in range(ns - 2):
                        L.step(act.activation(lw[n % 2][:, i, :], ps[:, u.bank, 0:T], ACT.Exp,
                                              bias=lc[:, STILES[sq][i], 0, d, x:x + 1], scale=-1.0))
                    act.sem_inc(bank_free[u.bank], 1)
                    act.sem_inc(sig("lexp"), 1)
                L.wait("merge_sumsq", l + 1)
                rstd(stat[:, 0:16], stat[:, 0:16], LV)
                rstd(stat[:, 16:20], stat[:, 16:20], 512)
                L.tell(act.activation(stat[:, 0:20], stat[:, 0:20], ACT.Exp, scale=-0.5), "merge_rstd")
                norm(f"n2_{l}", 2 - l, (sig("residual"), 5 + 2 * l))
                if l == 0:
                    for m in range(KF):
                        u = look(act, "ffn2", "up", m, 0)
                        if m >= 2:
                            L.wait("hidden_ready", 2 * KF + m - 1)
                        free(L, act.activation(fsil[:, m % 2, :], ps[:, u.bank, :], ACT.Silu), u)
            for t in range(TT):
                L.wait("top_ready", t + 1)
                L.tell(act.activation(temp[:, 600:601], temp[:, 600:601], ACT.Exp), "top_exp")
            with act.Fori(0, NE // 2) as i:
                for e in range(2):
                    for m in range(KF):
                        b = m % 2
                        act.wait_ge(bank_full[b], i * KF + (moe["bank"][b] + e * (KF // 2) + m // 2 + 1))
                        act.wait_ge(sig("hidden_ready"), i * (2 * KF) + (moe["hidden"] + e * KF + m - 1))
                        act.activation(fsil[:, b, 0:T], ps[:, b, 0:T], ACT.Silu).then_inc(sig("moe_silu"), 1)
            norm("final", 1, (sig("residual"), 8))

        @block.vector
        def _(dve):
            L = Lane(dve, sig, "dve_step")
            S, TTN, TS, STT = L.step, dve.tensor_tensor, dve.tensor_scalar, dve.scalar_tensor_tensor

            def copy(dst, src):
                return dve.tensor_copy(dst, src)

            def bc(v, axis, shape):
                return v.unsqueeze(axis).broadcast_to(shape)

            norms = [0]

            def norm(n, gain, shift=None, name="h_ready"):
                norms[0] += 1
                L.wait("rstd_ready", norms[0])
                for hf in range(n):
                    for k in range(KD):
                        S(STT(out=h[:, hf, k, :], in0=res[:, hf, k, :], scalar=gain(hf, k),
                              in1=temp[:, hf * T:(hf + 1) * T], op0=ALU.mult, op1=ALU.mult))
                        if shift:
                            S(TS(h[:, hf, k, :], h[:, hf, k, :], shift(hf, k), None, ALU.add))
                dve.sem_inc(sig(name), 1)

            def rope(x1, x2, y1, y2, c, s, t1, t2):
                S(TTN(t1, x1, s, ALU.mult))
                S(TTN(t2, x2, s, ALU.mult))
                S(TTN(y1, x1, c, ALU.mult))
                S(TTN(y2, x2, c, ALU.mult))
                S(TTN(y1, y1, t2, ALU.subtract))
                S(TTN(y2, y2, t1, ALU.add))

            def attend(at, out_of):
                items, sink = at.items, at.tag != "mla"

                def score_max(n):
                    u = look(dve, at.tag, "s", n)
                    S(dve.tensor_reduce(stat[:, 64 + n:65 + n], ps[:, u.bank, 0:at.keys], AX.X, ALU.max))
                    if sink:
                        hd = items[n][1]
                        L.tell(TS(stat[:, n:n + 1], stat[:, 64 + n:65 + n], -at.scale,
                                  rows[:, ROWS["sink"] + at_layer(at) * 8 + hd:ROWS["sink"] + at_layer(at) * 8 + hd + 1],
                                  ALU.mult, ALU.min), "att_m")
                        if hd == 7:
                            a = n - 7
                            L.tell(TTN(stat[:, 32 + a:40 + a], stat[:, a:a + 8],
                                       rows[:, ROWS["sink"] + at_layer(at) * 8:ROWS["sink"] + at_layer(at) * 8 + 8],
                                       ALU.subtract), "att_sink")
                    else:
                        L.tell(TS(stat[:, n:n + 1], stat[:, 64 + n:65 + n], -at.scale, None, ALU.mult), "att_m")

                def output(n):
                    t = items[n][0]
                    a = n - 7
                    u = look(dve, at.tag, "o", t)
                    L.wait("att_p", ITEMS[at.tag] + n + 1)
                    if sink:
                        L.wait("att_esink", SINKS[at.tag] + n // 8 + 1)
                        S(TTN(stat[:, 16 + a:24 + a], stat[:, 16 + a:24 + a], stat[:, 32 + a:40 + a], ALU.add))
                    S(dve.reciprocal(stat[:, 48 + a:56 + a], stat[:, 16 + a:24 + a]))
                    free(L, TTN(out_of(t).rearrange("p (a b) -> p a b", a=8),
                                ps[:, u.bank, :].rearrange("p (a b) -> p a b", a=8),
                                bc(stat[:, 48 + a:56 + a], 2, [P, 8, 64]), ALU.mult), u)

                score_max(0)
                score_max(1)
                for n in range(len(items)):
                    if n + 2 < len(items):
                        score_max(n + 2)
                    u = look(dve, at.tag, "pT", n)
                    if n >= at.nbuf:
                        pv_done(dve, at, n - at.nbuf)
                    free(L, copy(att_pT[at.tag][:, n % at.nbuf, 0:at.keys], ps[:, u.bank, 0:at.keys]), u, "att_pT")
                    if n and items[n - 1][1] == 7:
                        output(n - 1)
                output(len(items) - 1)

            def at_layer(at):
                return int(at.tag[-1])

            def mixT(tag, tiles, gain):
                for t in tiles:
                    for g in range(2):
                        u = look(dve, tag, "mixT", t, g)
                        for j in range(4):
                            f = 4 * g + j
                            dst, src = h[:, t // 2, f, (t % 2) * P:(t % 2 + 1) * P], ps[:, u.bank, j * P:(j + 1) * P]
                            ins = copy(dst, src) if gain(f) is None else TS(dst, src, gain(f), None, ALU.mult)
                            if j < 3:
                                S(ins)
                            else:
                                free(L, ins, u, "mixT_ready")

            L.wait("const_loaded", 48)
            neg_sink = rows[:, ROWS["sink"]:ROWS["sink"] + 16]
            S(TS(neg_sink, neg_sink, -1.0, None, ALU.mult))
            bg = cols[:, COLS["b_gates"]:COLS["b_gates"] + 8]
            S(TS(bg, bg, 1.0 / CAP, None, ALU.mult))
            L.wait("theta_ready", 1)
            u16, ln16 = stat[:, 80:96], temp[:, 256:272]
            ser, small = temp[:, 272:288], temp[:, 288:304]
            S(TS(ser, u16, 1.0 / 7, 1.0 / 6, ALU.mult, ALU.add))
            for n in (5, 4, 3, 2, 1):
                S(TTN(ser, ser, u16, ALU.mult))
                S(TS(ser, ser, 1.0 / n, None, ALU.add))
            S(STT(out=ser, in0=ser, scalar=-1.0, in1=u16, op0=ALU.mult, op1=ALU.mult))
            S(TS(small, u16, 1.0 / 16, None, ALU.is_lt))
            S(TTN(ser, ser, ln16, ALU.subtract))
            S(TTN(ser, ser, small, ALU.mult))
            S(TTN(u16, ser, ln16, ALU.add))
            L.wait("pos_loaded", 16)
            S(copy(posf, posi))
            inv = cst[:, CST["inv"]:CST["inv"] + 48]
            for t in range(TT):
                S(TS(ang[:, t, :], inv, posf[:, t:t + 1], None, ALU.mult))
            TWO_PI = 2 * np.pi
            c1 = 6.28125
            c2 = float(np.float32(TWO_PI - c1).view(np.int32) & np.int32(-4096)) if False else 0.0019350051879882812
            c3 = float(TWO_PI - c1 - c2)
            magic = 1.5 * 2.0 ** 23
            S(TS(angn, ang, float(1 / TWO_PI), None, ALU.mult))
            S(TS(angn, angn, magic, None, ALU.add))
            S(TS(angn, angn, -magic, None, ALU.add))
            for cc in (c1, c2, c3):
                S(STT(out=ang, in0=angn, scalar=-cc, in1=ang, op0=ALU.mult, op1=ALU.add))
            L.tell(TS(ang, ang, 3.141592, -3.141592, ALU.min, ALU.max), "angle_ready")
            L.wait("sin_ready", 1)
            S(TTN(cos, cos, cos, ALU.mult))
            S(TS(cos, cos, -2.0, 1.0, ALU.mult, ALU.add))

            norm(1, lambda hf, k: col("mix_even", k))
            evacuate(L, copy, "even_in", 0, EVEN["end"], range(TT), 1, lambda t, a, b: pe_[:, t, a:b], "proj_dve")
            L.wait("mla_c_rstd", 1)
            for t in range(TT):
                for i, (a, n) in enumerate(((0, CQ), (CQ, CKV))):
                    v = pe_[:, t, a:a + n]
                    ins = TS(v, v, stat[:, 2 * i + t:2 * i + t + 1], None, ALU.mult)
                    if i == 0:
                        S(ins)
                    else:
                        L.tell(ins, "mla_c")
            for t in range(TT):
                for g, (a, n) in enumerate(((0, 3), (3, 2))):
                    u = look(dve, "mla_cT", t, g)
                    for j in range(n):
                        gain = col("q_norm", j) if g == 0 else col("kv_norm", j)
                        ins = TS(cT[:, a + j, t * P:(t + 1) * P], ps[:, u.bank, j * P:(j + 1) * P], gain, None, ALU.mult)
                        if j < n - 1:
                            S(ins)
                        else:
                            free(L, ins, u)
                dve.sem_inc(sig("mla_cT"), 1)
            L.wait("mla_qkv", 1)
            for t in range(TT):
                S(copy(kx[:, t, :, 0:MNOPE], kv[:, t, :, 0:MNOPE]))
                S(copy(kx[:, t, :, MNOPE:], bc(pe_[:, t, EVEN["kr"]:EVEN["kr"] + MROPE], 1, [P, MH, MROPE])))
            sq = area(spare, 0, TT * MH, MQK)
            both = [v.rearrange("p t h d -> p (t h) d") for v in (qh, kx)]
            for i, v in enumerate(both):
                S(TTN(sq, v, v, ALU.mult))
                ins = dve.tensor_reduce(stat[:, 16 * i:16 * i + 16], sq, AX.X, ALU.add)
                S(ins)
            dve.sem_inc(sig("mla_sumsq"), 1)
            L.wait("mla_rstd", 1)
            t1, t2 = (area(spare, 1536 + 256 * i, TT, MH, 16) for i in range(2))
            for i, (v, v4, g) in enumerate(((both[0], qh, "qh"), (both[1], kx, "kh"))):
                S(TTN(v, v, bc(stat[:, 16 * i:16 * i + 16], 2, [P, 16, MQK]), ALU.mult))
                S(TTN(v, v, bc(rows[:, ROWS[g]:ROWS[g] + MQK], 1, [P, 16, MQK]), ALU.mult))
                for t in range(TT):
                    x1, x2 = v4[:, t, :, MNOPE:MNOPE + 16], v4[:, t, :, MNOPE + 16:]
                    c, s = (bc(w[:, t, 0:16], 1, [P, MH, 16]) for w in (cos, sin))
                    rope(x1, x2, x1, x2, c, s, t1[:, t], t2[:, t])
                dve.sem_inc(sig("mla_heads"), 1)
            for t in range(TT):
                for g in range(2):
                    u = look(dve, "mla", "kT", t, g)
                    free(L, copy(kT[0:MQK, 4 * g:4 * g + 4, t * P:(t + 1) * P],
                                 ps[0:MQK, u.bank, :].rearrange("p (a b) -> p a b", a=4)), u, "mla_kT")
            attend(ATT["mla"], lambda t: mix0[:, t, 0:512])
            c, s = (w[:, :, 16:48] for w in (cos, sin))
            t1, t2 = (area(spare, 1024 * i, TT, 16, 32) for i in range(2))
            for t in range(TT):
                x = pe_[:, t, EVEN["rq"]:EVEN["rv"]].rearrange("p (h d) -> p h d", d=RD)
                y = rqk[:, t, :, :, :].rearrange("p a h d -> p (a h) d")
                rope(x[:, :, 0:32], x[:, :, 32:64], y[:, :, 0:32], y[:, :, 32:64],
                     bc(c[:, t, :], 1, [P, 16, 32]), bc(s[:, t, :], 1, [P, 16, 32]), t1[:, t], t2[:, t])
            dve.sem_inc(sig("ret_rope"), 1)
            L.wait("rel_loaded", 16)

            def exponent(x):
                S(TS(decay[:, x % 2, :, :], relp, u16[:, x:x + 1], None, ALU.mult))
                L.tell(STT(out=decay[:, x % 2, :, :], in0=relm, scalar=u16[:, 8 + x:9 + x],
                           in1=decay[:, x % 2, :, :], op0=ALU.mult, op1=ALU.add), "ret_e")

            exponent(0)
            for x in range(RH):
                if x + 1 < RH:
                    exponent(x + 1)
                u = look(dve, "ret_s", x)
                L.wait("ret_d", x + 1)
                if x >= 2:
                    L.wait("ret_pv", x - 1)
                free(L, STT(out=sdec[:, x % 2, :, :].rearrange("p a b -> p (a b)"), in0=ps[:, u.bank, :],
                            scalar=RD ** -0.5, in1=decay[:, x % 2, :, :].rearrange("p a b -> p (a b)"),
                            op0=ALU.mult, op1=ALU.mult), u, "ret_sdec")
            for t in range(TT):
                u = look(dve, "ret_o", t)
                free(L, copy(mix0[:, t, 512:1024], ps[:, u.bank, :]), u)
                S(TTN(temp[:, 512:1024], mix0[:, t, 512:1024], mix0[:, t, 512:1024], ALU.mult))
                S(dve.tensor_reduce(stat[:, 8 * t:8 * t + 8], temp[:, 512:1024].rearrange("p (a b) -> p a b", a=8),
                                    AX.X, ALU.add))
            dve.sem_inc(sig("ret_sumsq"), 1)
            L.wait("ret_rstd", 1)
            L.wait("rg_ready", 1)
            for t in range(TT):
                v = mix0[:, t, 512:1024]
                v3 = v.rearrange("p (a b) -> p a b", a=8)
                S(TTN(v3, v3, bc(stat[:, 8 * t:8 * t + 8], 2, [P, 8, 64]), ALU.mult))
                L.tell(TTN(v, v, pe_[:, t, EVEN["rg"]:EVEN["end"]], ALU.mult), "mix_ready")
            mixT("even", range(TT), lambda f: col("ret_g", f - 4) if f >= 4 else None)

            def add_out(tag):
                for m in range(KD):
                    u = look(dve, tag, m)
                    free(L, TTN(res[:, 0, m, :], ps[:, u.bank, 0:T], res[:, 0, m, :], ALU.add), u)
                dve.sem_inc(sig("residual"), 1)

            add_out("even_out")

            def ffn1(l):
                norm(1, lambda hf, k: col("ffn", 8 * l + k))

                def product(m):
                    u = uses[f"ffn{l}", "up", m]
                    L.wait("silu1", KF * l + m + 1)
                    L.tell(TTN(g1[:, 0, m, :], ps[:, u.bank, T:2 * T], fsil[:, m % 2, 0:T], ALU.mult), "hidden_ready")
                    dve.sem_inc(bank_free[u.bank], 1)

                for m in range(KF):
                    u = look(dve, f"ffn{l}", "up", m)
                    x, y = ps[:, u.bank, 0:T], fconv[:, m % 2, 0:T]
                    w = [col("conv_w", (3 * l + i) * KF + m) for i in range(3)]
                    S(TS(y, x, w[1], col("conv_b", KF * l + m), ALU.mult, ALU.add))
                    S(STT(out=y[:, 1:T], in0=x[:, 0:T - 1], scalar=w[0], in1=y[:, 1:T], op0=ALU.mult, op1=ALU.add))
                    L.tell(STT(out=y[:, 0:T - 1], in0=x[:, 1:T], scalar=w[2], in1=y[:, 0:T - 1],
                               op0=ALU.mult, op1=ALU.add), "conv1")
                    if m:
                        product(m - 1)
                product(KF - 1)
                for q in range(4):
                    u = look(dve, f"ffn{l}", "down", 0, q)
                    v = res[:, 0, 2 * q:2 * q + 2, :].rearrange("p a b -> p (a b)")
                    free(L, TTN(v, ps[:, u.bank, :], v, ALU.add), u)
                dve.sem_inc(sig("residual"), 1)

            ffn1(0)

            norm(1, lambda hf, k: col("mix_odd", k))
            S(dve.memset(gA, 0.0))
            evacuate(L, copy, "odd_in", 0, ODD["end"], range(TT), 1, lambda t, a, b: po[:, t, a:b], "proj_dve")
            for t in range(TT):
                u = look(dve, "gla_gT", t)
                free(L, copy(gaT[0:GR, :, t * P:(t + 1) * P],
                             ps[0:GR, u.bank, 0:T].rearrange("p (a b) -> p a b", a=2)), u, "gla_gT")
            for i in range(4):
                u = look(dve, "gla_la", i // 2, i % 2)
                L.wait("gla_soft", i + 1)
                v = la[:, i // 2, i % 2, :]
                free(L, STT(out=v, in0=ps[:, u.bank, :], scalar=0.0, in1=temp[:, 512 * (i % 2):512 * (i % 2) + 512],
                            op0=ALU.min, op1=ALU.subtract), u)
                L.tell(TS(v, v, 1.0 / TAU, None, ALU.mult), "gla_la")
            for i in range(4):
                L.wait("gla_kd", i + 1)
                L.wait("proj_act", PROJ["odd_in"])
                L.tell(TTN(kdT[:, i // 2, i % 2, :], temp[:, 512 * (i % 2):512 * (i % 2) + 512],
                           po[:, i % 2, ODD["k"]:ODD["k"] + 512], ALU.mult), "gla_kdT")
            L.wait("gla_T", 4)
            L.wait("gla_const", 80)
            qs = GK ** -0.5
            for x in range(GH):
                for d in range(2):
                    n = 2 * x + d
                    L.wait("gla_ex", n + 1)
                    q, k = gqk[:, x, :], gqk[:, 4 + x, :]
                    S(STT(out=gqkx[:, d, 0, :], in0=q, scalar=qs, in1=gex[:, 1, :], op0=ALU.mult, op1=ALU.mult))
                    S(TTN(gqkx[:, d, 1, :], k, gex[:, 2, :], ALU.mult))
                    L.tell(STT(out=gqkx[:, d, 2, :], in0=q, scalar=qs, in1=gex[:, 0, :], op0=ALU.mult, op1=ALU.mult),
                           "gla_qk")
                    for i in range(3):
                        u = look(dve, "gla_st", n, i)
                        if i == 0:
                            free(L, copy(gst[:, d, 0, :], ps[:, u.bank, 0:GV]), u)
                            continue
                        c = i if d == 0 else 3 - i
                        last = c * GC + GC - 1 if d == 0 else c * GC
                        free(L, STT(out=gst[:, d, i, :], in0=gst[:, d, i - 1, :], scalar=gex[:, 0, last:last + 1],
                                    in1=ps[:, u.bank, 0:GV], op0=ALU.mult, op1=ALU.add), u)
                    dve.sem_inc(sig("gla_states"), 1)
                    u = look(dve, "gla_A", n)
                    for t in range(TT):
                        ins = dve.copy_predicated(gA[:, d, t, :], glamask[:, d, :].bitcast(I32),
                                                  ps[:, u.bank, t * P:(t + 1) * P])
                        if t == 0:
                            S(ins)
                        else:
                            free(L, ins, u, "gla_Am")
                u = look(dve, "gla_o", x)
                free(L, copy(po[:, :, x * GV:(x + 1) * GV], ps[:, u.bank, :].rearrange("p (a b) -> p a b", a=2)), u)
            for t in range(TT):
                v = po[:, t, 0:1024]
                S(TTN(temp[:, :], v, v, ALU.mult))
                S(dve.tensor_reduce(stat[:, 4 * t:4 * t + 4], temp[:, :].rearrange("p (a b) -> p a b", a=4), AX.X, ALU.add))
            dve.sem_inc(sig("gla_sumsq"), 1)
            L.wait("gla_rstd", 1)
            L.wait("gr_ready", 1)
            for t in range(TT):
                v = po[:, t, 0:1024]
                v3 = v.rearrange("p (a b) -> p a b", a=4)
                S(TTN(v3, v3, bc(stat[:, 4 * t:4 * t + 4], 2, [P, 4, GV]), ALU.mult))
                L.tell(TTN(v, v, po[:, t, ODD["r"]:ODD["r"] + 1024], ALU.mult), "mix_ready")
            mixT("odd", range(TT), lambda f: col("gla_g", f))
            add_out("odd_out")
            ffn1(1)

            L.wait("mod_done", 1)
            bm = cols[:, COLS["b_mod"]:COLS["b_mod"] + 96]
            m = mods[:, :, :, :].rearrange("p l c x -> p (l c) x")
            S(TTN(m, m, bc(bm, 2, [P, 96, 2]), ALU.add))
            for l in range(2):
                for j, name in ((1, "norm1"), (4, "norm2")):
                    g = cols[:, COLS[name] + 8 * l:COLS[name] + 8 * l + 8]
                    m = mods[:, l, 8 * j:8 * j + 8, :]
                    S(STT(out=m, in0=m, scalar=1.0, in1=bc(g, 2, [P, 8, 2]), op0=ALU.add, op1=ALU.mult))

            def gated(l, j, hf, m):
                return mods[:, l, 8 * j + m, hf:hf + 1]

            for l in range(2):
                norm(2, lambda hf, k: gated(l, 1, hf, k), lambda hf, k: gated(l, 0, hf, k))
                L.tell(dve.memset(vaug[:, :, :, LV:LV + 1], 1.0), "vaug_ones")
                before, after = in_stages(l)
                for tag, a, b, tiles, dst in before:
                    evacuate(L, copy, tag, a, b, tiles, 1, dst, "proj_dve")
                for c in range(4):
                    u = look(dve, "conv", l, c)
                    x = ps[:, u.bank, :].rearrange("p (a b) -> p a b", a=2)
                    y = conv[:, c, :].rearrange("p (a b) -> p a b", a=2)
                    w = [col("conv_w2", 20 * l + 4 * i + c) for i in range(5)]
                    if l == 1 and c < 2:
                        x, y = x[:, 0:1, :], y[:, 0:1, :]
                    S(TS(y, x, w[2], col("conv_b2", 4 * l + c), ALU.mult, ALU.add))
                    for i, o in ((0, -2), (1, -1), (3, 1), (4, 2)):
                        a, b = max(0, -o), T - max(0, o)
                        ins = STT(out=y[:, :, a:b], in0=x[:, :, a + o:b + o], scalar=w[i], in1=y[:, :, a:b],
                                  op0=ALU.mult, op1=ALU.add)
                        if i < 4:
                            S(ins)
                        else:
                            free(L, ins, u, "conv2")
                for tag, a, b, tiles, dst in after:
                    evacuate(L, copy, tag, a, b, tiles, 1, dst, "proj_dve")
                u = look(dve, "gT", l)
                free(L, copy(gT, ps[:, u.bank, 0:64].rearrange("p (a b) -> p a b", a=4)), u, "gT")
                L.wait("proj_act", PROJ[f"kv{l}"])
                look(dve, "gates", l, 3)
                ax = cst[:, CST["axial"]:CST["axial"] + 128].rearrange("p (t w a c) -> p t w a c", t=2, w=2, a=2)
                for t in range(TT):
                    t1, t2 = (area(temp, 256 * i, 8, 2, 16) for i in range(2))
                    for src, dst, n in ((p2[:, t, 0:512].rearrange("p (h a w c) -> p h a w c", a=2, w=2, c=16),
                                         ro[:, t, :].rearrange("p (h a w c) -> p h a w c", a=2, w=2, c=16), 8),
                                        (p2[:, t, 512:640].rearrange("p (h a w c) -> p h a w c", a=2, w=2, c=16),
                                         kdup[:, t, :, 0, :].rearrange("p h (a w c) -> p h a w c", a=2, w=2), 2)):
                        cs = [bc(ax[:, t, w, :, :], 1, [P, n, 2, 16]) for w in range(2)]
                        rope(src[:, :, :, 0, :], src[:, :, :, 1, :], dst[:, :, :, 0, :], dst[:, :, :, 1, :],
                             cs[0], cs[1], t1[:, 0:n], t2[:, 0:n])
                    S(copy(kdup[:, t, :, 1, :], kdup[:, t, :, 0, :]))
                for t in (2, 3):
                    for i in range(2):
                        S(copy(kdup[:, t, :, i, :], p2[:, t, 512:640].rearrange("p (a b) -> p a b", a=2)))
                for _ in range(2):
                    dve.sem_inc(sig("att_rope"), 1)
                for t in (range(4) if l == 0 else range(TT)):
                    u = look(dve, "aqT", l, t)
                    free(L, copy(aqT[:, :, t * P:(t + 1) * P], ps[:, u.bank, :].rearrange("p (a b) -> p a b", a=4)),
                         u, "aqT")
                attend(ATT[f"wx{l}"], lambda t: mix2[:, t, 0:512])
                if l == 0:
                    attend(ATT["wc0"], lambda t: mix2[:, t, 0:512])
                dve.sem_inc(sig("att_done"), 1)
                L.wait("gates_ready", l + 1)
                one = cst[0:4, CST["ones"]:CST["ones"] + 1].broadcast_to([4, T])

                def scan(dst, src, op):
                    for d in range(2):
                        for sq in (1, 0):
                            a, b = sq * T, (sq + 1) * T
                            o, i = dst(d)[:, a:b], src(d)[:, a:b]
                            first = 0.0 if sq else (dst(d)[:, 2 * T - 1:2 * T] if d == 0 else dst(d)[:, T:T + 1])
                            if d == 1:
                                o, i = o[:, T - 1::-1], i[:, T - 1::-1]
                            S(dve.tensor_tensor_scan(o, one, i, first, ALU.mult, op))

                scan(lambda d: brow[0:4, d, :], lambda d: gates[0:4, 2 * d + 1, :], ALU.subtract)
                for d in range(2):
                    S(STT(out=gates[0:4, 2 * d, :], in0=gates[0:4, 2 * d, :], scalar=CAP, in1=brow[0:4, d, :],
                          op0=ALU.mult, op1=ALU.subtract))
                scan(lambda d: mrow[0:4, d, :], lambda d: gates[0:4, 2 * d, :], ALU.max)
                L.tell(TTN(brow[0:4, :, :], brow[0:4, :, :], mrow[0:4, :, :], ALU.add), "lrows")
                u = look(dve, "lcols", l)
                free(L, copy(temp[:, 0:64], ps[:, u.bank, 0:64]), u, "lc_ready")
                L.wait("lem_ready", l + 1)
                L.wait("lmask", 16 * (l + 1))
                lc = temp[:, 0:64].rearrange("p (t w d h) -> p t w d h", t=4, w=2, d=2)
                em = temp[:, 64:128].rearrange("p (t w d h) -> p t w d h", t=4, w=2, d=2)
                steps = lsteps(l)

                def exponents(n):
                    sq, x, d = steps[n]
                    ns = len(STILES[sq])
                    u = look(dve, "lm", l, n)
                    for i in (ns - 2, ns - 1):
                        ins = TS(lw[n % 2][:, i, :], ps[:, u.bank, 0:T], lc[:, STILES[sq][i], 0, d, x:x + 1], 0.0,
                                 ALU.subtract, ALU.max)
                        if i == ns - 2:
                            S(ins)
                        else:
                            L.tell(ins, "lw")

                def weights(n):
                    sq, x, d = steps[n]
                    L.wait("lexp", 16 * l + n + 1)
                    if n >= 2:
                        look(dve, "lo", l, n - 2)
                    for i in range(len(STILES[sq]) // 2):
                        u = look(dve, "ls", l, sq, x, i)
                        dst = lp[n % 2][:, 2 * i:2 * i + 2, :].rearrange("p a b -> p (a b)")
                        w = lw[n % 2][:, 2 * i:2 * i + 2, :].rearrange("p a b -> p (a b)")
                        ins = STT(out=dst, in0=ps[:, u.bank, :], scalar=LK ** -0.5, in1=w, op0=ALU.mult, op1=ALU.mult)
                        if d == 0:
                            S(ins)
                        else:
                            free(L, ins, u)
                    dve.sem_inc(sig("lweights"), 1)

                def heads_out(n):
                    sq, x, d = steps[n]
                    u = look(dve, "lo", l, n)
                    o = ps[:, u.bank, 0:2 * (LV + 1)].rearrange("p (t c) -> p t c", t=2)
                    r = stat[:, 0:2]
                    S(copy(r, o[:, :, LV]))
                    S(STT(out=r, in0=o[:, :, LV], scalar=-1.0, in1=r, op0=ALU.mult, op1=ALU.max))
                    S(TTN(r, r, em[:, 2 * sq:2 * sq + 2, 1, d, x], ALU.max))
                    S(dve.reciprocal(r, r))
                    for t in range(TT):
                        dst = mix2[:, 2 * sq + t, 512 + x * LV:512 + (x + 1) * LV]
                        if d == 0:
                            ins = TS(dst, o[:, t, 0:LV], r[:, t:t + 1], None, ALU.mult)
                        else:
                            ins = STT(out=dst, in0=o[:, t, 0:LV], scalar=r[:, t:t + 1], in1=dst,
                                      op0=ALU.mult, op1=ALU.add)
                        if t == 0:
                            S(ins)
                        else:
                            free(L, ins, u)

                exponents(0)
                for n in range(len(steps)):
                    if n + 1 < len(steps):
                        exponents(n + 1)
                    weights(n)
                    if n:
                        heads_out(n - 1)
                heads_out(len(steps) - 1)
                tiles = range(4) if l == 0 else range(TT)
                S(dve.memset(stat[:, 0:20], 1.0))
                for t in tiles:
                    for half, dst, nh in ((1, stat[:, 4 * t:4 * t + 4], 4), (0, stat[:, 16 + t:17 + t], 1)):
                        v = mix2[:, t, 512 * half:512 * half + 512]
                        S(TTN(temp[:, 512:1024], v, v, ALU.mult))
                        S(dve.tensor_reduce(dst, temp[:, 512:1024].rearrange("p (a b) -> p a b", a=nh), AX.X, ALU.add))
                dve.sem_inc(sig("merge_sumsq"), 1)
                L.wait("merge_rstd", l + 1)
                L.wait("o_ready", l + 1)
                for t in tiles:
                    v = mix2[:, t, 512:1024]
                    v3 = v.rearrange("p (a b) -> p a b", a=4)
                    S(TTN(v3, v3, bc(stat[:, 4 * t:4 * t + 4], 2, [P, 4, LV]), ALU.mult))
                    S(TTN(v, v, p2[:, t, 768:1280], ALU.mult))
                    v = mix2[:, t, 0:512]
                    L.tell(TS(v, v, stat[:, 16 + t:17 + t], None, ALU.mult), "mix_ready")
                mixT(f"mix{l}", tiles, lambda f: col("g_att", 4 * l + f) if f < 4 else col("g_ml", 4 * l + f - 4))
                nh = 2 - l
                for m in range(KD):
                    u = look(dve, f"out{l}", m)
                    for hf in range(nh):
                        v = res[:, hf, m, :]
                        ins = STT(out=v, in0=ps[:, u.bank, hf * T:(hf + 1) * T], scalar=gated(l, 2, hf, m), in1=v,
                                  op0=ALU.mult, op1=ALU.add)
                        if hf < nh - 1:
                            S(ins)
                        else:
                            free(L, ins, u)
                dve.sem_inc(sig("residual"), 1)
                norm(nh, lambda hf, k: gated(l, 4, hf, k), lambda hf, k: gated(l, 3, hf, k))
                if l == 0:
                    for m in range(KF):
                        u = look(dve, "ffn2", "up", m, 1)
                        ug = uses["ffn2", "up", m, 0]
                        dve.wait_ge(bank_free[ug.bank], ug.nth + 1)
                        L.tell(TTN(g2[:, m, :], ps[:, u.bank, :], fsil[:, m % 2, :], ALU.mult), "hidden_ready")
                        dve.sem_inc(bank_free[u.bank], 1)
                    for hf in range(2):
                        for q in range(4):
                            u = look(dve, "ffn2", "down", hf, q)
                            for i in range(2):
                                m = 2 * q + i
                                v = res[:, hf, m, :]
                                ins = STT(out=v, in0=ps[:, u.bank, i * T:(i + 1) * T], scalar=gated(l, 5, hf, m),
                                          in1=v, op0=ALU.mult, op1=ALU.add)
                                if i == 0:
                                    S(ins)
                                else:
                                    free(L, ins, u)
                    dve.sem_inc(sig("residual"), 1)

            L.tell(dve.memset(temp[:, 0:512], 0.0), "zero_ready")
            iota = cst[:, CST["iota8"]:CST["iota8"] + 8]
            lg, eq, oh1, oh2 = (temp[:, 512 + 8 * i:520 + 8 * i] for i in range(4))
            m1, m2, mx, ex, w1 = (temp[:, 596 + i:597 + i] for i in (0, 1, 2, 4, 5))
            for t in range(TT):
                u = look(dve, "router", t)
                free(L, TTN(lg, ps[:, u.bank, 0:NE], rows[:, ROWS["b_router"]:ROWS["b_router"] + NE], ALU.add), u)
                for mval, oh in ((m1, oh1), (m2, oh2)):
                    S(dve.tensor_reduce(mval, lg, AX.X, ALU.max))
                    S(TS(eq, lg, mval, None, ALU.is_ge))
                    S(TTN(eq, eq, iota, ALU.mult))
                    S(dve.tensor_reduce(mx, eq, AX.X, ALU.max))
                    S(TS(oh, eq, mx, None, ALU.is_equal))
                    S(STT(out=lg, in0=oh, scalar=-HUGE, in1=lg, op0=ALU.mult, op1=ALU.add))
                L.tell(TTN(ex, m2, m1, ALU.subtract), "top_ready")
                L.wait("top_exp", t + 1)
                S(TS(w1, ex, 1.0, None, ALU.add))
                S(dve.reciprocal(w1, w1))
                S(TTN(ex, ex, w1, ALU.mult))
                c = stat[:, 16 * t:16 * t + NE]
                S(TS(c, oh1, w1, None, ALU.mult))
                L.tell(STT(out=c, in0=oh2, scalar=ex, in1=c, op0=ALU.mult, op1=ALU.add), "combine")
            u = look(dve, "combT")
            free(L, copy(combT[0:NE, :], ps[0:NE, u.bank, 0:T]), u, "combT")
            for j in range(NE // 2):
                u = look(dve, "comb", j)
                free(L, copy(comb[:, 2 * j:2 * j + 2, :].rearrange("p a b -> p (a b)"), ps[:, u.bank, :]), u)
            with dve.Fori(0, NE // 2) as i:
                for e in range(2):
                    dve.wait_ge(chunk_used, i * KF + (moe["used"] + (e - 1) * (KF // 2)))
                    for m in range(KF):
                        b, k = m % 2, e * KF + m
                        dve.wait_ge(sig("moe_silu"), i * (2 * KF) + (k + 1))
                        TTN(fval[:, b, :], ps[:, b, T:2 * T], comb[:, i * 2 + e, :], ALU.mult).then_inc(sig("moe_val"), 1)
                        dve.wait_ge(sig("moe_val"), i * (2 * KF) + (k + 1))
                        TTN(g1[:, e, m, :], fval[:, b, :], fsil[:, b, 0:T], ALU.mult).then_inc(sig("hidden_ready"), 1)
                        dve.sem_inc(bank_free[b], 1)
            for q in range(4):
                u = look(dve, "moe_acc", q)
                for i in range(2):
                    m = 2 * q + i
                    v = res[:, 0, m, :]
                    ins = STT(out=v, in0=ps[:, u.bank, i * T:(i + 1) * T], scalar=gated(1, 5, 0, m), in1=v,
                              op0=ALU.mult, op1=ALU.add)
                    if i == 0:
                        S(ins)
                    else:
                        free(L, ins, u)
            dve.sem_inc(sig("residual"), 1)
            norm(1, lambda hf, k: col("final", k), name="out_ready")

    return nc


WEIGHTS = ["w_in_even", "mla_w_uq", "mla_w_ukv", "w_out_even", "w_in_odd", "gla_w_gate_fwd", "gla_b_gate_fwd",
           "gla_w_gate_bwd", "gla_b_gate_bwd", "w_out_odd", "ffn_w_up", "ffn_w_down", "w_mod_2", "w_in_2", "w_out_2",
           "ffn_w1_2", "ffn_w3_2", "ffn_w2_2", "w_router_2", "exp_w1_2", "exp_w3_2", "exp_w2_2"]


def kernel(**inputs):
    import numpy as _np
    import concourse.bacc as _bacc
    from concourse import mybir as _mybir
    from concourse.bass_utils import run_bass_kernel_spmd as _run

    I = {k: _np.asarray(v) for k, v in inputs.items()}

    def on_partitions(a):
        return a.reshape(-1, P).T

    cond = _np.stack([I["c_2"].reshape(D), I["c_ctx_2"].reshape(D)], 0).reshape(2, KD, P).transpose(2, 1, 0)
    bg = _np.zeros((P, 8), _np.float32)
    bg[0:4] = I["b_gates_2"].reshape(2, 4, 4).transpose(2, 0, 1).reshape(4, 8)
    parts = [on_partitions(I["mix_norm_even"]), on_partitions(I["mix_norm_odd"]), on_partitions(I["ffn_norm"]),
             on_partitions(I["ffn_conv_w"]), on_partitions(I["ffn_conv_b"]), on_partitions(I["mla_q_norm"]),
             on_partitions(I["mla_kv_norm"]), on_partitions(I["ret_out_norm"]), on_partitions(I["gla_out_norm"]),
             on_partitions(I["norm1_g_2"]), on_partitions(I["norm2_g_2"]), on_partitions(I["b_mod_2"]),
             on_partitions(I["conv_w_2"]), on_partitions(I["conv_b_2"]), on_partitions(I["g_att_2"]),
             on_partitions(I["g_ml_2"]), on_partitions(I["final_g_2"]), cond.reshape(P, 16), bg]
    rows = [I["mla_q_head_norm"], I["mla_k_head_norm"], I["ret_theta_fwd"], I["ret_theta_bwd"], I["attn_sink_2"],
            I["b_router_2"]]
    arrays = {w: _np.ascontiguousarray(I[w]) for w in WEIGHTS}
    arrays["cols"] = _np.ascontiguousarray(_np.concatenate(parts, 1))
    arrays["rows"] = _np.concatenate([r.reshape(-1) for r in rows])
    arrays["pos"] = _np.ascontiguousarray(I["positions"].reshape(TT, P).T)
    arrays["xT"] = _np.ascontiguousarray(I["x"].reshape(T, KD, P).transpose(2, 1, 0))
    arrays["ctxT"] = _np.ascontiguousarray(I["ctx_2"].reshape(T, KD, P).transpose(2, 1, 0))
    arrays["consts"] = constants()

    nc = _bacc.Bacc("TRN2", target_bir_lowering=False, num_devices=1)
    A, feed = {}, {}
    for name, a in arrays.items():
        feed[f"in_{name}"] = a
        A[name] = nc.dram_tensor(f"in_{name}", a.shape, _mybir.dt.from_np(a.dtype), kind="ExternalInput").ap()
    out = nc.dram_tensor("out_xT", (P, KD, T), F32, kind="ExternalOutput").ap()
    build(nc, A, out)
    r = _run(nc, [feed], core_ids=[0])
    y = r.results[0]["out_xT"]
    return y.transpose(2, 1, 0).reshape(1, T, D)
```

```python
from collections import namedtuple
from contextlib import ExitStack

import numpy as np

import concourse.bass as bass
from concourse import mybir
from concourse.alu_op_type import AluOpType as ALU

ACT = mybir.ActivationFunctionType
AX = mybir.AxisListType
F32 = mybir.dt.float32
I32 = mybir.dt.int32
F32R = mybir.dt.float32r

P = 128
T = 256
TT = T // P
D = 1024
KD = D // P
F = 2816
KF = F // P
EPS = 1e-6
HUGE = 1e30

MH, MQK, MNOPE, MROPE, MV = 8, 96, 64, 32, 64
CQ, CKV = 384, 256
EVEN = dict(cq=0, ckv=384, kr=640, rq=672, rk=1184, rv=1696, rg=2208, end=2720)
ODD = dict(q=0, k=512, v=1024, r=2048, gf=3072, gb=3088, end=3104)
RH, RD = 8, 64
GH, GK, GV, GC, GR, TAU = 4, 128, 256, 64, 16, 16.0
AH, AG, AD = 8, 2, 64
LH, LK, LV = 4, 64, 128
CAP = 15.0
NE = 8
IN2 = dict(q=0, k=512, v=640, conv=768, mv=1280, o=1792, g=2304)

SLOTS = 6
HIS = 3
SLOT = 2048
CPE = KF + KF // 2

COLS = {}
NCOLS = 0
for _name, _n in (("mix_even", 8), ("mix_odd", 8), ("ffn", 16), ("conv_w", 132), ("conv_b", 44), ("q_norm", 3),
                  ("kv_norm", 2), ("ret_g", 4), ("gla_g", 8), ("norm1", 16), ("norm2", 16), ("b_mod", 96),
                  ("conv_w2", 40), ("conv_b2", 8), ("g_att", 8), ("g_ml", 8), ("final", 8), ("cond", 16),
                  ("b_gates", 8)):
    COLS[_name] = NCOLS
    NCOLS += _n
ROWS = {}
NROWS = 0
for _name, _n in (("qh", 96), ("kh", 96), ("theta", 16), ("sink", 16), ("b_router", 8)):
    ROWS[_name] = NROWS
    NROWS += _n
CST = {}
NCST = 0
for _name, _n in (("ident", 128), ("ones", 128), ("sel4", 512), ("axial", 128), ("inv", 48), ("iota8", 8), ("eps", 1),
                  ("relp", 512), ("relm", 512), ("gla_m", 768), ("gla_mask", 256), ("wmask", 512),
                  ("lmask", 1024), ("sel8", 1024), ("before", 128), ("slots", 128), ("slot", 2)):
    CST[_name] = NCST
    NCST += _n
NKEEP = CST["relp"]

Use = namedtuple("Use", "bank nth")
PROJ = {"even_in": 1, "odd_in": 2, "q0": 3, "kv0": 4, "mv0": 5, "o0": 6, "q1": 7, "kv1": 8, "mv1": 9, "o1": 10}
ITEMS = {"mla": 0, "wx0": 16, "wc0": 32, "wx1": 48}
SINKS = {"wx0": 0, "wc0": 2, "wx1": 4}
MOD_PIECES = 48
FILL = {"start": 3, "latents": 2, "heads": 7, "attention": 16, "ret_rope": 3, "even_mix": 2, "ffn0": 1, "odd": 1,
        "gla_gates": 2, "gla": 8, "odd_mix": 2, "ffn1": 1}
assert sum(FILL.values()) == MOD_PIECES
MIXED = {"even": 0, "odd": 2, "mix0": 4, "mix1": 8}


def constants():
    c = np.zeros((P, NCST), np.float32)
    p = np.arange(P)

    def put(name, a):
        a = np.asarray(a, np.float32)
        a = a.reshape(a.shape[0], -1)
        c[:a.shape[0], CST[name]:CST[name] + a.shape[1]] = a

    put("ident", np.eye(P))
    put("ones", np.ones((P, P)))
    put("sel4", np.repeat(np.eye(4), P, axis=1))
    put("sel8", np.repeat(np.eye(8), P, axis=1))
    put("before", p[:, None] < p[None, :])
    put("slots", np.broadcast_to(p, (P, P)))
    put("slot", np.stack([p, p + P], 1))
    put("iota8", np.broadcast_to(8.0 - np.arange(8), (P, 8)))
    put("eps", np.full((P, 1), EPS))
    inv16 = np.float32(10000.0) ** (-np.arange(16, dtype=np.float32) / np.float32(16))
    inv32 = np.float32(10000.0) ** (-np.arange(32, dtype=np.float32) / np.float32(32))
    put("inv", np.broadcast_to(np.concatenate([inv16, inv32]), (P, 48)))
    tok = np.arange(T)
    ang = np.stack([(tok // 64).astype(np.float32)[:, None] * inv16, (tok % 64).astype(np.float32)[:, None] * inv16], 1)
    axial = np.stack([np.cos(ang), np.sin(ang)], 1)
    put("axial", axial.reshape(TT, P, 64).transpose(1, 0, 2))
    i = np.arange(T)[None, None, :]
    j = (np.arange(TT)[None, :] * P + p[:, None])[:, :, None]
    put("relp", np.maximum(i - j, 0))
    put("relm", np.maximum(j - i, 0))
    s, t = p[:, None], p[None, :]
    same = (s // GC) == (t // GC)
    cf, cb = (same & (s <= t)).astype(np.float32), (same & (s >= t)).astype(np.float32)
    tot = same.astype(np.float32)
    midf, midb = (t // GC) * GC + GC // 2, (t // GC) * GC + GC // 2 - 1
    mats = [cf, cf - cf[s, midf], tot - cf, cb, cb - cb[s, midb], tot - cb]
    put("gla_m", np.concatenate(mats, 1))
    put("gla_mask", np.concatenate([same & (s <= t), same & (s > t)], 1))
    q = np.arange(T).reshape(TT, P).T[:, :, None]
    k = np.arange(T)[None, None, :]
    put("wmask", np.where(np.abs(q - k) <= 128, 0.0, -HUGE))
    put("lmask", np.stack([j <= i, j >= i], 1))
    return c


class Lane:

    def __init__(self, engine, sig, name):
        self.engine, self.sig, self.order, self.steps, self.told = engine, sig, sig(name), 0, {}

    def step(self, ins):
        ins.then_inc(self.order, 1)
        self.steps += 1
        self.engine.wait_ge(self.order, self.steps)

    def tell(self, ins, name):
        ins.then_inc(self.sig(name), 1)
        self.told[name] = self.told.get(name, 0) + 1
        self.engine.wait_ge(self.sig(name), self.told[name])

    def wait(self, name, n):
        self.engine.wait_ge(self.sig(name), n)


def build(nc, A, out):
    ctx = ExitStack()
    with ctx:
        def sb(name, shape, dt=F32):
            return ctx.enter_context(nc.sbuf_tensor(name, shape, dt))

        sems = {}

        def sig(name):
            if name not in sems:
                sems[name] = ctx.enter_context(nc.semaphore(name))
            return sems[name]

        def sb_twice(name, shape):
            at = -(-nc.sbuf_base // 32) * 32
            return sb(name, shape), nc.alloc_sbuf_tensor_at(name + "_r", shape, F32R, offset=at)

        ring, ring_lo = sb_twice("ring", [P, SLOTS, SLOT])
        ring_hi = sb("ring_hi", [P, HIS, SLOT], F32R)
        res = sb("res", [P, 2, KD, T])
        h, h_lo = sb_twice("h", [P, 2, KD, T])
        extra = sb("extra", [P, 2 * KD * T], F32R)
        areaA, areaA_r = sb_twice("areaA", [P, 11280])
        areaB, areaB_r = sb_twice("areaB", [P, 8192])
        temp = sb("temp", [P, 1024])
        cst = sb("cst", [P, NKEEP])
        cols = sb("cols", [P, NCOLS])
        rows = sb("rows", [P, NROWS])
        mods = sb("mods", [P, 2, 48, 2])
        stat = sb("stat", [P, 96])
        passes = sb("passes", [P, 2], I32)
        ps = ctx.enter_context(nc.psum_tensor("ps", [P, 8, 512], F32))

        def keep(name, n):
            return cst[:, CST[name]:CST[name] + n]

        def col(name, i):
            return cols[:, COLS[name] + i:COLS[name] + i + 1]

        ident, ones = keep("ident", P), keep("ones", P)
        eps = keep("eps", 1)
        hflat = h[:, :, :, :].rearrange("p a k t -> p (a k t)")
        spare = h[:, 1, :, :].rearrange("p k t -> p (k t)")

        def area(t, at, *dims):
            n = int(np.prod(dims))
            names = "abcdef"[:len(dims)]
            v = t[:, at:at + n]
            if len(dims) > 1:
                v = v.rearrange(f"p ({' '.join(names)}) -> p {' '.join(names)}", **dict(zip(names, dims)))
            return v

        pe_ = area(areaA, 0, TT, EVEN["end"])
        qh = area(areaA, 5440, TT, MH, MQK)
        kv = area(areaA, 6976, TT, MH, 128)
        kx = area(areaA, 9024, TT, MH, MQK)
        qT = area(areaB, 0, MH, T)
        kT = area(areaB, 2048, MH, T)
        mix0 = area(areaB, 4096, TT, D)
        cT = area(areaB, 6144, 5, T)
        relp, relm = area(areaA, 5440, TT, T), area(areaA, 5952, TT, T)
        rqk = area(areaA, 6976, TT, 2, RH, RD)
        rT = area(areaB, 0, 8, T)
        decay = area(areaB, 2048, 2, TT, T)
        sdec = area(areaB, 3072, 2, TT, T)
        ang = area(temp, 0, TT, 48)
        angn = area(temp, 96, TT, 48)
        sin = area(areaA, 11088, TT, 48)
        cos = area(areaA, 11184, TT, 48)
        posi = temp[:, 192:194].bitcast(I32)
        posf = temp[:, 194:196]
        po = area(areaA, 0, TT, ODD["end"])
        gqk = area(areaA, 6208, 8, T)
        la = area(areaA, 8256, 2, TT, 512)
        gaT = area(areaA, 10304, 2, T)
        kdT = area(areaB, 0, 2, TT, 512)
        glam = area(areaB, 2048, 6, P)
        glamask = area(areaB, 2816, 2, P)
        wg = area(areaB, 3072, 2, 512)
        gex = area(areaB, 4096, 3, T)
        gqkx = area(areaB, 4864, 2, 3, T)
        gst = area(areaB, 6400, 2, 3, GV)
        gA = area(spare, 0, 2, 2, P)
        gbias = area(spare, 512, 2, 512)
        p2 = area(areaA, 0, 4, 1280)
        vaug = area(areaA, 5120, 4, LH, LV + 1)
        mix2 = area(areaA, 7184, 4, D)
        conv = area(areaB, 0, 4, 2 * T)
        aqT = area(areaB, 2048, 4, 2 * T)
        akT = area(areaB, 4096, 2, 2 * T)
        wmask = area(areaB, 5120, TT, T)
        lmask = area(areaB, 2048, 2, TT, T)
        gates = area(areaB, 6144, 4, 2 * T)
        ro = area(hflat, 0, TT, 512)
        kdup = area(hflat, 1024, 4, AG, 2, AD)
        brow = area(hflat, 0, 2, 2 * T)
        mrow = area(hflat, 1024, 2, 2 * T)
        lw = [area(hflat, 2048, 4, T), area(areaB, 3072, 4, T)]
        lp = [area(hflat, 3072, 4, T), area(areaB, 4096, 4, T)]
        h_hi = area(extra, 0, 2, KD, T)
        g1 = [area(areaA_r, i * KF * T, KF, T) for i in range(2)]
        g2 = area(areaA, 0, KF, 2 * T)
        g2r = [area(areaB_r, 2048 + 4096 * i, 4, 2 * T) for i in range(2)]
        fconv = area(areaB, 0, 2, 512)
        fsil = area(areaB, 1024, 2, 512)
        fval = area(areaB, 6144, 2, T)
        hid = [area(areaA_r, 0, KF, P), area(areaB_r, 5376, KF, P)]
        pick = area(areaA, 2816, 2 * NE + 1, TT, P)
        htok = area(areaA, 7168, TT, D)
        yexp = area(areaA, 9216, D)
        wrow = area(areaA, 10240, 4, T)
        put_back = area(areaB, 0, 2 * NE + 1, T)
        moe_const = area(areaB, 4352, NE * P + 2 * P + 2)
        sel8, before, slots, slot = (moe_const[:, a:b] for a, b in ((0, NE * P), (NE * P, NE * P + P),
                                                                    (NE * P + P, NE * P + 2 * P),
                                                                    (NE * P + 2 * P, NE * P + 2 * P + 2)))
        rw8 = area(areaB, 5640, 2 * T)
        xexp = [area(extra, 2048 * i, 2, KD, P) for i in range(2)]
        msil = area(temp, 512, 2, P)
        mprod = area(temp, 768, 2, P)
        mturn = area(areaA, 10240, 2, P)
        combine, taken, rank = (stat[:, 16 * i:16 * i + 16].rearrange("p (t e) -> p t e", t=TT) for i in range(3))
        modrow = area(res[:, 1, :, :].rearrange("p k t -> p (k t)"), 0, 2, 256)
        gT = area(temp, 960, 4, 16)

        bank_full = [sig(f"bank{b}_full") for b in range(8)]
        bank_free = [sig(f"bank{b}_free") for b in range(8)]
        slot_full = [sig(f"slot{s}_full") for s in range(SLOTS)]
        chunk_used = sig("chunk_used")

        uses, bank_uses, turn = {}, [0] * 8, [0, 6]
        chunks = []
        slot_loads = [0] * SLOTS
        splits = []
        used = [0]
        moe, ffn2_down = {}, []

        block = ctx.enter_context(nc.Block())

        STILES = {0: [2, 3, 0, 1], 1: [2, 3]}

        def lsteps(l):
            return [(sq, x, d) for sq in range(2 - l) for x in range(LH) for d in range(2)]

        Att = namedtuple("Att", "tag items keys nbuf scale dk")

        ATT = {"mla": Att("mla", [(t, x) for t in range(TT) for x in range(MH)], T, 3, MQK ** -0.5, MQK)}
        for l in range(2):
            ATT[f"wx{l}"] = Att(f"wx{l}", [(t, x) for t in range(TT) for x in range(AH)], 2 * T, 2, AD ** -0.5, AD)
        ATT["wc0"] = Att("wc0", [(t, x) for t in range(2, 4) for x in range(AH)], T, 2, AD ** -0.5, AD)
        att_p = {"mla": area(spare, 0, 3, T)}
        att_pT = {"mla": area(spare, 768, 3, T)}
        for k in ("wx0", "wx1", "wc0"):
            att_p[k] = area(hflat, 2048, 2, 2 * T)
            att_pT[k] = area(hflat, 3072, 2, 2 * T)

        @block.tensor
        def _(pe):
            def take(*key, bank=None):
                if bank is None:
                    bank = turn[0] % turn[1]
                    turn[0] += 1
                u = Use(bank, bank_uses[bank])
                bank_uses[bank] += 1
                assert key not in uses, key
                uses[key] = u
                if u.nth:
                    pe.wait_ge(bank_free[bank], u.nth)
                return u

            def full(ins, u):
                ins.then_inc(bank_full[u.bank], 1)

            def chunk(src, n, pattern, **dims):
                i = len(chunks)
                view = ring[:, i % SLOTS, 0:n].rearrange(pattern, **dims)
                slot_loads[i % SLOTS] += 16 * (2 if isinstance(src, tuple) else 1)
                chunks.append([src, view, None, slot_loads[i % SLOTS]])
                pe.wait_ge(slot_full[i % SLOTS], slot_loads[i % SLOTS])
                return view

            def split_chunk(src, pattern, **dims):
                i = len(chunks)
                slot_loads[i % SLOTS] += 16 * (2 if isinstance(src, tuple) else 1)
                chunks.append([src, ring[:, i % SLOTS, :].rearrange(pattern, **dims), None, slot_loads[i % SLOTS]])
                splits.append(i)
                pe.wait_ge(sig("weights_lo"), len(splits))
                return (ring_hi[:, (len(splits) - 1) % HIS, :].rearrange(pattern, **dims),
                        ring_lo[:, i % SLOTS, :].rearrange(pattern, **dims))

            def release(ins):
                ins.then_inc(chunk_used, 1)
                used[0] += 1
                chunks[-1][2] = (chunk_used, used[0])

            def release_with(u, n=1):
                for c in chunks[-n:]:
                    if c[2] is None:
                        c[2] = (bank_full[u.bank], u.nth + 1)

            def mm(o, l, r, start=True, stop=True):
                return pe.matmul(o, l, r, start=start, stop=stop, skip_group_check=True)

            def mm3(o, left, right, start, stop):
                mm(o, left(0), right(0), start, False)
                mm(o, left(0), right(1), False, False)
                return mm(o, left(1), right(0), False, stop)

            def kpm(w):
                return w.rearrange("(k p) c -> p k c", p=P)

            def sum_squares(tag, halves):
                pe.wait_ge(sig("squares_ready"), norm_count[0] + 1)
                norm_count[0] += 1
                u = take("norm", tag, bank=4 if tag == "final" else None)
                n = len(halves)
                for k in range(KD):
                    m = mm(ps[:, u.bank, 0:n * T], ones, h[:, 0:n, k, :] if n > 1 else h[:, 0, k, :],
                           k == 0, k == KD - 1)
                full(m, u)

            norm_count = [0]

            def project(tag, w, c0, c1, tiles):
                for j, a in enumerate(range(c0, c1, 512)):
                    b = min(a + 512, c1)
                    us = []
                    for half in range(2):
                        v = chunk(kpm(w[half * 512:(half + 1) * 512, a:b]), 4 * (b - a), "p (k c) -> p k c", k=4)
                        for x, t in enumerate(tiles):
                            if half == 0:
                                us.append(take(tag, j, t))
                            for k in range(4):
                                kk = 4 * half + k
                                m = mm(ps[:, us[x].bank, 0:b - a], h[:, t // 2, kk, (t % 2) * P:(t % 2) * P + P],
                                       v[:, k, :], kk == 0, kk == KD - 1)
                            if half == 1:
                                full(m, us[x])
                        if half == 0:
                            release(m)
                    release_with(us[-1])

            def out_project(tag, w, halves, n):
                pe.wait_ge(sig("mixT_ready"), n)
                for c in range(4):
                    v = chunk(kpm(w[:, c * 256:(c + 1) * 256]), SLOT, "p (k c) -> p k c", k=8)
                    for m2 in range(2):
                        u = take(tag, 2 * c + m2)
                        for k in range(KD):
                            m = mm(ps[:, u.bank, 0:halves * T], v[:, k, m2 * P:(m2 + 1) * P],
                                   h[:, 0:2, k, :] if halves > 1 else h[:, 0, k, :], k == 0, k == KD - 1)
                        full(m, u)
                    release_with(u)

            def transpose_mix(tag, src, tiles):
                for t in tiles:
                    pe.wait_ge(sig("mix_ready"), MIXED[tag] + t + 1)
                    for g in range(2):
                        u = take(tag, "mixT", t, g)
                        for j in range(4):
                            f = 4 * g + j
                            m = pe.transpose(ps[:, u.bank, j * P:(j + 1) * P], src[:, t, f * P:(f + 1) * P], ident)
                        full(m, u)

            def ffn(tag, wa, wb, wd, halves, first_bank):
                hs = (h_hi, h_lo)
                for m0 in range(KF):
                    src = (kpm(wa[:, m0 * P:(m0 + 1) * P]), kpm(wb[:, m0 * P:(m0 + 1) * P]))
                    v = split_chunk(src, "p (k a c) -> p k a c", k=8, a=2)
                    if halves == 1:
                        u = take(tag, "up", m0, bank=m0 % 4)
                        for a in range(2):
                            for k in range(KD):
                                m = mm3(ps[:, u.bank, a * T:(a + 1) * T], lambda s: v[s][:, k, a, :],
                                        lambda s: hs[s][:, 0, k, :], k == 0, k == KD - 1)
                        full(m, u)
                        release_with(u)
                    else:
                        for a in range(2):
                            u = take(tag, "up", m0, a, bank=2 * (m0 % 2) + a)
                            for k in range(KD):
                                m = mm3(ps[:, u.bank, :], lambda s: v[s][:, k, a, :], lambda s: hs[s][:, 0:2, k, :],
                                        k == 0, k == KD - 1)
                            full(m, u)
                        release_with(u)
                us = {}
                if halves == 2:
                    ffn2_down.append(len(chunks))
                for c in range(KF // 2):
                    v = split_chunk(kpm(wd[c * 256:(c + 1) * 256, :]), "p (k c) -> p k c", k=2)
                    for kk in range(2):
                        kt = 2 * c + kk
                        pe.wait_ge(sig("hidden_ready"), hidden[0] + kt + 1)
                        for hf in range(halves):
                            for m0 in range(KD):
                                if (hf, m0 // 2) not in us:
                                    us[hf, m0 // 2] = take(tag, "down", hf, m0 // 2, bank=(4 + m0 // 2 + 4 * hf) % 8)
                                u = us[hf, m0 // 2]
                                m = mm3(ps[:, u.bank, (m0 % 2) * T:(m0 % 2 + 1) * T],
                                        lambda s: v[s][:, kk, m0 * P:(m0 + 1) * P],
                                        lambda s: (g1[s][:, kt, :] if halves == 1
                                                   else g2r[s][:, kt % 4, hf * T:(hf + 1) * T]),
                                        kt == 0 and m0 % 2 == 0, kt == KF - 1)
                                if kt == KF - 1 and m0 % 2 == 1:
                                    full(m, u)
                    if c < KF // 2 - 1:
                        release(m)
                    else:
                        release_with(u)
                hidden[0] += KF

            hidden = [0]

            def attend(at, qk, v):
                n_items, nk = len(at.items), at.keys // P

                def scores(n):
                    u = take(at.tag, "s", n, bank=n % 3)
                    parts = qk(*at.items[n])
                    for i, (l, r, c0, w, st, sp) in enumerate(parts):
                        m = mm(ps[:, u.bank, c0:c0 + w], l, r, st, sp)
                    full(m, u)

                def turn_p(n):
                    pe.wait_ge(sig("att_p"), ITEMS[at.tag] + n + 1)
                    u = take(at.tag, "pT", n, bank=3 if at.tag == "mla" else 3 + n % 3)
                    for k in range(nk):
                        m = pe.transpose(ps[:, u.bank, k * P:(k + 1) * P],
                                         att_p[at.tag][:, n % at.nbuf, k * P:(k + 1) * P], ident)
                    full(m, u)

                def pv(n):
                    t, hd = at.items[n]
                    if hd == 0:
                        attend.o = take(at.tag, "o", t, bank=(4 if at.tag == "mla" else 6) + t % 2)
                    pe.wait_ge(sig("att_pT"), ITEMS[at.tag] + n + 1)
                    for k in range(nk):
                        m = mm(ps[:, attend.o.bank, hd * 64:hd * 64 + 64],
                               att_pT[at.tag][:, n % at.nbuf, k * P:(k + 1) * P], v(k, hd), k == 0, k == nk - 1)
                    if hd == 7:
                        full(m, attend.o)
                    else:
                        m.then_inc(sig("att_pv"), 1)

                scores(0)
                scores(1)
                for n in range(n_items):
                    if n + 2 < n_items:
                        scores(n + 2)
                    if at.tag == "mla":
                        fill(1)
                    turn_p(n)
                    if n:
                        pv(n - 1)
                pv(n_items - 1)

            pe.wait_ge(sig("const_loaded"), 48)

            def turn_mod(i):
                pe.wait_ge(sig("mod_row"), i + 1)
                u = take("modT", i, bank=6)
                for m2 in range(2):
                    m = pe.transpose(ps[:, u.bank, 2 * m2:2 * m2 + 2], modrow[0:2, i % 2, m2 * P:(m2 + 1) * P],
                                     ident[0:2, 0:2])
                full(m, u)

            filled = [0]

            def fill(n):
                for i in range(filled[0], filled[0] + n):
                    l, c = divmod(i, MOD_PIECES // 2)
                    v = chunk(kpm(A["w_mod_2"][l, :, c * 256:(c + 1) * 256]), SLOT, "p (k c) -> p k c", k=8)
                    u = take("mod", i, bank=7)
                    for k in range(KD):
                        m = mm(ps[0:2, u.bank, 0:256], cols[:, COLS["cond"] + 2 * k:COLS["cond"] + 2 * k + 2],
                               v[:, k, :], k == 0, k == KD - 1)
                    full(m, u)
                    release_with(u)
                    if i:
                        turn_mod(i - 1)
                filled[0] += n

            pe.wait_ge(sig("cond_ready"), 1)
            fill(FILL["start"])

            sum_squares("even", [0])
            pe.wait_ge(sig("h_ready"), 1)
            project("even_in", A["w_in_even"][0], 0, EVEN["end"], range(TT))
            fill(FILL["latents"])
            for t in range(TT):
                pe.wait_ge(sig("mla_c"), t + 1)
                for g, (a, n) in enumerate(((0, 3), (3, 2))):
                    u = take("mla_cT", t, g)
                    for j in range(n):
                        m = pe.transpose(ps[:, u.bank, j * P:(j + 1) * P], pe_[:, t, (a + j) * P:(a + j + 1) * P], ident)
                    full(m, u)
            pe.wait_ge(sig("mla_cT"), TT)
            for half in range(2):
                v = chunk(A["mla_w_uq"][0][:, half * 384:(half + 1) * 384].rearrange("(k p) c -> p k c", p=P),
                          3 * 384, "p (k c) -> p k c", k=3)
                for t in range(TT):
                    u = take("mla_q", t, half)
                    for k in range(3):
                        m = mm(ps[:, u.bank, 0:384], cT[:, k, t * P:(t + 1) * P], v[:, k, :], k == 0, k == 2)
                    full(m, u)
                release_with(u)
            v = chunk(A["mla_w_ukv"][0].rearrange("(k p) c -> p k c", p=P), SLOT, "p (k c) -> p k c", k=2)
            for half in range(2):
                for t in range(TT):
                    u = take("mla_kv", t, half)
                    for k in range(2):
                        m = mm(ps[:, u.bank, :], cT[:, 3 + k, t * P:(t + 1) * P], v[:, k, half * 512:(half + 1) * 512],
                               k == 0, k == 1)
                    full(m, u)
            release_with(u)
            fill(FILL["heads"])
            pe.wait_ge(sig("mla_heads"), 2)
            for t in range(TT):
                for name, src in (("qT", qh), ("kT", kx)):
                    for g in range(2):
                        u = take("mla", name, t, g)
                        for j in range(4):
                            m = pe.transpose(ps[0:MQK, u.bank, j * P:(j + 1) * P], src[:, t, 4 * g + j, :], ident)
                        full(m, u)
            pe.wait_ge(sig("mla_qT"), 4)
            pe.wait_ge(sig("mla_kT"), 4)
            attend(ATT["mla"],
                   lambda t, x: [(qT[0:MQK, x, t * P:(t + 1) * P], kT[0:MQK, x, :], 0, T, True, True)],
                   lambda k, x: kv[:, k, x, MNOPE:])
            fill(FILL["ret_rope"])
            pe.wait_ge(sig("ret_rope"), 1)
            for t in range(TT):
                for g in range(2):
                    u = take("ret_T", t, g)
                    for j in range(4):
                        src = rqk[:, t, g, 2 * j:2 * j + 2, :].rearrange("p a b -> p (a b)")
                        m = pe.transpose(ps[:, u.bank, j * P:(j + 1) * P], src, ident)
                    full(m, u)
            pe.wait_ge(sig("ret_T"), 4)
            for x in range(RH + 1):
                if x < RH:
                    u = take("ret_s", x, bank=x % 4)
                    b0 = 64 * (x % 2)
                    for s in range(TT):
                        m = mm(ps[:, u.bank, s * T:(s + 1) * T], rT[b0:b0 + 64, 4 + x // 2, s * P:(s + 1) * P],
                               rT[b0:b0 + 64, x // 2, :])
                    full(m, u)
                if x >= 1:
                    y = x - 1
                    if y == 0:
                        ro_use = [take("ret_o", t, bank=4 + t) for t in range(TT)]
                    pe.wait_ge(sig("ret_sdec"), y + 1)
                    for t in range(TT):
                        for s in range(TT):
                            m = mm(ps[:, ro_use[t].bank, y * 64:y * 64 + 64], sdec[:, y % 2, s, t * P:(t + 1) * P],
                                   pe_[:, s, EVEN["rv"] + 64 * y:EVEN["rv"] + 64 * y + 64], s == 0, s == TT - 1)
                        if y == RH - 1:
                            full(m, ro_use[t])
                    if y < RH - 1:
                        m.then_inc(sig("ret_pv"), 1)
            fill(FILL["even_mix"])
            transpose_mix("even", mix0, range(TT))
            out_project("even_out", A["w_out_even"][0], 1, 2 * (MIXED["even"] + TT))

            def first_ffn(l):
                fill(FILL[f"ffn{l}"])
                sum_squares(f"ffn{l}", [0])
                pe.wait_ge(sig("h_ready"), 2 + 2 * l)
                pe.wait_ge(sig("h_lo"), KD * (l + 1))
                ffn(f"ffn{l}", A["ffn_w_up"][l][:, 0:F], A["ffn_w_up"][l][:, F:2 * F], A["ffn_w_down"][l], 1, 4)

            first_ffn(0)

            fill(FILL["odd"])
            sum_squares("odd", [0])
            pe.wait_ge(sig("h_ready"), 3)
            project("odd_in", A["w_in_odd"][0], 0, ODD["end"], range(TT))
            pe.wait_ge(sig("proj_act"), PROJ["odd_in"])
            pe.wait_ge(sig("proj_dve"), PROJ["odd_in"])
            for t in range(TT):
                u = take("gla_gT", t)
                for d in range(2):
                    a = ODD["gf"] + GR * d
                    m = pe.transpose(ps[0:GR, u.bank, d * P:(d + 1) * P], po[:, t, a:a + GR], ident)
                full(m, u)
            for t in range(TT):
                for g in range(2):
                    u = take("gla_T", t, g)
                    for j in range(4):
                        a = 512 * g + P * j
                        m = pe.transpose(ps[:, u.bank, j * P:(j + 1) * P], po[:, t, a:a + P], ident)
                    full(m, u)
            pe.wait_ge(sig("gla_gT"), TT)
            pe.wait_ge(sig("gla_const"), 80)
            for d in range(2):
                for t in range(TT):
                    u = take("gla_la", d, t)
                    mm(ps[:, u.bank, :], gaT[0:GR, d, t * P:(t + 1) * P], wg[0:GR, d, :], True, False)
                    m = mm(ps[:, u.bank, :], cst[0:1, CST["ones"]:CST["ones"] + P], gbias[0:1, d, :], False, True)
                    full(m, u)
            fill(FILL["gla_gates"])
            for d in range(2):
                for t in range(TT):
                    pe.wait_ge(sig("gla_la"), 2 * d + t + 1)
                    u = take("gla_kd", d, t)
                    m = mm(ps[:, u.bank, :], glam[:, 3 * d + 2, :], la[:, d, t, :])
                    full(m, u)
            pe.wait_ge(sig("gla_T"), 2 * TT)
            for x in range(GH):
                oacc = None
                for d in range(2):
                    n = 2 * x + d
                    u = take("gla_b", n)
                    for w in range(2):
                        for t in range(TT):
                            m = mm(ps[:, u.bank, w * T + t * P:w * T + (t + 1) * P],
                                   la[:, d, t, x * P:(x + 1) * P], glam[:, 3 * d + w, :])
                    full(m, u)
                    pe.wait_ge(sig("gla_kdT"), 4)
                    for i in range(3):
                        c = i if d == 0 else 3 - i
                        u = take("gla_st", n, i)
                        b0 = GC * (c % 2)
                        m = mm(ps[:, u.bank, 0:GV],
                               kdT[b0:b0 + GC, d, c // 2, x * P:(x + 1) * P],
                               po[b0:b0 + GC, c // 2, ODD["v"] + x * GV:ODD["v"] + (x + 1) * GV])
                        full(m, u)
                    fill(FILL["gla"] // (2 * GH))
                    pe.wait_ge(sig("gla_qk"), n + 1)
                    u = take("gla_A", n)
                    for t in range(TT):
                        m = mm(ps[:, u.bank, t * P:(t + 1) * P], gqkx[:, d, 1, t * P:(t + 1) * P],
                               gqkx[:, d, 0, t * P:(t + 1) * P])
                    full(m, u)
                pe.wait_ge(sig("gla_Am"), 2 * x + 2)
                pe.wait_ge(sig("gla_states"), 2 * x + 2)
                u = take("gla_o", x)
                for t in range(TT):
                    parts = []
                    for d in range(2):
                        parts.append((slice(0, P), gA[:, d, t, :],
                                      po[:, t, ODD["v"] + x * GV:ODD["v"] + (x + 1) * GV]))
                    first = True
                    for (_, l, r) in parts:
                        mm(ps[:, u.bank, t * GV:(t + 1) * GV], l, r, first, False)
                        first = False
                    for d in range(2):
                        for c in (2 * t, 2 * t + 1):
                            i = c if d == 0 else 3 - c
                            if i == 0:
                                continue
                            b0 = GC * (c % 2)
                            m = mm(ps[b0:b0 + GC, u.bank, t * GV:(t + 1) * GV], gqkx[:, d, 2, c * GC:(c + 1) * GC],
                                   gst[:, d, i - 1, :], False, True)
                full(m, u)
            fill(FILL["odd_mix"])
            transpose_mix("odd", po, range(TT))
            out_project("odd_out", A["w_out_odd"][0], 1, 2 * (MIXED["odd"] + TT))
            first_ffn(1)

            turn_mod(MOD_PIECES - 1)
            turn[1] = 8
            for l in range(2):
                sum_squares(f"n1_{l}", [0, 1])
                pe.wait_ge(sig("h_ready"), 5 + 2 * l)
                w = A["w_in_2"][l]
                xs, both = range(TT), range(4)
                project(f"q{l}", w, 0, 512, both if l == 0 else xs)
                project(f"kv{l}", w, 512, 768, both)
                for c in range(2):
                    v = chunk(kpm(w[:, 768 + c * 256:768 + (c + 1) * 256]), SLOT, "p (k c) -> p k c", k=8)
                    for m2 in range(2):
                        u = take("conv", l, 2 * c + m2)
                        for k in range(KD):
                            if l == 0 or c == 1:
                                m = mm(ps[:, u.bank, :], v[:, k, m2 * P:(m2 + 1) * P], h[:, :, k, :],
                                       k == 0, k == KD - 1)
                            else:
                                m = mm(ps[:, u.bank, 0:T], v[:, k, m2 * P:(m2 + 1) * P], h[:, 0, k, :],
                                       k == 0, k == KD - 1)
                        full(m, u)
                    release_with(u)
                project(f"mv{l}", w, 1280, 1792, both)
                project(f"o{l}", w, 1792, 2304, both if l == 0 else xs)
                v = chunk(kpm(w[:, 2304:2320]), 128, "p (k c) -> p k c", k=8)
                u = take("gT", l)
                for t in both:
                    for k in range(KD):
                        m = mm(ps[:, u.bank, 16 * t:16 * t + 16], h[:, t // 2, k, (t % 2) * P:(t % 2) * P + P],
                               v[:, k, :], k == 0, k == KD - 1)
                full(m, u)
                release_with(u)
                pe.wait_ge(sig("gT"), l + 1)
                for g in range(4):
                    u = take("gates", l, g)
                    for t in both:
                        m = pe.transpose(ps[0:4, u.bank, t * P:(t + 1) * P], gT[:, t, 4 * g:4 * g + 4], ident)
                    full(m, u)
                pe.wait_ge(sig("att_rope"), 2 * (l + 1))
                for t in both:
                    if t < 2 or l == 0:
                        u = take("aqT", l, t)
                        for j in range(4):
                            src = ro[:, t, j * P:(j + 1) * P] if t < 2 else p2[:, t, j * P:(j + 1) * P]
                            m = pe.transpose(ps[:, u.bank, j * P:(j + 1) * P], src, ident)
                        full(m, u)
                for g in range(AG):
                    u = take("akT", l, g)
                    for t in both:
                        src = kdup[:, t, g, :, :].rearrange("p a b -> p (a b)")
                        m = pe.transpose(ps[:, u.bank, t * P:(t + 1) * P], src, ident)
                    full(m, u)
                pe.wait_ge(sig("aqT"), 4 if l == 0 else 6)
                pe.wait_ge(sig("akT"), 2 * (l + 1))
                pe.wait_ge(sig("wmask"), 16)

                def window(t, x):
                    b0 = 64 * (x % 2)
                    q = aqT[b0:b0 + 64, x // 2, t * P:(t + 1) * P]
                    return [(q, akT[b0:b0 + 64, x // 4, 0:T], 0, T, True, False),
                            (ident, wmask[:, t, :], 0, T, False, True),
                            (q, akT[b0:b0 + 64, x // 4, T:2 * T], T, T, True, True)]

                attend(ATT[f"wx{l}"], window, lambda k, x: p2[:, k, 640 + 64 * (x // 4):704 + 64 * (x // 4)])
                if l == 0:
                    def to_ctx(t, x):
                        b0 = 64 * (x % 2)
                        return [(aqT[b0:b0 + 64, x // 2, t * P:(t + 1) * P], akT[b0:b0 + 64, x // 4, T:2 * T],
                                 0, T, True, True)]

                    attend(ATT["wc0"], to_ctx, lambda k, x: p2[:, 2 + k, 640 + 64 * (x // 4):704 + 64 * (x // 4)])
                pe.wait_ge(sig("lrows"), l + 1)
                u = take("lcols", l)
                for t in both:
                    for w_, src in enumerate((gates, brow)):
                        for d in range(2):
                            c0 = (t * 4 + w_ * 2 + d) * 4
                            s_ = (gates[0:4, 2 * d, t * P:(t + 1) * P] if w_ == 0 else brow[0:4, d, t * P:(t + 1) * P])
                            m = pe.transpose(ps[:, u.bank, c0:c0 + 4], s_, ident[0:4, 0:4])
                full(m, u)
                pe.wait_ge(sig("conv_done"), 4 * (l + 1))
                pe.wait_ge(sig("vaug_ones"), l + 1)
                pe.wait_ge(sig("proj_act"), PROJ[f"mv{l}"])
                pe.wait_ge(sig("proj_dve"), PROJ[f"mv{l}"])
                steps = lsteps(l)

                def row_max(n):
                    sq, x, d = steps[n]
                    if d == 0:
                        b0 = 64 * (x % 2)
                        for i, s in enumerate(STILES[sq]):
                            if i % 2 == 0:
                                u = take("ls", l, sq, x, i // 2, bank=i // 2 + 2 * (x % 2))
                            m = mm(ps[:, u.bank, (i % 2) * T:(i % 2 + 1) * T],
                                   conv[b0:b0 + 64, 2 + x // 2, s * P:(s + 1) * P],
                                   conv[b0:b0 + 64, x // 2, sq * T:(sq + 1) * T])
                            if i % 2 == 1:
                                full(m, u)
                    u = take("lm", l, n, bank=4 + n % 2)
                    full(mm(ps[:, u.bank, 0:T], cst[0:4, CST["sel4"] + x * P:CST["sel4"] + (x + 1) * P],
                            mrow[0:4, d, sq * T:(sq + 1) * T]), u)

                row_max(0)
                row_max(1)
                for n, (sq, x, d) in enumerate(steps):
                    if n + 2 < len(steps):
                        row_max(n + 2)
                    pe.wait_ge(sig("lp"), 16 * l + n + 1)
                    u = take("lo", l, n, bank=6 + n % 2)
                    for t in range(TT):
                        tiles = [i for i, s in enumerate(STILES[sq])
                                 if s // 2 != sq or (s % 2 <= t if d == 0 else s % 2 >= t)]
                        for i in tiles:
                            m = mm(ps[:, u.bank, t * 129:t * 129 + 129], lp[n % 2][:, i, t * P:(t + 1) * P],
                                   vaug[:, STILES[sq][i], x, :], i == tiles[0], i == tiles[-1])
                    full(m, u)
                turn[0] = 0
                tiles = both if l == 0 else xs
                transpose_mix(f"mix{l}", mix2, tiles)
                out_project(f"out{l}", A["w_out_2"][l], 2 if l == 0 else 1, 2 * (MIXED[f"mix{l}"] + len(tiles)))
                sum_squares(f"n2_{l}", [0, 1] if l == 0 else [0])
                pe.wait_ge(sig("h_ready"), 6 + 2 * l)
                if l == 0:
                    pe.wait_ge(sig("h_lo"), 4 * KD)
                    ffn("ffn2", A["ffn_w1_2"][0], A["ffn_w3_2"][0], A["ffn_w2_2"][0], 2, 4)

            us = []
            for t in range(TT):
                u = take("router", t)
                us.append(u)
            v = chunk(kpm(A["w_router_2"][0]), 64, "p (k c) -> p k c", k=8)
            for t in range(TT):
                for k in range(KD):
                    m = mm(ps[:, us[t].bank, 0:NE], h[:, 0, k, t * P:(t + 1) * P], v[:, k, :], k == 0, k == KD - 1)
                full(m, us[t])
            release_with(us[-1])
            for t in range(TT):
                for g in range(2):
                    u = take("htok", t, g)
                    for j in range(4):
                        m = pe.transpose(ps[:, u.bank, j * P:(j + 1) * P], h[:, 0, 4 * g + j, t * P:(t + 1) * P], ident)
                    full(m, u)
            pe.wait_ge(sig("moe_const"), 16)
            pe.wait_ge(sig("combine"), TT)
            u = take("rank")
            mm(ps[:, u.bank, 0:NE], before, taken[:, 0, :])
            mm(ps[:, u.bank, NE:2 * NE], ones, taken[:, 0, :], True, False)
            mm(ps[:, u.bank, NE:2 * NE], before, taken[:, 1, :], False, True)
            mm(ps[:, u.bank, 2 * NE:3 * NE], ones, taken[:, 0, :], True, False)
            full(mm(ps[:, u.bank, 2 * NE:3 * NE], ones, taken[:, 1, :], False, True), u)
            pe.wait_ge(sig("rank"), 1)
            u = take("rw8")
            for w_, src in enumerate((rank, combine)):
                for t in range(TT):
                    m = pe.transpose(ps[0:NE, u.bank, w_ * T + t * P:w_ * T + (t + 1) * P], src[:, t, :], ident)
            full(m, u)
            pe.wait_ge(sig("rw8"), 1)
            for e in range(NE):
                u = take("rw", e)
                full(mm(ps[:, u.bank, :], sel8[0:NE, e * P:(e + 1) * P], rw8[0:NE, :]), u)
            moe_acc = [take("moe_acc", q, bank=4 + q) for q in range(4)]
            pe.wait_ge(sig("zero_ready"), 1)
            for q in range(4):
                mm(ps[:, 4 + q, :], temp[:, 0:P], temp[:, 0:512], True, False)

            def gather(x, half):
                for k in range(4):
                    for t in range(TT):
                        kk = 4 * half + k
                        m = mm(ps[:, 2, k * P:(k + 1) * P], htok[:, t, kk * P:(kk + 1) * P], pick[:, x, t, :],
                               t == 0, t == TT - 1)
                m.then_inc(sig("gather_full"), 1)

            def turn_tile(i, e, m0):
                n = e * KF + m0
                pe.wait_ge(sig("moe_val"), i * (2 * KF) + (n + 3))
                pe.wait_ge(sig("moe_turned"), i * (2 * KF) + (n + 1))
                pe.transpose(ps[:, 3, 0:P], mprod[:, m0 % 2, :], ident).then_inc(sig("moe_turn"), 1)

            def scatter(x, last):
                for k in range(KD):
                    m = mm(ps[:, 4 + k // 2, (k % 2) * T:(k % 2 + 1) * T], yexp[:, k * P:(k + 1) * P],
                           put_back[:, x, :], False, last)
                    if last and k % 2:
                        full(m, moe_acc[k // 2])

            loads = list(slot_loads)
            plan = []
            for n in range(2 * CPE):
                e, c = divmod(n, CPE)
                s = (len(chunks) + n) % SLOTS
                loads[s] += 32 if c < KF else 16
                if c < KF:
                    tells = (sig(f"moe_up{c % 2}"), e * (KF // 2) + c // 2 + 1, KF)
                else:
                    tells = (sig("moe_down"), HIS + e * (KF // 2) + c - KF + 1, KF)
                plan.append((s, loads[s], tells))
            per_slot = [b - a for a, b in zip(slot_loads, loads)]
            moe.update(chunk=len(chunks), plan=plan, split=len(splits), per_slot=per_slot)
            for _ in range(HIS):
                pe.sem_inc(sig("moe_down"), 1)

            def expert_weights(i, n, pattern, **dims):
                pe.wait_ge(sig("weights_lo"), i * (2 * CPE) + (len(splits) + n + 1))
                return (ring_hi[:, (len(splits) + n) % HIS, :].rearrange(pattern, **dims),
                        ring_lo[:, plan[n][0], :].rearrange(pattern, **dims))

            for b in range(4):
                if bank_uses[b]:
                    pe.wait_ge(bank_free[b], bank_uses[b])
            pe.wait_ge(sig("pick"), 1)
            pe.wait_ge(sig("htok"), 2 * TT)
            gather(0, 0)
            pe.wait_ge(sig("xexp"), 1)
            gather(0, 1)
            pe.wait_ge(sig("passes"), 1)
            n_passes = pe.value_load(passes[0:1, 0:1], min_val=1, max_val=2)
            with pe.Fori(0, n_passes * (NE // 2)) as i:
                for e in range(2):
                    pe.wait_ge(sig("xexp"), i * 4 + (2 * e + 2))
                    for m0 in range(KF):
                        v = expert_weights(i, e * CPE + m0, "p (k c) -> p k c", k=8)
                        b = m0 % 2
                        pe.wait_ge(sig("moe_val"), i * (2 * KF) + (e * KF + m0 + 1))
                        for k in range(KD):
                            m = mm3(ps[:, b, 0:2 * P], lambda s: xexp[s][:, e, k, :], lambda s: v[s][:, k, :],
                                    k == 0, k == KD - 1)
                        m.then_inc(sig(f"moe_up{b}"), 1)
                        if m0 == 1:
                            pe.wait_ge(sig("yexp"), i * 2 + (e + 1))
                        if m0:
                            turn_tile(i, e, m0 - 1)
                        if m0 == 5:
                            scatter(i * 2 + e, False)
                        if m0 == 14:
                            if e == 0:
                                pe.wait_ge(sig("pick"), 2)
                            gather(i * 2 + (e + 1), 0)
                        if m0 == 18:
                            pe.wait_ge(sig("xexp"), i * 4 + (2 * e + 3))
                            gather(i * 2 + (e + 1), 1)
                    turn_tile(i, e, KF - 1)
                    pe.wait_ge(sig("xexp"), i * 4 + (2 * e + 4))
                    pe.wait_ge(sig("moe_turned"), i * (2 * KF) + (e * KF + KF + 1))
                    for c in range(KF // 2):
                        v = expert_weights(i, e * CPE + KF + c, "p (k c) -> p k c", k=2)
                        for kk in range(2):
                            kt = 2 * c + kk
                            pe.wait_ge(sig("moe_hidden"), i * (2 * KF) + (e * KF + kt + 3))
                            for a in range(2):
                                m = mm3(ps[:, 2 + a, :], lambda s: hid[s][:, kt, :],
                                        lambda s: v[s][:, kk, a * 512:(a + 1) * 512], kt == 0, kt == KF - 1)
                        m.then_inc(sig("moe_down"), 1)
            pe.wait_ge(sig("yexp"), n_passes * NE + 1)
            scatter(n_passes * NE, True)
            sum_squares("final", [0])

        @block.sync
        def _(sp):
            def load(src, view, slot):
                if isinstance(src, tuple):
                    for a in range(2):
                        sp.dma_start(view[:, :, a, :], src[a]).then_inc(slot_full[slot], 16)
                else:
                    sp.dma_start(view, src).then_inc(slot_full[slot], 16)

            def kpm(w):
                return w.rearrange("(k p) c -> p k c", p=P)

            sp.dma_start(cst[:, :], A["consts"][:, 0:NKEEP]).then_inc(sig("const_loaded"), 16)
            sp.dma_start(cols[:, :], A["cols"]).then_inc(sig("const_loaded"), 16)
            sp.dma_start(rows[:, :], A["rows"].partition_broadcast(P)).then_inc(sig("const_loaded"), 16)
            sp.dma_start(res[:, 0, :, :], A["xT"]).then_inc(sig("x_loaded"), 16)
            for n, (src, view, _, _) in enumerate(chunks):
                if n >= SLOTS:
                    sp.wait_ge(*chunks[n - SLOTS][2])
                load(src, view, n % SLOTS)

            def load_expert(pair, n):
                e, c = divmod(n, CPE)
                slot = moe["plan"][n][0]
                x = pair * 2 + e
                if c < KF:
                    src = tuple(kpm(A[w][0, x, :, c * P:(c + 1) * P]) for w in ("exp_w1_2", "exp_w3_2"))
                    load(src, ring[:, slot, :].rearrange("p (k a c) -> p k a c", k=8, a=2), slot)
                else:
                    src = kpm(A["exp_w2_2"][0, x, (c - KF) * 256:(c - KF + 1) * 256, :])
                    load(src, ring[:, slot, :].rearrange("p (k c) -> p k c", k=2), slot)

            for n in range(SLOTS):
                sp.wait_ge(*chunks[moe["chunk"] + n - SLOTS][2])
                load_expert(0, n)
            sp.wait_ge(sig("passes"), 1)
            last = sp.value_load(passes[0:1, 1:2], min_val=NE // 2 - 1, max_val=NE - 1)
            with sp.Fori(0, last) as i:
                for n in range(SLOTS, 2 * CPE + SLOTS):
                    sem, value, per = moe["plan"][n - SLOTS][2]
                    sp.wait_ge(sem, i * per + value)
                    sp.sem_inc(sig("slot_open"), 1)
                    load_expert((i + n // (2 * CPE)) % (NE // 2), n % (2 * CPE))
            for n in range(SLOTS, 2 * CPE):
                sem, value, per = moe["plan"][n - SLOTS][2]
                sp.wait_ge(sem, last * per + value)
                sp.sem_inc(sig("slot_open"), 1)
                load_expert(NE // 2 - 1, n)

        @block.gpsimd
        def _(pool):
            C = A["consts"]
            pool.dma_start(posi, A["pos"]).then_inc(sig("pos_loaded"), 16)
            pool.wait_ge(sig("mla_qT"), 4)
            pool.dma_start(areaA[:, 5440:6464], C[:, CST["relp"]:CST["relp"] + 1024]).then_inc(sig("rel_loaded"), 16)
            pool.wait_ge(sig("residual"), 1)
            pool.dma_start(areaB[:, 2048:3072], C[:, CST["gla_m"]:CST["gla_m"] + 1024]).then_inc(sig("gla_const"), 16)
            for d, x in enumerate(("fwd", "bwd")):
                pool.dma_start(wg[0:GR, d, :], A[f"gla_w_gate_{x}"][0]).then_inc(sig("gla_const"), 16)
                pool.dma_start(gbias[0:1, d, :], A[f"gla_b_gate_{x}"]).then_inc(sig("gla_const"), 16)
            def split_hidden(n, src, hi, lo):
                pool.wait_ge(sig("ffn_val"), n + 1)
                pool.tensor_tensor(hi, src, ones[:, 0:1].broadcast_to([P, hi.shape[-1]]), ALU.mult).then_inc(sig("hidden_hi"), 1)
                pool.wait_ge(sig("hidden_hi"), n + 1)
                pool.tensor_tensor(lo, src, hi.bitcast(F32), ALU.subtract).then_inc(sig("hidden_ready"), 1)

            def h_rest(n, first):
                for i in range(n * KD):
                    hf, k = divmod(i, KD)
                    pool.wait_ge(sig("h_hi"), first + i + 1)
                    pool.tensor_tensor(h_lo[:, hf, k, :], h[:, hf, k, :], h_hi[:, hf, k, :].bitcast(F32),
                                       ALU.subtract).then_inc(sig("h_lo"), 1)

            for l in range(2):
                h_rest(1, KD * l)
                for m in range(KF):
                    split_hidden(KF * l + m, fval[:, m % 2, :], g1[0][:, m, :], g1[1][:, m, :])
            pool.wait_ge(sig("mod_done"), 1)
            pool.dma_start(res[:, 1, :, :], A["ctxT"]).then_inc(sig("ctx_loaded"), 16)
            pool.wait_ge(sig("residual"), 4)
            pool.dma_start(areaB[:, 5120:5632], C[:, CST["wmask"]:CST["wmask"] + 512]).then_inc(sig("wmask"), 16)
            for l in range(2):
                pool.wait_ge(sig("att_done"), l + 1)
                pool.dma_start(areaB[:, 2048:3072], C[:, CST["lmask"]:CST["lmask"] + 1024]).then_inc(sig("lmask"), 16)
                pool.wait_ge(sig("lmask"), 16 * (l + 1))
                for n, (sq, x, d) in enumerate(lsteps(l)):
                    pool.wait_ge(sig("lweights"), 16 * l + n + 1)
                    ns = len(STILES[sq])
                    own = lp[n % 2][:, ns - 2:ns, :]
                    pool.tensor_tensor(own, own, lmask[:, d, :, :], ALU.mult).then_inc(sig("lp"), 1)
                if l == 0:
                    h_rest(2, 2 * KD)
                    for m in range(KF):
                        if m >= 4:
                            pool.wait_ge(*chunks[ffn2_down[0] + (m - 4) // 2][2])
                        split_hidden(2 * KF + m, g2[:, m, :], g2r[0][:, m % 4, :], g2r[1][:, m % 4, :])
            pool.wait_ge(sig("residual"), 7)
            pool.dma_start(moe_const, C[:, CST["sel8"]:CST["sel8"] + NE * P + 2 * P + 2]).then_inc(sig("moe_const"), 16)
            pool.wait_ge(sig("passes"), 1)
            n_passes = pool.value_load(passes[0:1, 0:1], min_val=1, max_val=2)
            with pool.Fori(0, n_passes * (NE // 2)) as i:
                for e in range(2):
                    for m in range(KF):
                        pool.wait_ge(sig("moe_turned"), i * (2 * KF) + (e * KF + m + 2))
                        pool.tensor_tensor(hid[0][:, m, :], mturn[:, m % 2, :], ones, ALU.mult).then_inc(sig("moe_hi"), 1)
                        pool.wait_ge(sig("moe_hi"), i * (2 * KF) + (e * KF + m + 1))
                        pool.tensor_tensor(hid[1][:, m, :], mturn[:, m % 2, :], hid[0][:, m, :].bitcast(F32),
                                           ALU.subtract).then_inc(sig("moe_hidden"), 1)
            pool.wait_ge(sig("out_ready"), 1)
            pool.dma_start(out, h[:, 0, :, :]).then_inc(sig("out_stored"), 16)
            pool.wait_ge(sig("out_stored"), 16)

        def look(engine, *key):
            u = uses[key]
            engine.wait_ge(bank_full[u.bank], u.nth + 1)
            return u

        def free(lane, ins, u, name=None):
            ins.then_inc(bank_free[u.bank], 1)
            lane.engine.wait_ge(bank_free[u.bank], u.nth + 1)
            if name:
                lane.engine.sem_inc(sig(name), 1)

        def evacuate(lane, copy, tag, c0, c1, tiles, mine, dst, name):
            for j, a in enumerate(range(c0, c1, 512)):
                b = min(a + 512, c1)
                for t in tiles:
                    if t % 2 == mine:
                        u = look(lane.engine, tag, j, t)
                        ins = copy(dst(t, a - c0, b - c0), ps[:, u.bank, 0:b - a])
                        free(lane, ins, u)
            lane.engine.sem_inc(sig(name), 1)

        def in_stages(l):
            b = range(4)
            x = b if l == 0 else range(TT)
            return [(f"q{l}", 0, 512, x, lambda t, a, c: p2[:, t, a:c]),
                    (f"kv{l}", 512, 768, b, lambda t, a, c: p2[:, t, 512 + a:512 + c])], \
                   [(f"mv{l}", 1280, 1792, b, lambda t, a, c: vaug[:, t, :, 0:LV]),
                    (f"o{l}", 1792, 2304, x, lambda t, a, c: p2[:, t, 768 + a:768 + c])]

        def pv_done(engine, at, n):
            t, hd = at.items[n]
            if hd == 7:
                look(engine, at.tag, "o", t)
            else:
                engine.wait_ge(sig("att_pv"), ITEMS[at.tag] * 7 // 8 + sum(1 for i in at.items[:n + 1] if i[1] < 7))

        @block.scalar
        def _(act):
            L = Lane(act, sig, "act_step")

            def copy(dst, src):
                return act.activation(dst, src, ACT.Copy)

            def rstd(dst, src, n):
                L.step(act.activation(dst, src, ACT.Ln, bias=eps, scale=1.0 / n))

            def norm(tag, n, before):
                act.wait_ge(*before)
                L.tell(act.activation(h[:, 0:n, :, :], res[:, 0:n, :, :], ACT.Square), "squares_ready")
                u = look(act, "norm", tag)
                free(L, act.activation(temp[:, 0:n * T], ps[:, u.bank, 0:n * T], ACT.Ln, bias=eps, scale=1.0 / D), u)
                L.tell(act.activation(temp[:, 0:n * T], temp[:, 0:n * T], ACT.Exp, scale=-0.5), "rstd_ready")

            def attend(at):
                k0 = at.keys
                for n, (t, hd) in enumerate(at.items):
                    L.wait("att_m", ITEMS[at.tag] + n + 1)
                    if n >= at.nbuf:
                        look(act, at.tag, "pT", n - at.nbuf)
                    u = look(act, at.tag, "s", n)
                    free(L, act.activation(att_p[at.tag][:, n % at.nbuf, 0:k0], ps[:, u.bank, 0:k0], ACT.Exp,
                                           bias=stat[:, n:n + 1], scale=at.scale, accum_out=stat[:, 16 + n:17 + n]),
                         u, "att_p")
                    if at.tag == "mla":
                        fill(1)
                    if hd == 7 and at.tag != "mla":
                        L.wait("att_sink", SINKS[at.tag] + n // 8 + 1)
                        L.tell(act.activation(stat[:, 32 + n - 7:33 + n], stat[:, 32 + n - 7:33 + n], ACT.Exp),
                               "att_esink")

            def weights_hi(j):
                n = splits[j]
                act.wait_ge(slot_full[n % SLOTS], chunks[n][3])
                if j >= HIS:
                    act.wait_ge(*chunks[splits[j - HIS]][2])
                L.tell(copy(ring_hi[:, j % HIS, :], ring[:, n % SLOTS, :]), "weights_hi")

            def h_rounded(n, first):
                for i in range(n * KD):
                    hf, k = divmod(i, KD)
                    L.wait("h_raw", first + i + 1)
                    L.tell(copy(h_hi[:, hf, k, :], h[:, hf, k, :]), "h_hi")

            filled = [0]

            def turned_mod(i):
                l, c = divmod(i, MOD_PIECES // 2)
                u = look(act, "modT", i)
                free(L, copy(mods[:, l, 2 * c:2 * c + 2, :], ps[:, u.bank, 0:4].rearrange("p (a b) -> p a b", a=2)), u)

            def fill(n):
                for i in range(filled[0], filled[0] + n):
                    u = look(act, "mod", i)
                    free(L, copy(modrow[0:2, i % 2, :], ps[0:2, u.bank, 0:256]), u, "mod_row")
                    if i:
                        turned_mod(i - 1)
                filled[0] += n

            act.wait_ge(sig("const_loaded"), 48)
            c = cols[:, COLS["cond"]:COLS["cond"] + 16]
            L.tell(act.activation(c, c, ACT.Silu), "cond_ready")
            u16 = stat[:, 80:96]
            L.step(act.activation(u16, rows[:, ROWS["theta"]:ROWS["theta"] + 16], ACT.Exp, scale=-float(np.log(2.0))))
            L.tell(act.activation(temp[:, 256:272], u16, ACT.Ln, scale=-1.0, bias=1.0), "theta_ready")
            L.wait("angle_ready", 1)
            L.step(act.activation(sin, ang, ACT.Sin))
            L.tell(act.activation(cos, ang, ACT.Sin, scale=0.5), "sin_ready")

            fill(FILL["start"])
            norm("even", 1, (sig("x_loaded"), 16))
            evacuate(L, copy, "even_in", 0, EVEN["end"], range(TT), 0, lambda t, a, b: pe_[:, t, a:b], "proj_act")
            L.wait("proj_dve", PROJ["even_in"])
            for t in range(TT):
                for i, (a, n) in enumerate(((0, CQ), (CQ, CKV))):
                    L.step(act.activation(spare[:, 0:n], pe_[:, t, a:a + n], ACT.Square,
                                          accum_out=stat[:, 2 * i + t:2 * i + t + 1]))
            for i, n in enumerate((CQ, CKV)):
                rstd(stat[:, 2 * i:2 * i + 2], stat[:, 2 * i:2 * i + 2], n)
            L.tell(act.activation(stat[:, 0:4], stat[:, 0:4], ACT.Exp, scale=-0.5), "mla_c_rstd")
            fill(FILL["latents"])
            for t in range(TT):
                r = pe_[:, t, EVEN["rg"]:EVEN["end"]]
                L.step(act.activation(r, r, ACT.Silu))
            act.sem_inc(sig("rg_ready"), 1)
            for half in range(2):
                for t in range(TT):
                    u = look(act, "mla_q", t, half)
                    dst = qh[:, t, 4 * half:4 * half + 4, :].rearrange("p a b -> p (a b)")
                    free(L, copy(dst, ps[:, u.bank, 0:384]), u)
            for half in range(2):
                for t in range(TT):
                    u = look(act, "mla_kv", t, half)
                    dst = kv[:, t, 4 * half:4 * half + 4, :].rearrange("p a b -> p (a b)")
                    free(L, copy(dst, ps[:, u.bank, :]), u)
            act.sem_inc(sig("mla_qkv"), 1)
            fill(2)
            L.wait("mla_sumsq", 1)
            rstd(stat[:, 0:32], stat[:, 0:32], MQK)
            L.tell(act.activation(stat[:, 0:32], stat[:, 0:32], ACT.Exp, scale=-0.5), "mla_rstd")
            fill(FILL["heads"] - 2)
            for t in range(TT):
                for g in range(2):
                    u = look(act, "mla", "qT", t, g)
                    free(L, copy(qT[0:MQK, 4 * g:4 * g + 4, t * P:(t + 1) * P],
                                 ps[0:MQK, u.bank, :].rearrange("p (a b) -> p a b", a=4)), u, "mla_qT")
            attend(ATT["mla"])
            fill(FILL["ret_rope"])
            for t in range(TT):
                for g in range(2):
                    u = look(act, "ret_T", t, g)
                    free(L, copy(rT[:, 4 * g:4 * g + 4, t * P:(t + 1) * P],
                                 ps[:, u.bank, :].rearrange("p (a b) -> p a b", a=4)), u, "ret_T")
            for x in range(RH):
                L.wait("ret_e", x + 1)
                L.tell(act.activation(decay[:, x % 2, :, :], decay[:, x % 2, :, :], ACT.Exp), "ret_d")
            L.wait("ret_sumsq", 1)
            rstd(stat[:, 0:16], stat[:, 0:16], RD)
            L.tell(act.activation(stat[:, 0:16], stat[:, 0:16], ACT.Exp, scale=-0.5), "ret_rstd")

            fill(FILL["even_mix"])

            def ffn1(l):
                fill(FILL[f"ffn{l}"])
                j = l * CPE
                weights_hi(j)
                weights_hi(j + 1)
                norm(f"ffn{l}", 1, (sig("residual"), 1 + 2 * l))
                h_rounded(1, KD * l)
                for m in range(CPE):
                    if m + 2 < CPE:
                        weights_hi(j + m + 2)
                    if m < KF:
                        L.wait("conv1", KF * l + m + 1)
                        L.tell(act.activation(fsil[:, m % 2, 0:T], fconv[:, m % 2, 0:T], ACT.Silu), "silu1")

            ffn1(0)

            fill(FILL["odd"])
            norm("odd", 1, (sig("residual"), 2))
            evacuate(L, copy, "odd_in", 0, ODD["end"], range(TT), 0, lambda t, a, b: po[:, t, a:b], "proj_act")
            L.wait("proj_dve", PROJ["odd_in"])
            for t in range(TT):
                for g in range(2):
                    u = look(act, "gla_T", t, g)
                    free(L, copy(gqk[:, 4 * g:4 * g + 4, t * P:(t + 1) * P],
                                 ps[:, u.bank, :].rearrange("p (a b) -> p a b", a=4)), u, "gla_T")
            for i in range(4):
                u = look(act, "gla_la", i // 2, i % 2)
                if i >= 2:
                    L.wait("gla_la", i - 1)
                b = temp[:, 512 * (i % 2):512 * (i % 2) + 512]
                L.step(act.activation(b, ps[:, u.bank, :], ACT.Abs))
                L.step(act.activation(b, b, ACT.Exp, scale=-1.0))
                L.tell(act.activation(b, b, ACT.Ln, bias=1.0), "gla_soft")
            fill(FILL["gla_gates"])
            for i in range(4):
                u = look(act, "gla_kd", i // 2, i % 2)
                if i < 2:
                    L.wait("gla_la", 3 + i)
                else:
                    L.wait("gla_kdT", i - 1)
                free(L, act.activation(temp[:, 512 * (i % 2):512 * (i % 2) + 512], ps[:, u.bank, :], ACT.Exp), u, "gla_kd")
            for t in range(TT):
                r = po[:, t, ODD["r"]:ODD["gf"]]
                L.step(act.activation(r, r, ACT.Silu))
            act.sem_inc(sig("gr_ready"), 1)
            for n in range(2 * GH):
                u = look(act, "gla_b", n)
                if n:
                    L.wait("gla_states", n)
                L.step(act.activation(gex[:, 0:2, :], ps[:, u.bank, :].rearrange("p (a b) -> p a b", a=2), ACT.Exp))
                free(L, act.activation(gex[:, 2, :], ps[:, u.bank, T:2 * T], ACT.Exp, scale=-1.0), u, "gla_ex")
                fill(FILL["gla"] // (2 * GH))
            L.wait("gla_sumsq", 1)
            rstd(stat[:, 0:8], stat[:, 0:8], GV)
            L.tell(act.activation(stat[:, 0:8], stat[:, 0:8], ACT.Exp, scale=-0.5), "gla_rstd")
            fill(FILL["odd_mix"])
            ffn1(1)
            turned_mod(MOD_PIECES - 1)
            act.sem_inc(sig("mod_done"), 1)

            for l in range(2):
                if l == 0:
                    L.wait("ctx_loaded", 16)
                norm(f"n1_{l}", 2, (sig("residual"), 4 + 2 * l))
                before, after = in_stages(l)
                for tag, a, b, tiles, dst in before:
                    evacuate(L, copy, tag, a, b, tiles, 0, dst, "proj_act")
                for c in range(4):
                    L.wait("conv2", 4 * l + c + 1)
                    v = conv[:, c, :] if l == 0 or c >= 2 else conv[:, c, 0:T]
                    L.tell(act.activation(v, v, ACT.Silu), "conv_done")
                for tag, a, b, tiles, dst in after:
                    evacuate(L, copy, tag, a, b, tiles, 0, dst, "proj_act")
                for g in range(4):
                    u = look(act, "gates", l, g)
                    free(L, act.activation(gates[0:4, g, :], ps[0:4, u.bank, :], ACT.Tanh,
                                           bias=cols[0:4, COLS["b_gates"] + 4 * l + g:COLS["b_gates"] + 4 * l + g + 1],
                                           scale=1.0 / CAP), u)
                for d in range(2):
                    f = gates[0:4, 2 * d + 1, :]
                    L.step(act.activation(f, f, ACT.Exp, scale=-CAP))
                    L.step(act.activation(f, f, ACT.Ln, bias=1.0))
                act.sem_inc(sig("gates_ready"), 1)
                L.wait("proj_dve", PROJ[f"o{l}"])
                for t in (range(4) if l == 0 else range(TT)):
                    o = p2[:, t, 768:1280]
                    L.step(act.activation(o, o, ACT.Sigmoid))
                act.sem_inc(sig("o_ready"), 1)
                for g in range(AG):
                    u = look(act, "akT", l, g)
                    free(L, copy(akT[:, g, :], ps[:, u.bank, :]), u, "akT")
                attend(ATT[f"wx{l}"])
                if l == 0:
                    attend(ATT["wc0"])
                L.wait("lc_ready", l + 1)
                L.tell(act.activation(temp[:, 64:128], temp[:, 0:64], ACT.Exp, scale=-1.0), "lem_ready")
                lc = temp[:, 0:64].rearrange("p (t w d h) -> p t w d h", t=4, w=2, d=2)
                for n, (sq, x, d) in enumerate(lsteps(l)):
                    ns = len(STILES[sq])
                    L.wait("lw", 16 * l + n + 1)
                    own = lw[n % 2][:, ns - 2:ns, :]
                    L.step(act.activation(own, own, ACT.Exp, scale=-1.0))
                    u = uses["lm", l, n]
                    for i in range(ns - 2):
                        L.step(act.activation(lw[n % 2][:, i, :], ps[:, u.bank, 0:T], ACT.Exp,
                                              bias=lc[:, STILES[sq][i], 0, d, x:x + 1], scale=-1.0))
                    act.sem_inc(bank_free[u.bank], 1)
                    act.sem_inc(sig("lexp"), 1)
                L.wait("merge_sumsq", l + 1)
                rstd(stat[:, 0:16], stat[:, 0:16], LV)
                rstd(stat[:, 16:20], stat[:, 16:20], 512)
                L.tell(act.activation(stat[:, 0:20], stat[:, 0:20], ACT.Exp, scale=-0.5), "merge_rstd")
                if l == 0:
                    weights_hi(2 * CPE)
                    weights_hi(2 * CPE + 1)
                norm(f"n2_{l}", 2 - l, (sig("residual"), 5 + 2 * l))
                if l == 0:
                    h_rounded(2, 2 * KD)
                    for m in range(CPE):
                        if m + 2 < CPE:
                            weights_hi(2 * CPE + m + 2)
                        if m >= KF:
                            continue
                        u = look(act, "ffn2", "up", m, 0)
                        if m >= 2:
                            L.wait("ffn_val", 2 * KF + m - 1)
                        free(L, act.activation(fsil[:, m % 2, :], ps[:, u.bank, :], ACT.Silu), u)
            for t in range(TT):
                for g in range(2):
                    u = look(act, "htok", t, g)
                    free(L, copy(htok[:, t, 512 * g:512 * g + 512], ps[:, u.bank, :]), u, "htok")
            for t in range(TT):
                L.wait("top_ready", t + 1)
                L.tell(act.activation(temp[:, 600:601], temp[:, 600:601], ACT.Exp), "top_exp")

            def gathered(dst, half):
                act.activation(xexp[0][:, dst, 4 * half:4 * half + 4, :].rearrange("p k t -> p (k t)"), ps[:, 2, :],
                               ACT.Copy).then_inc(sig("xexp_hi"), 1)

            def turned(i, e, m):
                act.wait_ge(sig("moe_turn"), i * (2 * KF) + (e * KF + m + 1))
                act.wait_ge(sig("moe_hidden"), i * (2 * KF) + (e * KF + m + 1))
                act.activation(mturn[:, m % 2, :], ps[:, 3, 0:P], ACT.Copy).then_inc(sig("moe_turned"), 1)

            def expert_hi(i, n):
                s, loaded, _ = moe["plan"][n]
                act.wait_ge(slot_full[s], i * moe["per_slot"][s] + loaded)
                sem, value, per = moe["plan"][n - HIS][2]
                act.wait_ge(sem, i * per + (value if n >= HIS else value - per))
                copy(ring_hi[:, (moe["split"] + n) % HIS, :], ring[:, s, :]).then_inc(sig("weights_hi"), 1)

            for e in range(NE):
                u = look(act, "rw", e)
                if e >= 4:
                    v = uses["rw", e - 4]
                    act.wait_ge(bank_free[v.bank], v.nth + 1)
                L.tell(copy(wrow[:, e % 4, :], ps[:, u.bank, T:2 * T]), "wrow")
            for half in range(2):
                act.wait_ge(sig("gather_full"), half + 1)
                gathered(0, half)
            act.wait_ge(sig("passes"), 1)
            n_passes = act.value_load(passes[0:1, 0:1], min_val=1, max_val=2)
            with act.Fori(0, n_passes * (NE // 2)) as i:
                expert_hi(i, 0)
                expert_hi(i, 1)
                for e in range(2):
                    for m in range(CPE):
                        n = e * CPE + m
                        if m == KF:
                            turned(i, e, m - 1)
                        if n + 2 < 2 * CPE:
                            expert_hi(i, n + 2)
                        if m in (15, 19):
                            act.wait_ge(sig("gather_full"), i * 4 + (2 * e + 3 + (m == 19)))
                            gathered(1 - e, int(m == 19))
                        if m >= KF:
                            continue
                        b = m % 2
                        act.wait_ge(sig(f"moe_up{b}"), i * KF + (e * (KF // 2) + m // 2 + 1))
                        act.wait_ge(sig("moe_val"), i * (2 * KF) + (e * KF + m + 1))
                        act.activation(msil[:, b, :], ps[:, b, 0:P], ACT.Silu).then_inc(sig("moe_silu"), 1)
                        if m:
                            turned(i, e, m - 1)
            norm("final", 1, (sig("residual"), 8))

        @block.vector
        def _(dve):
            L = Lane(dve, sig, "dve_step")
            S, TTN, TS, STT = L.step, dve.tensor_tensor, dve.tensor_scalar, dve.scalar_tensor_tensor

            def copy(dst, src):
                return dve.tensor_copy(dst, src)

            def bc(v, axis, shape):
                return v.unsqueeze(axis).broadcast_to(shape)

            norms = [0]

            def norm(n, gain, shift=None, name="h_ready", split=False):
                norms[0] += 1
                L.wait("rstd_ready", norms[0])

                for i in range(n * KD):
                    hf, k = divmod(i, KD)
                    if shift:
                        if k % 4 == 0:
                            S(TTN(h[:, hf, k:k + 4, :], res[:, hf, k:k + 4, :],
                                  bc(temp[:, hf * T:(hf + 1) * T], 1, [P, 4, T]), ALU.mult))
                        ins = TS(h[:, hf, k, :], h[:, hf, k, :], gain(hf, k), shift(hf, k), ALU.mult, ALU.add)
                    else:
                        ins = STT(out=h[:, hf, k, :], in0=res[:, hf, k, :], scalar=gain(hf, k),
                                  in1=temp[:, hf * T:(hf + 1) * T], op0=ALU.mult, op1=ALU.mult)
                    if split:
                        L.tell(ins, "h_raw")
                    else:
                        S(ins)
                dve.sem_inc(sig(name), 1)

            def weights_lo(j):
                s = splits[j] % SLOTS
                L.wait("weights_hi", j + 1)
                L.tell(TTN(ring_lo[:, s, :], ring[:, s, :], ring_hi[:, j % HIS, :].bitcast(F32), ALU.subtract),
                       "weights_lo")

            def rope(x1, x2, y1, y2, c, s, t1, t2):
                S(TTN(t1, x1, s, ALU.mult))
                S(TTN(t2, x2, s, ALU.mult))
                S(TTN(y1, x1, c, ALU.mult))
                S(TTN(y2, x2, c, ALU.mult))
                S(TTN(y1, y1, t2, ALU.subtract))
                S(TTN(y2, y2, t1, ALU.add))

            def attend(at, out_of):
                items, sink = at.items, at.tag != "mla"

                def score_max(n):
                    u = look(dve, at.tag, "s", n)
                    S(dve.tensor_reduce(stat[:, 64 + n:65 + n], ps[:, u.bank, 0:at.keys], AX.X, ALU.max))
                    if sink:
                        hd = items[n][1]
                        L.tell(TS(stat[:, n:n + 1], stat[:, 64 + n:65 + n], -at.scale,
                                  rows[:, ROWS["sink"] + at_layer(at) * 8 + hd:ROWS["sink"] + at_layer(at) * 8 + hd + 1],
                                  ALU.mult, ALU.min), "att_m")
                        if hd == 7:
                            a = n - 7
                            L.tell(TTN(stat[:, 32 + a:40 + a], stat[:, a:a + 8],
                                       rows[:, ROWS["sink"] + at_layer(at) * 8:ROWS["sink"] + at_layer(at) * 8 + 8],
                                       ALU.subtract), "att_sink")
                    else:
                        L.tell(TS(stat[:, n:n + 1], stat[:, 64 + n:65 + n], -at.scale, None, ALU.mult), "att_m")

                def output(n):
                    t = items[n][0]
                    a = n - 7
                    u = look(dve, at.tag, "o", t)
                    L.wait("att_p", ITEMS[at.tag] + n + 1)
                    if sink:
                        L.wait("att_esink", SINKS[at.tag] + n // 8 + 1)
                        S(TTN(stat[:, 16 + a:24 + a], stat[:, 16 + a:24 + a], stat[:, 32 + a:40 + a], ALU.add))
                    S(dve.reciprocal(stat[:, 48 + a:56 + a], stat[:, 16 + a:24 + a]))
                    free(L, TTN(out_of(t).rearrange("p (a b) -> p a b", a=8),
                                ps[:, u.bank, :].rearrange("p (a b) -> p a b", a=8),
                                bc(stat[:, 48 + a:56 + a], 2, [P, 8, 64]), ALU.mult), u)

                score_max(0)
                score_max(1)
                for n in range(len(items)):
                    if n + 2 < len(items):
                        score_max(n + 2)
                    u = look(dve, at.tag, "pT", n)
                    if n >= at.nbuf:
                        pv_done(dve, at, n - at.nbuf)
                    free(L, copy(att_pT[at.tag][:, n % at.nbuf, 0:at.keys], ps[:, u.bank, 0:at.keys]), u, "att_pT")
                    if n and items[n - 1][1] == 7:
                        output(n - 1)
                output(len(items) - 1)

            def at_layer(at):
                return int(at.tag[-1])

            def mixT(tag, tiles, gain):
                for t in tiles:
                    for g in range(2):
                        u = look(dve, tag, "mixT", t, g)
                        for j in range(4):
                            f = 4 * g + j
                            dst, src = h[:, t // 2, f, (t % 2) * P:(t % 2 + 1) * P], ps[:, u.bank, j * P:(j + 1) * P]
                            ins = copy(dst, src) if gain(f) is None else TS(dst, src, gain(f), None, ALU.mult)
                            if j < 3:
                                S(ins)
                            else:
                                free(L, ins, u, "mixT_ready")

            L.wait("const_loaded", 48)
            neg_sink = rows[:, ROWS["sink"]:ROWS["sink"] + 16]
            S(TS(neg_sink, neg_sink, -1.0, None, ALU.mult))
            bg = cols[:, COLS["b_gates"]:COLS["b_gates"] + 8]
            S(TS(bg, bg, 1.0 / CAP, None, ALU.mult))
            L.wait("theta_ready", 1)
            u16, ln16 = stat[:, 80:96], temp[:, 256:272]
            ser, small = temp[:, 272:288], temp[:, 288:304]
            S(TS(ser, u16, 1.0 / 7, 1.0 / 6, ALU.mult, ALU.add))
            for n in (5, 4, 3, 2, 1):
                S(TTN(ser, ser, u16, ALU.mult))
                S(TS(ser, ser, 1.0 / n, None, ALU.add))
            S(STT(out=ser, in0=ser, scalar=-1.0, in1=u16, op0=ALU.mult, op1=ALU.mult))
            S(TS(small, u16, 1.0 / 16, None, ALU.is_lt))
            S(TTN(ser, ser, ln16, ALU.subtract))
            S(TTN(ser, ser, small, ALU.mult))
            S(TTN(u16, ser, ln16, ALU.add))
            L.wait("pos_loaded", 16)
            S(copy(posf, posi))
            inv = cst[:, CST["inv"]:CST["inv"] + 48]
            for t in range(TT):
                S(TS(ang[:, t, :], inv, posf[:, t:t + 1], None, ALU.mult))
            TWO_PI = 2 * np.pi
            c1 = 6.28125
            c2 = 0.0019350051879882812
            c3 = float(TWO_PI - c1 - c2)
            magic = 1.5 * 2.0 ** 23
            S(TS(angn, ang, float(1 / TWO_PI), None, ALU.mult))
            S(TS(angn, angn, magic, None, ALU.add))
            S(TS(angn, angn, -magic, None, ALU.add))
            for cc in (c1, c2, c3):
                S(STT(out=ang, in0=angn, scalar=-cc, in1=ang, op0=ALU.mult, op1=ALU.add))
            L.tell(TS(ang, ang, 3.141592, -3.141592, ALU.min, ALU.max), "angle_ready")
            L.wait("sin_ready", 1)
            S(TTN(cos, cos, cos, ALU.mult))
            S(TS(cos, cos, -2.0, 1.0, ALU.mult, ALU.add))

            norm(1, lambda hf, k: col("mix_even", k))
            evacuate(L, copy, "even_in", 0, EVEN["end"], range(TT), 1, lambda t, a, b: pe_[:, t, a:b], "proj_dve")
            L.wait("mla_c_rstd", 1)
            for t in range(TT):
                for i, (a, n) in enumerate(((0, CQ), (CQ, CKV))):
                    v = pe_[:, t, a:a + n]
                    ins = TS(v, v, stat[:, 2 * i + t:2 * i + t + 1], None, ALU.mult)
                    if i == 0:
                        S(ins)
                    else:
                        L.tell(ins, "mla_c")
            for t in range(TT):
                for g, (a, n) in enumerate(((0, 3), (3, 2))):
                    u = look(dve, "mla_cT", t, g)
                    for j in range(n):
                        gain = col("q_norm", j) if g == 0 else col("kv_norm", j)
                        ins = TS(cT[:, a + j, t * P:(t + 1) * P], ps[:, u.bank, j * P:(j + 1) * P], gain, None, ALU.mult)
                        if j < n - 1:
                            S(ins)
                        else:
                            free(L, ins, u)
                dve.sem_inc(sig("mla_cT"), 1)
            L.wait("mla_qkv", 1)
            for t in range(TT):
                S(copy(kx[:, t, :, 0:MNOPE], kv[:, t, :, 0:MNOPE]))
                S(copy(kx[:, t, :, MNOPE:], bc(pe_[:, t, EVEN["kr"]:EVEN["kr"] + MROPE], 1, [P, MH, MROPE])))
            sq = area(spare, 0, TT * MH, MQK)
            both = [v.rearrange("p t h d -> p (t h) d") for v in (qh, kx)]
            for i, v in enumerate(both):
                S(TTN(sq, v, v, ALU.mult))
                ins = dve.tensor_reduce(stat[:, 16 * i:16 * i + 16], sq, AX.X, ALU.add)
                S(ins)
            dve.sem_inc(sig("mla_sumsq"), 1)
            L.wait("mla_rstd", 1)
            t1, t2 = (area(spare, 1536 + 256 * i, TT, MH, 16) for i in range(2))
            for i, (v, v4, g) in enumerate(((both[0], qh, "qh"), (both[1], kx, "kh"))):
                S(TTN(v, v, bc(stat[:, 16 * i:16 * i + 16], 2, [P, 16, MQK]), ALU.mult))
                S(TTN(v, v, bc(rows[:, ROWS[g]:ROWS[g] + MQK], 1, [P, 16, MQK]), ALU.mult))
                for t in range(TT):
                    x1, x2 = v4[:, t, :, MNOPE:MNOPE + 16], v4[:, t, :, MNOPE + 16:]
                    c, s = (bc(w[:, t, 0:16], 1, [P, MH, 16]) for w in (cos, sin))
                    rope(x1, x2, x1, x2, c, s, t1[:, t], t2[:, t])
                dve.sem_inc(sig("mla_heads"), 1)
            for t in range(TT):
                for g in range(2):
                    u = look(dve, "mla", "kT", t, g)
                    free(L, copy(kT[0:MQK, 4 * g:4 * g + 4, t * P:(t + 1) * P],
                                 ps[0:MQK, u.bank, :].rearrange("p (a b) -> p a b", a=4)), u, "mla_kT")
            attend(ATT["mla"], lambda t: mix0[:, t, 0:512])
            c, s = (w[:, :, 16:48] for w in (cos, sin))
            t1, t2 = (area(spare, 1024 * i, TT, 16, 32) for i in range(2))
            for t in range(TT):
                x = pe_[:, t, EVEN["rq"]:EVEN["rv"]].rearrange("p (h d) -> p h d", d=RD)
                y = rqk[:, t, :, :, :].rearrange("p a h d -> p (a h) d")
                rope(x[:, :, 0:32], x[:, :, 32:64], y[:, :, 0:32], y[:, :, 32:64],
                     bc(c[:, t, :], 1, [P, 16, 32]), bc(s[:, t, :], 1, [P, 16, 32]), t1[:, t], t2[:, t])
            dve.sem_inc(sig("ret_rope"), 1)
            L.wait("rel_loaded", 16)

            def exponent(x):
                S(TS(decay[:, x % 2, :, :], relp, u16[:, x:x + 1], None, ALU.mult))
                L.tell(STT(out=decay[:, x % 2, :, :], in0=relm, scalar=u16[:, 8 + x:9 + x],
                           in1=decay[:, x % 2, :, :], op0=ALU.mult, op1=ALU.add), "ret_e")

            exponent(0)
            for x in range(RH):
                if x + 1 < RH:
                    exponent(x + 1)
                u = look(dve, "ret_s", x)
                L.wait("ret_d", x + 1)
                if x >= 2:
                    L.wait("ret_pv", x - 1)
                free(L, STT(out=sdec[:, x % 2, :, :].rearrange("p a b -> p (a b)"), in0=ps[:, u.bank, :],
                            scalar=RD ** -0.5, in1=decay[:, x % 2, :, :].rearrange("p a b -> p (a b)"),
                            op0=ALU.mult, op1=ALU.mult), u, "ret_sdec")
            for t in range(TT):
                u = look(dve, "ret_o", t)
                free(L, copy(mix0[:, t, 512:1024], ps[:, u.bank, :]), u)
                S(TTN(temp[:, 512:1024], mix0[:, t, 512:1024], mix0[:, t, 512:1024], ALU.mult))
                S(dve.tensor_reduce(stat[:, 8 * t:8 * t + 8], temp[:, 512:1024].rearrange("p (a b) -> p a b", a=8),
                                    AX.X, ALU.add))
            dve.sem_inc(sig("ret_sumsq"), 1)
            L.wait("ret_rstd", 1)
            L.wait("rg_ready", 1)
            for t in range(TT):
                v = mix0[:, t, 512:1024]
                v3 = v.rearrange("p (a b) -> p a b", a=8)
                S(TTN(v3, v3, bc(stat[:, 8 * t:8 * t + 8], 2, [P, 8, 64]), ALU.mult))
                L.tell(TTN(v, v, pe_[:, t, EVEN["rg"]:EVEN["end"]], ALU.mult), "mix_ready")
            mixT("even", range(TT), lambda f: col("ret_g", f - 4) if f >= 4 else None)

            def add_out(tag):
                for m in range(KD):
                    u = look(dve, tag, m)
                    free(L, TTN(res[:, 0, m, :], ps[:, u.bank, 0:T], res[:, 0, m, :], ALU.add), u)
                dve.sem_inc(sig("residual"), 1)

            add_out("even_out")

            def ffn1(l):
                j = l * CPE
                weights_lo(j)
                weights_lo(j + 1)
                norm(1, lambda hf, k: col("ffn", 8 * l + k), split=True)

                def product(m):
                    u = uses[f"ffn{l}", "up", m]
                    L.wait("silu1", KF * l + m + 1)
                    if m >= 2:
                        L.wait("hidden_ready", KF * l + m - 1)
                    free(L, TTN(fval[:, m % 2, :], ps[:, u.bank, T:2 * T], fsil[:, m % 2, 0:T], ALU.mult), u,
                         "ffn_val")

                for m in range(KF):
                    u = look(dve, f"ffn{l}", "up", m)
                    x, y = ps[:, u.bank, 0:T], fconv[:, m % 2, 0:T]
                    w = [col("conv_w", (3 * l + i) * KF + m) for i in range(3)]
                    S(TS(y, x, w[1], col("conv_b", KF * l + m), ALU.mult, ALU.add))
                    S(STT(out=y[:, 1:T], in0=x[:, 0:T - 1], scalar=w[0], in1=y[:, 1:T], op0=ALU.mult, op1=ALU.add))
                    L.tell(STT(out=y[:, 0:T - 1], in0=x[:, 1:T], scalar=w[2], in1=y[:, 0:T - 1],
                               op0=ALU.mult, op1=ALU.add), "conv1")
                    if m:
                        product(m - 1)
                    weights_lo(j + m + 2)
                product(KF - 1)
                for m in range(KF + 2, CPE):
                    weights_lo(j + m)
                for q in range(4):
                    u = look(dve, f"ffn{l}", "down", 0, q)
                    v = res[:, 0, 2 * q:2 * q + 2, :].rearrange("p a b -> p (a b)")
                    free(L, TTN(v, ps[:, u.bank, :], v, ALU.add), u)
                dve.sem_inc(sig("residual"), 1)

            ffn1(0)

            norm(1, lambda hf, k: col("mix_odd", k))
            S(dve.memset(gA, 0.0))
            evacuate(L, copy, "odd_in", 0, ODD["end"], range(TT), 1, lambda t, a, b: po[:, t, a:b], "proj_dve")
            for t in range(TT):
                u = look(dve, "gla_gT", t)
                free(L, copy(gaT[0:GR, :, t * P:(t + 1) * P],
                             ps[0:GR, u.bank, 0:T].rearrange("p (a b) -> p a b", a=2)), u, "gla_gT")
            for i in range(4):
                u = look(dve, "gla_la", i // 2, i % 2)
                L.wait("gla_soft", i + 1)
                v = la[:, i // 2, i % 2, :]
                free(L, STT(out=v, in0=ps[:, u.bank, :], scalar=0.0, in1=temp[:, 512 * (i % 2):512 * (i % 2) + 512],
                            op0=ALU.min, op1=ALU.subtract), u)
                L.tell(TS(v, v, 1.0 / TAU, None, ALU.mult), "gla_la")
            for i in range(4):
                L.wait("gla_kd", i + 1)
                L.wait("proj_act", PROJ["odd_in"])
                L.tell(TTN(kdT[:, i // 2, i % 2, :], temp[:, 512 * (i % 2):512 * (i % 2) + 512],
                           po[:, i % 2, ODD["k"]:ODD["k"] + 512], ALU.mult), "gla_kdT")
            L.wait("gla_T", 4)
            L.wait("gla_const", 80)
            qs = GK ** -0.5
            for x in range(GH):
                for d in range(2):
                    n = 2 * x + d
                    L.wait("gla_ex", n + 1)
                    q, k = gqk[:, x, :], gqk[:, 4 + x, :]
                    S(STT(out=gqkx[:, d, 0, :], in0=q, scalar=qs, in1=gex[:, 1, :], op0=ALU.mult, op1=ALU.mult))
                    S(TTN(gqkx[:, d, 1, :], k, gex[:, 2, :], ALU.mult))
                    L.tell(STT(out=gqkx[:, d, 2, :], in0=q, scalar=qs, in1=gex[:, 0, :], op0=ALU.mult, op1=ALU.mult),
                           "gla_qk")
                    for i in range(3):
                        u = look(dve, "gla_st", n, i)
                        if i == 0:
                            free(L, copy(gst[:, d, 0, :], ps[:, u.bank, 0:GV]), u)
                            continue
                        c = i if d == 0 else 3 - i
                        last = c * GC + GC - 1 if d == 0 else c * GC
                        free(L, STT(out=gst[:, d, i, :], in0=gst[:, d, i - 1, :], scalar=gex[:, 0, last:last + 1],
                                    in1=ps[:, u.bank, 0:GV], op0=ALU.mult, op1=ALU.add), u)
                    dve.sem_inc(sig("gla_states"), 1)
                    u = look(dve, "gla_A", n)
                    for t in range(TT):
                        ins = dve.copy_predicated(gA[:, d, t, :], glamask[:, d, :].bitcast(I32),
                                                  ps[:, u.bank, t * P:(t + 1) * P])
                        if t == 0:
                            S(ins)
                        else:
                            free(L, ins, u, "gla_Am")
                u = look(dve, "gla_o", x)
                free(L, copy(po[:, :, x * GV:(x + 1) * GV], ps[:, u.bank, :].rearrange("p (a b) -> p a b", a=2)), u)
            for t in range(TT):
                v = po[:, t, 0:1024]
                S(TTN(temp[:, :], v, v, ALU.mult))
                S(dve.tensor_reduce(stat[:, 4 * t:4 * t + 4], temp[:, :].rearrange("p (a b) -> p a b", a=4), AX.X, ALU.add))
            dve.sem_inc(sig("gla_sumsq"), 1)
            L.wait("gla_rstd", 1)
            L.wait("gr_ready", 1)
            for t in range(TT):
                v = po[:, t, 0:1024]
                v3 = v.rearrange("p (a b) -> p a b", a=4)
                S(TTN(v3, v3, bc(stat[:, 4 * t:4 * t + 4], 2, [P, 4, GV]), ALU.mult))
                L.tell(TTN(v, v, po[:, t, ODD["r"]:ODD["r"] + 1024], ALU.mult), "mix_ready")
            mixT("odd", range(TT), lambda f: col("gla_g", f))
            add_out("odd_out")
            ffn1(1)

            L.wait("mod_done", 1)
            bm = cols[:, COLS["b_mod"]:COLS["b_mod"] + 96]
            m = mods[:, :, :, :].rearrange("p l c x -> p (l c) x")
            S(TTN(m, m, bc(bm, 2, [P, 96, 2]), ALU.add))
            for l in range(2):
                for j, name in ((1, "norm1"), (4, "norm2")):
                    g = cols[:, COLS[name] + 8 * l:COLS[name] + 8 * l + 8]
                    m = mods[:, l, 8 * j:8 * j + 8, :]
                    S(STT(out=m, in0=m, scalar=1.0, in1=bc(g, 2, [P, 8, 2]), op0=ALU.add, op1=ALU.mult))

            def gated(l, j, hf, m):
                return mods[:, l, 8 * j + m, hf:hf + 1]

            for l in range(2):
                norm(2, lambda hf, k: gated(l, 1, hf, k), lambda hf, k: gated(l, 0, hf, k))
                L.tell(dve.memset(vaug[:, :, :, LV:LV + 1], 1.0), "vaug_ones")
                before, after = in_stages(l)
                for tag, a, b, tiles, dst in before:
                    evacuate(L, copy, tag, a, b, tiles, 1, dst, "proj_dve")
                for c in range(4):
                    u = look(dve, "conv", l, c)
                    x = ps[:, u.bank, :].rearrange("p (a b) -> p a b", a=2)
                    y = conv[:, c, :].rearrange("p (a b) -> p a b", a=2)
                    w = [col("conv_w2", 20 * l + 4 * i + c) for i in range(5)]
                    if l == 1 and c < 2:
                        x, y = x[:, 0:1, :], y[:, 0:1, :]
                    S(TS(y, x, w[2], col("conv_b2", 4 * l + c), ALU.mult, ALU.add))
                    for i, o in ((0, -2), (1, -1), (3, 1), (4, 2)):
                        a, b = max(0, -o), T - max(0, o)
                        ins = STT(out=y[:, :, a:b], in0=x[:, :, a + o:b + o], scalar=w[i], in1=y[:, :, a:b],
                                  op0=ALU.mult, op1=ALU.add)
                        if i < 4:
                            S(ins)
                        else:
                            free(L, ins, u, "conv2")
                for tag, a, b, tiles, dst in after:
                    evacuate(L, copy, tag, a, b, tiles, 1, dst, "proj_dve")
                u = look(dve, "gT", l)
                free(L, copy(gT, ps[:, u.bank, 0:64].rearrange("p (a b) -> p a b", a=4)), u, "gT")
                L.wait("proj_act", PROJ[f"kv{l}"])
                look(dve, "gates", l, 3)
                ax = cst[:, CST["axial"]:CST["axial"] + 128].rearrange("p (t w a c) -> p t w a c", t=2, w=2, a=2)
                for t in range(TT):
                    t1, t2 = (area(temp, 256 * i, 8, 2, 16) for i in range(2))
                    for src, dst, n in ((p2[:, t, 0:512].rearrange("p (h a w c) -> p h a w c", a=2, w=2, c=16),
                                         ro[:, t, :].rearrange("p (h a w c) -> p h a w c", a=2, w=2, c=16), 8),
                                        (p2[:, t, 512:640].rearrange("p (h a w c) -> p h a w c", a=2, w=2, c=16),
                                         kdup[:, t, :, 0, :].rearrange("p h (a w c) -> p h a w c", a=2, w=2), 2)):
                        cs = [bc(ax[:, t, w, :, :], 1, [P, n, 2, 16]) for w in range(2)]
                        rope(src[:, :, :, 0, :], src[:, :, :, 1, :], dst[:, :, :, 0, :], dst[:, :, :, 1, :],
                             cs[0], cs[1], t1[:, 0:n], t2[:, 0:n])
                    S(copy(kdup[:, t, :, 1, :], kdup[:, t, :, 0, :]))
                for t in (2, 3):
                    for i in range(2):
                        S(copy(kdup[:, t, :, i, :], p2[:, t, 512:640].rearrange("p (a b) -> p a b", a=2)))
                for _ in range(2):
                    dve.sem_inc(sig("att_rope"), 1)
                for t in (range(4) if l == 0 else range(TT)):
                    u = look(dve, "aqT", l, t)
                    free(L, copy(aqT[:, :, t * P:(t + 1) * P], ps[:, u.bank, :].rearrange("p (a b) -> p a b", a=4)),
                         u, "aqT")
                attend(ATT[f"wx{l}"], lambda t: mix2[:, t, 0:512])
                if l == 0:
                    attend(ATT["wc0"], lambda t: mix2[:, t, 0:512])
                dve.sem_inc(sig("att_done"), 1)
                L.wait("gates_ready", l + 1)
                one = cst[0:4, CST["ones"]:CST["ones"] + 1].broadcast_to([4, T])

                def scan(dst, src, op):
                    for d in range(2):
                        for sq in (1, 0):
                            a, b = sq * T, (sq + 1) * T
                            o, i = dst(d)[:, a:b], src(d)[:, a:b]
                            first = 0.0 if sq else (dst(d)[:, 2 * T - 1:2 * T] if d == 0 else dst(d)[:, T:T + 1])
                            if d == 1:
                                o, i = o[:, T - 1::-1], i[:, T - 1::-1]
                            S(dve.tensor_tensor_scan(o, one, i, first, ALU.mult, op))

                scan(lambda d: brow[0:4, d, :], lambda d: gates[0:4, 2 * d + 1, :], ALU.subtract)
                for d in range(2):
                    S(STT(out=gates[0:4, 2 * d, :], in0=gates[0:4, 2 * d, :], scalar=CAP, in1=brow[0:4, d, :],
                          op0=ALU.mult, op1=ALU.subtract))
                scan(lambda d: mrow[0:4, d, :], lambda d: gates[0:4, 2 * d, :], ALU.max)
                L.tell(TTN(brow[0:4, :, :], brow[0:4, :, :], mrow[0:4, :, :], ALU.add), "lrows")
                u = look(dve, "lcols", l)
                free(L, copy(temp[:, 0:64], ps[:, u.bank, 0:64]), u, "lc_ready")
                L.wait("lem_ready", l + 1)
                L.wait("lmask", 16 * (l + 1))
                lc = temp[:, 0:64].rearrange("p (t w d h) -> p t w d h", t=4, w=2, d=2)
                em = temp[:, 64:128].rearrange("p (t w d h) -> p t w d h", t=4, w=2, d=2)
                steps = lsteps(l)

                def exponents(n):
                    sq, x, d = steps[n]
                    ns = len(STILES[sq])
                    u = look(dve, "lm", l, n)
                    for i in (ns - 2, ns - 1):
                        ins = TS(lw[n % 2][:, i, :], ps[:, u.bank, 0:T], lc[:, STILES[sq][i], 0, d, x:x + 1], 0.0,
                                 ALU.subtract, ALU.max)
                        if i == ns - 2:
                            S(ins)
                        else:
                            L.tell(ins, "lw")

                def weights(n):
                    sq, x, d = steps[n]
                    L.wait("lexp", 16 * l + n + 1)
                    if n >= 2:
                        look(dve, "lo", l, n - 2)
                    for i in range(len(STILES[sq]) // 2):
                        u = look(dve, "ls", l, sq, x, i)
                        dst = lp[n % 2][:, 2 * i:2 * i + 2, :].rearrange("p a b -> p (a b)")
                        w = lw[n % 2][:, 2 * i:2 * i + 2, :].rearrange("p a b -> p (a b)")
                        ins = STT(out=dst, in0=ps[:, u.bank, :], scalar=LK ** -0.5, in1=w, op0=ALU.mult, op1=ALU.mult)
                        if d == 0:
                            S(ins)
                        else:
                            free(L, ins, u)
                    dve.sem_inc(sig("lweights"), 1)

                def heads_out(n):
                    sq, x, d = steps[n]
                    u = look(dve, "lo", l, n)
                    o = ps[:, u.bank, 0:2 * (LV + 1)].rearrange("p (t c) -> p t c", t=2)
                    r = stat[:, 0:2]
                    S(copy(r, o[:, :, LV]))
                    S(STT(out=r, in0=o[:, :, LV], scalar=-1.0, in1=r, op0=ALU.mult, op1=ALU.max))
                    S(TTN(r, r, em[:, 2 * sq:2 * sq + 2, 1, d, x], ALU.max))
                    S(dve.reciprocal(r, r))
                    for t in range(TT):
                        dst = mix2[:, 2 * sq + t, 512 + x * LV:512 + (x + 1) * LV]
                        if d == 0:
                            ins = TS(dst, o[:, t, 0:LV], r[:, t:t + 1], None, ALU.mult)
                        else:
                            ins = STT(out=dst, in0=o[:, t, 0:LV], scalar=r[:, t:t + 1], in1=dst,
                                      op0=ALU.mult, op1=ALU.add)
                        if t == 0:
                            S(ins)
                        else:
                            free(L, ins, u)

                exponents(0)
                for n in range(len(steps)):
                    if n + 1 < len(steps):
                        exponents(n + 1)
                    weights(n)
                    if n:
                        heads_out(n - 1)
                heads_out(len(steps) - 1)
                tiles = range(4) if l == 0 else range(TT)
                S(dve.memset(stat[:, 0:20], 1.0))
                for t in tiles:
                    for half, dst, nh in ((1, stat[:, 4 * t:4 * t + 4], 4), (0, stat[:, 16 + t:17 + t], 1)):
                        v = mix2[:, t, 512 * half:512 * half + 512]
                        S(TTN(temp[:, 512:1024], v, v, ALU.mult))
                        S(dve.tensor_reduce(dst, temp[:, 512:1024].rearrange("p (a b) -> p a b", a=nh), AX.X, ALU.add))
                dve.sem_inc(sig("merge_sumsq"), 1)
                L.wait("merge_rstd", l + 1)
                L.wait("o_ready", l + 1)
                for t in tiles:
                    v = mix2[:, t, 512:1024]
                    v3 = v.rearrange("p (a b) -> p a b", a=4)
                    S(TTN(v3, v3, bc(stat[:, 4 * t:4 * t + 4], 2, [P, 4, LV]), ALU.mult))
                    S(TTN(v, v, p2[:, t, 768:1280], ALU.mult))
                    v = mix2[:, t, 0:512]
                    L.tell(TS(v, v, stat[:, 16 + t:17 + t], None, ALU.mult), "mix_ready")
                mixT(f"mix{l}", tiles, lambda f: col("g_att", 4 * l + f) if f < 4 else col("g_ml", 4 * l + f - 4))
                nh = 2 - l
                for m in range(KD):
                    u = look(dve, f"out{l}", m)
                    for hf in range(nh):
                        v = res[:, hf, m, :]
                        ins = STT(out=v, in0=ps[:, u.bank, hf * T:(hf + 1) * T], scalar=gated(l, 2, hf, m), in1=v,
                                  op0=ALU.mult, op1=ALU.add)
                        if hf < nh - 1:
                            S(ins)
                        else:
                            free(L, ins, u)
                dve.sem_inc(sig("residual"), 1)
                if l == 0:
                    weights_lo(2 * CPE)
                    weights_lo(2 * CPE + 1)
                norm(nh, lambda hf, k: gated(l, 4, hf, k), lambda hf, k: gated(l, 3, hf, k), split=l == 0)
                if l == 0:
                    for m in range(CPE):
                        if m >= KF:
                            if m + 2 < CPE:
                                weights_lo(2 * CPE + m + 2)
                            continue
                        u = look(dve, "ffn2", "up", m, 1)
                        ug = uses["ffn2", "up", m, 0]
                        dve.wait_ge(bank_free[ug.bank], ug.nth + 1)
                        free(L, TTN(g2[:, m, :], ps[:, u.bank, :], fsil[:, m % 2, :], ALU.mult), u, "ffn_val")
                        weights_lo(2 * CPE + m + 2)
                    for hf in range(2):
                        for q in range(4):
                            u = look(dve, "ffn2", "down", hf, q)
                            for i in range(2):
                                m = 2 * q + i
                                v = res[:, hf, m, :]
                                ins = STT(out=v, in0=ps[:, u.bank, i * T:(i + 1) * T], scalar=gated(l, 5, hf, m),
                                          in1=v, op0=ALU.mult, op1=ALU.add)
                                if i == 0:
                                    S(ins)
                                else:
                                    free(L, ins, u)
                    dve.sem_inc(sig("residual"), 1)

            L.tell(dve.memset(temp[:, 0:512], 0.0), "zero_ready")
            iota = cst[:, CST["iota8"]:CST["iota8"] + 8]
            lg, eq, oh1, oh2 = (temp[:, 512 + 8 * i:520 + 8 * i] for i in range(4))
            m1, m2, mx, ex, w1 = (temp[:, 596 + i:597 + i] for i in (0, 1, 2, 4, 5))
            for t in range(TT):
                u = look(dve, "router", t)
                free(L, TTN(lg, ps[:, u.bank, 0:NE], rows[:, ROWS["b_router"]:ROWS["b_router"] + NE], ALU.add), u)
                for mval, oh in ((m1, oh1), (m2, oh2)):
                    S(dve.tensor_reduce(mval, lg, AX.X, ALU.max))
                    S(TS(eq, lg, mval, None, ALU.is_ge))
                    S(TTN(eq, eq, iota, ALU.mult))
                    S(dve.tensor_reduce(mx, eq, AX.X, ALU.max))
                    S(TS(oh, eq, mx, None, ALU.is_equal))
                    S(STT(out=lg, in0=oh, scalar=-HUGE, in1=lg, op0=ALU.mult, op1=ALU.add))
                L.tell(TTN(ex, m2, m1, ALU.subtract), "top_ready")
                S(TTN(taken[:, t, :], oh1, oh2, ALU.add))
                L.wait("top_exp", t + 1)
                S(TS(w1, ex, 1.0, None, ALU.add))
                S(dve.reciprocal(w1, w1))
                S(TTN(ex, ex, w1, ALU.mult))
                S(TS(combine[:, t, :], oh1, w1, None, ALU.mult))
                L.tell(STT(out=combine[:, t, :], in0=oh2, scalar=ex, in1=combine[:, t, :], op0=ALU.mult, op1=ALU.add),
                       "combine")
            u = look(dve, "rank")
            L.tell(copy(rank.rearrange("p t e -> p (t e)"), ps[:, u.bank, 0:2 * NE]), "rank")
            S(dve.tensor_reduce(m1, ps[:, u.bank, 2 * NE:3 * NE], AX.X, ALU.max))
            dve.sem_inc(bank_free[u.bank], 1)
            S(TS(m1, m1, P + 0.5, 1.0, ALU.is_gt, ALU.add))
            S(TS(m2, m1, float(NE // 2), -1.0, ALU.mult, ALU.add))
            L.tell(copy(passes[:, :], temp[:, 596:598]), "passes")

            def picks(r):
                for e in range(NE):
                    for t in range(TT):
                        at = rank[:, t, e:e + 1]
                        S(TS(pick[:, r * NE + e, t, :], slots, at, taken[:, t, e:e + 1], ALU.is_equal, ALU.mult))

            u = look(dve, "rw8")
            free(L, copy(rw8[0:NE, :], ps[0:NE, u.bank, :]), u, "rw8")
            L.wait("moe_const", 16)
            picks(0)
            dve.sem_inc(sig("pick"), 1)
            for e in range(NE):
                u = uses["rw", e]
                L.wait("wrow", e + 1)
                for r in range(2):
                    ins = STT(out=put_back[:, 1 + r * NE + e, :], in0=ps[:, u.bank, 0:T], scalar=slot[:, r:r + 1],
                              in1=wrow[:, e % 4, :], op0=ALU.is_equal, op1=ALU.mult)
                    if r == 0:
                        S(ins)
                    else:
                        free(L, ins, u)
            S(dve.memset(put_back[:, 0, :], 0.0))
            dve.sem_inc(sig("moe_turned"), 1)
            for _ in range(2):
                dve.sem_inc(sig("moe_val"), 1)
                dve.sem_inc(sig("moe_hidden"), 1)
            r_ = rank.rearrange("p t e -> p (t e)")
            S(TS(r_, r_, -float(P), None, ALU.add))
            picks(1)
            S(dve.memset(pick[:, 2 * NE, :, :], 0.0))
            dve.sem_inc(sig("pick"), 1)
            def gathered(dst, half):
                x = [v[:, dst, 4 * half:4 * half + 4, :].rearrange("p k t -> p (k t)") for v in xexp]
                TTN(x[1], ps[:, 2, :], x[0].bitcast(F32), ALU.subtract).then_inc(sig("xexp"), 1)

            def expert_lo(i, n):
                s, j = moe["plan"][n][0], moe["split"] + n
                dve.wait_ge(sig("weights_hi"), i * (2 * CPE) + (j + 1))
                TTN(ring_lo[:, s, :], ring[:, s, :], ring_hi[:, j % HIS, :].bitcast(F32),
                    ALU.subtract).then_inc(sig("weights_lo"), 1)

            def expert_out(wait):
                wait()
                dve.tensor_copy(yexp, ps[:, 2:4, :].rearrange("p a b -> p (a b)")).then_inc(sig("yexp"), 1)

            for half in range(2):
                dve.wait_ge(sig("xexp_hi"), half + 1)
                gathered(0, half)
            n_passes = dve.value_load(passes[0:1, 0:1], min_val=1, max_val=2)
            with dve.Fori(0, n_passes * (NE // 2)) as i:
                expert_lo(i, 0)
                expert_lo(i, 1)
                expert_out(lambda: dve.wait_ge(sig("moe_down"), i * KF + HIS))
                for e in range(2):
                    if e:
                        expert_out(lambda: dve.wait_ge(sig("moe_down"), i * KF + (HIS + KF // 2)))
                    for m in range(CPE):
                        n = e * CPE + m
                        if n + 2 < 2 * CPE and m != KF - 1:
                            expert_lo(i, n + 2)
                        if m in (15, 19):
                            dve.wait_ge(sig("xexp_hi"), i * 4 + (2 * e + 3 + (m == 19)))
                            gathered(1 - e, int(m == 19))
                        if m >= KF:
                            continue
                        b = m % 2
                        dve.wait_ge(sig("moe_silu"), i * (2 * KF) + (e * KF + m + 1))
                        TTN(mprod[:, b, :], ps[:, b, P:2 * P], msil[:, b, :], ALU.mult).then_inc(sig("moe_val"), 1)
                        if m == KF - 1:
                            expert_lo(i, n + 2)
            expert_out(lambda: dve.wait_ge(sig("moe_down"), n_passes * (NE // 2) * KF + HIS))
            for q in range(4):
                u = look(dve, "moe_acc", q)
                for i in range(2):
                    m = 2 * q + i
                    v = res[:, 0, m, :]
                    ins = STT(out=v, in0=ps[:, u.bank, i * T:(i + 1) * T], scalar=gated(1, 5, 0, m), in1=v,
                              op0=ALU.mult, op1=ALU.add)
                    if i == 0:
                        S(ins)
                    else:
                        free(L, ins, u)
            dve.sem_inc(sig("residual"), 1)
            norm(1, lambda hf, k: col("final", k), name="out_ready")

    return nc


WEIGHTS = ["w_in_even", "mla_w_uq", "mla_w_ukv", "w_out_even", "w_in_odd", "gla_w_gate_fwd", "gla_b_gate_fwd",
           "gla_w_gate_bwd", "gla_b_gate_bwd", "w_out_odd", "ffn_w_up", "ffn_w_down", "w_mod_2", "w_in_2", "w_out_2",
           "ffn_w1_2", "ffn_w3_2", "ffn_w2_2", "w_router_2", "exp_w1_2", "exp_w3_2", "exp_w2_2"]


def kernel(**inputs):
    import numpy as _np
    import concourse.bacc as _bacc
    from concourse import mybir as _mybir
    from concourse.bass_utils import run_bass_kernel_spmd as _run

    I = {k: _np.asarray(v) for k, v in inputs.items()}

    def on_partitions(a):
        return a.reshape(-1, P).T

    cond = _np.stack([I["c_2"].reshape(D), I["c_ctx_2"].reshape(D)], 0).reshape(2, KD, P).transpose(2, 1, 0)
    bg = _np.zeros((P, 8), _np.float32)
    bg[0:4] = I["b_gates_2"].reshape(2, 4, 4).transpose(2, 0, 1).reshape(4, 8)
    parts = [on_partitions(I["mix_norm_even"]), on_partitions(I["mix_norm_odd"]), on_partitions(I["ffn_norm"]),
             on_partitions(I["ffn_conv_w"]), on_partitions(I["ffn_conv_b"]), on_partitions(I["mla_q_norm"]),
             on_partitions(I["mla_kv_norm"]), on_partitions(I["ret_out_norm"]), on_partitions(I["gla_out_norm"]),
             on_partitions(I["norm1_g_2"]), on_partitions(I["norm2_g_2"]), on_partitions(I["b_mod_2"]),
             on_partitions(I["conv_w_2"]), on_partitions(I["conv_b_2"]), on_partitions(I["g_att_2"]),
             on_partitions(I["g_ml_2"]), on_partitions(I["final_g_2"]), cond.reshape(P, 16), bg]
    rows = [I["mla_q_head_norm"], I["mla_k_head_norm"], I["ret_theta_fwd"], I["ret_theta_bwd"], I["attn_sink_2"],
            I["b_router_2"]]
    arrays = {w: _np.ascontiguousarray(I[w]) for w in WEIGHTS}
    arrays["cols"] = _np.ascontiguousarray(_np.concatenate(parts, 1))
    arrays["rows"] = _np.concatenate([r.reshape(-1) for r in rows])
    arrays["pos"] = _np.ascontiguousarray(I["positions"].reshape(TT, P).T)
    arrays["xT"] = _np.ascontiguousarray(I["x"].reshape(T, KD, P).transpose(2, 1, 0))
    arrays["ctxT"] = _np.ascontiguousarray(I["ctx_2"].reshape(T, KD, P).transpose(2, 1, 0))
    arrays["consts"] = constants()

    nc = _bacc.Bacc("TRN2", target_bir_lowering=False, num_devices=1)
    A, feed = {}, {}
    for name, a in arrays.items():
        feed[f"in_{name}"] = a
        A[name] = nc.dram_tensor(f"in_{name}", a.shape, _mybir.dt.from_np(a.dtype), kind="ExternalInput").ap()
    out = nc.dram_tensor("out_xT", (P, KD, T), F32, kind="ExternalOutput").ap()
    build(nc, A, out)
    r = _run(nc, [feed], core_ids=[0])
    y = r.results[0]["out_xT"]
    return y.transpose(2, 1, 0).reshape(1, T, D)
```
